# Optimizing a Trainium2 kernel written in Bass

```python
import math
import jax
import jax.numpy as jnp
from jax import lax
import numpy as np

D_MODEL = 1024
BATCH = 1
SEQ = 512
DEPTH = 1
DEC_BATCH = 8
DEC_SEQ = 1
PAST_LEN = 512
PAGE_SIZE = 128

SB_HEADS = 8
SB_HEAD_DIM = 64
SB_BLOCK = 128
SB_BIAS_INIT = -7.0
GDN_HEADS = 8
GDN_K_DIM = 64
GDN_V_DIM = 64
GDN_CONV = 4
GDN_CHUNK = 64
N_MEM = 256
MEM_HEADS = 4
MEM_HEAD_DIM = 128
N_EXPERTS = 64
TOP_K = 8
N_GROUPS = 8
TOPK_GROUPS = 4
D_EXPERT = 256
D_SHARED = 256
ROUTE_SCALE = 2.5
MOE_BLOCK = 64
DN_ALPHA = (2 * DEPTH) ** 0.25
DN_BETA = (8 * DEPTH) ** -0.25
LN_EPS = 1e-5
RMS_EPS = 1e-6
L2_EPS = 1e-6

SB_W = SB_HEADS * SB_HEAD_DIM
GDN_QK_W = GDN_HEADS * GDN_K_DIM
GDN_V_W = GDN_HEADS * GDN_V_DIM
GDN_CONV_W = 2 * GDN_QK_W + GDN_V_W
MEM_W = MEM_HEADS * MEM_HEAD_DIM
N_BRANCH = 3
IN_SPLITS = (SB_W, SB_W, SB_W, GDN_CONV_W, GDN_V_W, GDN_HEADS, GDN_HEADS, MEM_W, N_BRANCH * D_MODEL)
D_IN = sum(IN_SPLITS)

kernel_name = 'hybrid_sb_gdn_mem_moe_decode_step'

def _split(x, sizes):
    offs = np.cumsum(np.array(sizes))[:-1].tolist()
    return jnp.split(x, offs, axis=-1)

def _heads(t, n):
    return t.reshape(t.shape[0], t.shape[1], n, -1)

def layer_norm(x, g, b):
    xf = x.astype(jnp.float32)
    mu = jnp.mean(xf, axis=-1, keepdims=True)
    var = jnp.mean(jnp.square(xf - mu), axis=-1, keepdims=True)
    return ((xf - mu) * lax.rsqrt(var + LN_EPS) * g + b).astype(x.dtype)

def l2norm(x):
    xf = x.astype(jnp.float32)
    return xf * lax.rsqrt(jnp.sum(xf * xf, axis=-1, keepdims=True) + L2_EPS)

def _sb_block(q, q_pos, k, v, k_pos, bias):
    z = jnp.einsum('bqhd,bkhd->bhqk', q, k, preferred_element_type=jnp.float32) * (SB_HEAD_DIM ** -0.5)
    z = z + bias.astype(jnp.float32)[None, :, None, None]
    causal = k_pos[None, :] < q_pos[:, None]
    log_keep = jnp.where(causal, jax.nn.log_sigmoid(-z), 0.0)
    incl = lax.cumsum(log_keep, axis=3, reverse=True)
    excl = jnp.concatenate([incl[..., 1:], jnp.zeros_like(incl[..., :1])], axis=-1)
    a = jnp.where(causal, jnp.exp(jax.nn.log_sigmoid(z) + excl), 0.0)
    return jnp.einsum('bhqk,bkhd->bqhd', a, v.astype(jnp.float32))

def stick_breaking(q, k, v, start, bias):
    B, L, H, Dh = q.shape
    qb = math.gcd(L, SB_BLOCK)
    nb = L // qb
    k_pos = jnp.arange(k.shape[1], dtype=jnp.int32)
    q_pos = (start + jnp.arange(L, dtype=jnp.int32)).reshape(nb, qb)
    q_blocks = q.reshape(B, nb, qb, H, Dh).transpose(1, 0, 2, 3, 4)
    out = lax.map(lambda a: _sb_block(a[0], a[1], k, v, k_pos, bias), (q_blocks, q_pos))
    return out.transpose(1, 0, 2, 3, 4).reshape(B, L, H, Dh).astype(q.dtype)

def causal_conv(x, buf, w):
    L = x.shape[1]
    xp = jnp.concatenate([buf.astype(x.dtype), x], axis=1)
    y = sum(xp[:, i:i + L] * w[i] for i in range(GDN_CONV))
    return jax.nn.silu(y), xp[:, -(GDN_CONV - 1):]

def gated_delta_rule(q, k, v, g, beta, s0):
    B, L, H, Dk = q.shape
    Dv = v.shape[-1]
    C = math.gcd(L, GDN_CHUNK)
    N = L // C

    def chunks(x):
        return x.reshape(B, N, C, H, -1).transpose(1, 0, 3, 2, 4)

    qc, kc, vc = chunks(q * (Dk ** -0.5)), chunks(k), chunks(v)
    gc = jnp.cumsum(g.reshape(B, N, C, H).transpose(1, 0, 3, 2), axis=-1)
    bc = beta.reshape(B, N, C, H).transpose(1, 0, 3, 2)[..., None]
    tril = jnp.tril(jnp.ones((C, C), bool))
    strict = jnp.tril(jnp.ones((C, C), bool), -1)
    decay = jnp.exp(jnp.where(tril, gc[..., :, None] - gc[..., None, :], -jnp.inf))
    kk = jnp.einsum('nbhid,nbhjd->nbhij', kc * bc, kc) * decay
    a_mat = jnp.eye(C, dtype=jnp.float32) + jnp.where(strict, kk, 0.0)
    rhs = jnp.concatenate([vc * bc, kc * bc * jnp.exp(gc)[..., None]], axis=-1)
    sol = lax.linalg.triangular_solve(a_mat, rhs, left_side=True, lower=True, unit_diagonal=True)
    u, w = sol[..., :Dv], sol[..., Dv:]
    qk = jnp.where(tril, jnp.einsum('nbhid,nbhjd->nbhij', qc, kc) * decay, 0.0)
    q_dec = qc * jnp.exp(gc)[..., None]
    k_tail = kc * jnp.exp(gc[..., -1:] - gc)[..., None]
    g_last = jnp.exp(gc[..., -1])

    def step(S, inp):
        u_i, w_i, qk_i, qd_i, kt_i, gl_i = inp
        v_new = u_i - jnp.einsum('bhcd,bhde->bhce', w_i, S)
        o = jnp.einsum('bhcd,bhde->bhce', qd_i, S) + jnp.einsum('bhij,bhje->bhie', qk_i, v_new)
        S = S * gl_i[..., None, None] + jnp.einsum('bhcd,bhce->bhde', kt_i, v_new)
        return S, o

    S, o = lax.scan(step, s0, (u, w, qk, q_dec, k_tail, g_last))
    return o.transpose(1, 0, 3, 2, 4).reshape(B, L, H, Dv), S

def memory_attention(q, mem_k, mem_v):
    s = jnp.einsum('blhd,bmhd->bhlm', q, mem_k, preferred_element_type=jnp.float32) * (MEM_HEAD_DIM ** -0.5)
    p = jax.nn.softmax(s, axis=-1)
    return jnp.einsum('bhlm,bmhd->blhd', p, mem_v.astype(jnp.float32)).astype(q.dtype)

def moe(x2d, w_router, router_bias, w_exp_gate, w_exp_up, w_exp_down, w_sh_gate, w_sh_up, w_sh_down):
    T, D = x2d.shape
    scores = jax.nn.sigmoid(jnp.dot(x2d, w_router, preferred_element_type=jnp.float32))
    biased = scores + router_bias.astype(jnp.float32)
    grp_score = lax.top_k(biased.reshape(T, N_GROUPS, N_EXPERTS // N_GROUPS), 2)[0].sum(-1)
    _, grp_idx = lax.top_k(grp_score, TOPK_GROUPS)
    grp_mask = jnp.any(grp_idx[..., None] == jnp.arange(N_GROUPS), axis=1)
    choice = jnp.where(jnp.repeat(grp_mask, N_EXPERTS // N_GROUPS, axis=1), biased, -jnp.inf)
    _, top_idx = lax.top_k(choice, TOP_K)
    top_w = jnp.take_along_axis(scores, top_idx, axis=1)
    top_w = top_w / jnp.sum(top_w, axis=-1, keepdims=True) * ROUTE_SCALE

    TK = T * TOP_K
    flat_e = top_idx.reshape(TK)
    flat_t = jnp.repeat(jnp.arange(T, dtype=jnp.int32), TOP_K)
    flat_w = top_w.reshape(TK)
    order = jnp.argsort(flat_e)
    sorted_e = flat_e[order]
    counts = jnp.bincount(flat_e, length=N_EXPERTS)
    padded = (counts + MOE_BLOCK - 1) // MOE_BLOCK * MOE_BLOCK
    start = jnp.cumsum(counts) - counts
    pend = jnp.cumsum(padded)
    pstart = pend - padded
    dest = pstart[sorted_e] + jnp.arange(TK) - start[sorted_e]
    n_blocks = -(-(TK + N_EXPERTS * (MOE_BLOCK - 1)) // MOE_BLOCK)
    n_rows = n_blocks * MOE_BLOCK
    row_tok = jnp.full((n_rows,), T, jnp.int32).at[dest].set(flat_t[order])
    row_w = jnp.zeros((n_rows,), jnp.float32).at[dest].set(flat_w[order])
    block_e = jnp.minimum(jnp.searchsorted(pend, jnp.arange(n_blocks) * MOE_BLOCK, side='right'), N_EXPERTS - 1)
    x_pad = jnp.concatenate([x2d, jnp.zeros((1, D), x2d.dtype)], axis=0)

    def expert_block(args):
        tok, e = args
        xb = x_pad[tok]
        h = jax.nn.silu(xb @ w_exp_gate[e]) * (xb @ w_exp_up[e])
        return h @ w_exp_down[e]

    yb = lax.map(expert_block, (row_tok.reshape(n_blocks, MOE_BLOCK), block_e))
    routed = jnp.zeros((T + 1, D), jnp.float32).at[row_tok].add(
        yb.reshape(n_rows, D).astype(jnp.float32) * row_w[:, None])[:T]
    shared = (jax.nn.silu(x2d @ w_sh_gate) * (x2d @ w_sh_up)) @ w_sh_down
    return (routed + shared.astype(jnp.float32)).astype(x2d.dtype)

def decoder_layer(x, past_k, past_v, s0, conv0, mem_k, mem_v, w_in, sb_logit_bias, conv_w, gdn_A_log, gdn_dt_bias,
                  gdn_norm_w, w_br_sb, w_br_gdn, w_br_mem, w_o, ln1_g, ln1_b, w_router, router_bias, w_exp_gate,
                  w_exp_up, w_exp_down, w_sh_gate, w_sh_up, w_sh_down, ln2_g, ln2_b):
    B, L, D = x.shape
    start = past_k.shape[1]
    sb_q, sb_k, sb_v, gdn_qkv, gdn_z, gdn_b, gdn_a, mem_q, gates = _split(x @ w_in, IN_SPLITS)

    sb_k = _heads(sb_k, SB_HEADS)
    sb_v = _heads(sb_v, SB_HEADS)
    k_all = jnp.concatenate([past_k.astype(x.dtype), sb_k], axis=1)
    v_all = jnp.concatenate([past_v.astype(x.dtype), sb_v], axis=1)
    o_sb = stick_breaking(_heads(sb_q, SB_HEADS), k_all, v_all, start, sb_logit_bias).reshape(B, L, SB_W)

    conv_out, conv_new = causal_conv(gdn_qkv, conv0, conv_w)
    g_q, g_k, g_v = _split(conv_out, (GDN_QK_W, GDN_QK_W, GDN_V_W))
    beta = jax.nn.sigmoid(gdn_b.astype(jnp.float32))
    g = -jnp.exp(gdn_A_log.astype(jnp.float32)) * jax.nn.softplus(gdn_a.astype(jnp.float32) + gdn_dt_bias)
    o_gdn, s_new = gated_delta_rule(l2norm(_heads(g_q, GDN_HEADS)), l2norm(_heads(g_k, GDN_HEADS)),
                                    _heads(g_v, GDN_HEADS).astype(jnp.float32), g, beta, s0.astype(jnp.float32))
    o_gdn = o_gdn * lax.rsqrt(jnp.mean(o_gdn * o_gdn, axis=-1, keepdims=True) + RMS_EPS) * gdn_norm_w
    o_gdn = (o_gdn * jax.nn.silu(_heads(gdn_z, GDN_HEADS).astype(jnp.float32))).astype(x.dtype).reshape(B, L, GDN_V_W)

    o_mem = memory_attention(_heads(mem_q, MEM_HEADS), mem_k, mem_v).reshape(B, L, MEM_W)

    g_sb, g_gdn, g_mem = _split(jax.nn.sigmoid(gates), (D_MODEL, D_MODEL, D_MODEL))
    merged = g_sb * (o_sb @ w_br_sb) + g_gdn * (o_gdn @ w_br_gdn) + g_mem * (o_mem @ w_br_mem)
    h = layer_norm(DN_ALPHA * x + merged @ w_o, ln1_g, ln1_b)

    f = moe(h.reshape(B * L, D), w_router, router_bias, w_exp_gate, w_exp_up, w_exp_down,
            w_sh_gate, w_sh_up, w_sh_down).reshape(B, L, D)
    y = layer_norm(DN_ALPHA * h + f, ln2_g, ln2_b)
    return y, sb_k, sb_v, s_new.astype(s0.dtype), conv_new.astype(conv0.dtype)

def setup_inputs(seed: int = 0) -> dict:
    key = jax.random.key(seed)
    k = jax.random.split(key, 40)
    f32 = jnp.float32

    def nrm(i, shape, scale=1.0):
        return jax.random.normal(k[i], shape, f32) * scale

    n_pages = PAST_LEN // PAGE_SIZE
    n_used = DEC_BATCH * n_pages
    n_pool = n_used + max(1, n_used // 4)
    page_table = jax.random.permutation(k[0], n_pool)[:n_used].reshape(DEC_BATCH, n_pages).astype(jnp.int32)
    dt = jnp.exp(jax.random.uniform(k[1], (GDN_HEADS,), f32, math.log(1e-3), math.log(1e-1)))
    gdn_dt_bias = dt + jnp.log(-jnp.expm1(-dt))
    gdn_A_log = jnp.log(jax.random.uniform(k[2], (GDN_HEADS,), f32, 1.0, 16.0))
    return {
        'x_prompt': nrm(3, (BATCH, SEQ, D_MODEL)),
        'x_sample': nrm(4, (DEC_BATCH, DEC_SEQ, D_MODEL)),
        'cache_sb_k': nrm(5, (n_pool, PAGE_SIZE, SB_HEADS, SB_HEAD_DIM)),
        'cache_sb_v': nrm(6, (n_pool, PAGE_SIZE, SB_HEADS, SB_HEAD_DIM)),
        'page_table': page_table,
        'state_gdn': nrm(7, (DEC_BATCH, GDN_HEADS, GDN_K_DIM, GDN_V_DIM), GDN_K_DIM ** -0.5),
        'state_gdn_conv': nrm(8, (DEC_BATCH, GDN_CONV - 1, GDN_CONV_W)),
        'cache_mem_k': nrm(9, (DEC_BATCH, N_MEM, MEM_HEADS, MEM_HEAD_DIM)),
        'cache_mem_v': nrm(10, (DEC_BATCH, N_MEM, MEM_HEADS, MEM_HEAD_DIM)),
        'mem_prompt': nrm(11, (BATCH, N_MEM, D_MODEL)),
        'w_in': nrm(12, (D_MODEL, D_IN), D_MODEL ** -0.5),
        'sb_logit_bias': SB_BIAS_INIT + nrm(33, (SB_HEADS,), 0.1),
        'conv_w': nrm(13, (GDN_CONV, GDN_CONV_W), GDN_CONV ** -0.5),
        'gdn_A_log': gdn_A_log,
        'gdn_dt_bias': gdn_dt_bias,
        'gdn_norm_w': 1.0 + nrm(14, (GDN_V_DIM,), 0.02),
        'w_mem_k': nrm(15, (D_MODEL, MEM_W), D_MODEL ** -0.5),
        'w_mem_v': nrm(16, (D_MODEL, MEM_W), D_MODEL ** -0.5),
        'w_br_sb': nrm(17, (SB_W, D_MODEL), SB_W ** -0.5 * DN_BETA),
        'w_br_gdn': nrm(18, (GDN_V_W, D_MODEL), GDN_V_W ** -0.5 * DN_BETA),
        'w_br_mem': nrm(19, (MEM_W, D_MODEL), MEM_W ** -0.5 * DN_BETA),
        'w_o': nrm(20, (D_MODEL, D_MODEL), D_MODEL ** -0.5 * DN_BETA),
        'ln1_g': 1.0 + nrm(21, (D_MODEL,), 0.02),
        'ln1_b': nrm(22, (D_MODEL,), 0.02),
        'w_router': nrm(23, (D_MODEL, N_EXPERTS), D_MODEL ** -0.5),
        'router_bias': nrm(24, (N_EXPERTS,), 0.01),
        'w_exp_gate': nrm(25, (N_EXPERTS, D_MODEL, D_EXPERT), D_MODEL ** -0.5),
        'w_exp_up': nrm(26, (N_EXPERTS, D_MODEL, D_EXPERT), D_MODEL ** -0.5),
        'w_exp_down': nrm(27, (N_EXPERTS, D_EXPERT, D_MODEL), D_EXPERT ** -0.5 * DN_BETA),
        'w_sh_gate': nrm(28, (D_MODEL, D_SHARED), D_MODEL ** -0.5),
        'w_sh_up': nrm(29, (D_MODEL, D_SHARED), D_MODEL ** -0.5),
        'w_sh_down': nrm(30, (D_SHARED, D_MODEL), D_SHARED ** -0.5 * DN_BETA),
        'ln2_g': 1.0 + nrm(31, (D_MODEL,), 0.02),
        'ln2_b': nrm(32, (D_MODEL,), 0.02),
    }

def reference(x_prompt, x_sample, cache_sb_k, cache_sb_v, page_table, state_gdn, state_gdn_conv, cache_mem_k,
              cache_mem_v, mem_prompt, w_in, sb_logit_bias, conv_w, gdn_A_log, gdn_dt_bias, gdn_norm_w, w_mem_k,
              w_mem_v, w_br_sb, w_br_gdn, w_br_mem, w_o, ln1_g, ln1_b, w_router, router_bias, w_exp_gate, w_exp_up,
              w_exp_down, w_sh_gate, w_sh_up, w_sh_down, ln2_g, ln2_b):
    weights = (w_in, sb_logit_bias, conv_w, gdn_A_log, gdn_dt_bias, gdn_norm_w, w_br_sb, w_br_gdn, w_br_mem, w_o,
               ln1_g, ln1_b, w_router, router_bias, w_exp_gate, w_exp_up, w_exp_down, w_sh_gate, w_sh_up, w_sh_down,
               ln2_g, ln2_b)

    B = x_prompt.shape[0]
    dt = x_prompt.dtype
    mem_k_p = (mem_prompt @ w_mem_k).reshape(B, N_MEM, MEM_HEADS, MEM_HEAD_DIM)
    mem_v_p = (mem_prompt @ w_mem_v).reshape(B, N_MEM, MEM_HEADS, MEM_HEAD_DIM)
    empty_kv = jnp.zeros((B, 0, SB_HEADS, SB_HEAD_DIM), dt)
    s0 = jnp.zeros((B, GDN_HEADS, GDN_K_DIM, GDN_V_DIM), dt)
    c0 = jnp.zeros((B, GDN_CONV - 1, GDN_CONV_W), dt)
    y_prompt, sb_k_p, sb_v_p, s_p, c_p = decoder_layer(x_prompt, empty_kv, empty_kv, s0, c0, mem_k_p, mem_v_p, *weights)

    DB, n_pages = page_table.shape
    past_k = cache_sb_k[page_table].reshape(DB, n_pages * PAGE_SIZE, SB_HEADS, SB_HEAD_DIM)
    past_v = cache_sb_v[page_table].reshape(DB, n_pages * PAGE_SIZE, SB_HEADS, SB_HEAD_DIM)
    y_sample, sb_k_s, sb_v_s, s_s, c_s = decoder_layer(x_sample, past_k, past_v, state_gdn, state_gdn_conv,
                                                       cache_mem_k, cache_mem_v, *weights)
    return (y_prompt, y_sample, sb_k_p, sb_v_p, s_p, c_p, mem_k_p, mem_v_p, sb_k_s, sb_v_s, s_s, c_s)


_drawn_inputs = setup_inputs


def setup_inputs(seed=0):
    import zlib

    import numpy as np

    out = dict(_drawn_inputs(seed))
    spreads = {}
    factors = {'sb_logit_bias': 8.0,
     'ln2_g': 24.222,
     'ln2_b': 22.95,
     'gdn_norm_w': 4.104,
     'cache_mem_k': 4.471,
     'cache_mem_v': 3.65}
    for name, (base, spread) in spreads.items():
        noise = np.random.default_rng([zlib.crc32(name.encode()), seed]).standard_normal(out[name].shape)
        drawn = base * np.exp(spread * noise) if base else spread * noise
        out[name] = jnp.asarray(drawn.astype(out[name].dtype))
    for name, factor in factors.items():
        out[name] = (out[name] * factor).astype(out[name].dtype)
    return out
```

```python
import numpy as np
from contextlib import ExitStack

import concourse.bass as bass
import concourse.mybir as mybir

F32 = mybir.dt.float32
I32 = mybir.dt.int32
ALU = mybir.AluOpType
ACT = mybir.ActivationFunctionType
AX = mybir.AxisListType

P = 128
D = 1024
KC = D // P
SEQ = 512
NB = 8
T = SEQ + NB
TH = T // 2
NT = SEQ // P
H = 8
HD = 64
MH = 4
NM = 256
PAST = 512
PG = PAST // P
N_POOL = 40
SBW = H * HD
D_IN = 7184
CQ, CK, CV, CG, CZ, CM = 0, 4, 8, 12, 24, 28
NCH = 32
BA0 = 3584
MQ0 = 3600
GT0 = 4112
NE = 64
NG = 8
DE = 256
TOPK = 8
CAP = 128
NOV = T * TOPK // CAP
NBLK = NE + NOV
ALPHA = 2.0 ** 0.25
LN_EPS = 1e-5
RMS_EPS = 1e-6
L2_EPS = 1e-6
ROUTE_SCALE = 2.5
BIG = 1e30


class Shared:
    pass


class Link:

    def __init__(self, eng, sem):
        self.eng, self.sem, self.n, self.off = eng, sem, 0, 0

    def __call__(self, ins):
        self.n += 1
        ins.then_inc(self.sem, 1)
        self.eng.wait_ge(self.sem, self.off + self.n)
        return ins

    def loop(self, i, per, base):
        self.off, self.n = i * per + base, 0

    def after(self, total):
        self.off, self.n = 0, total


def tok_tiles():
    return [(t * P, P) for t in range(NT)] + [(SEQ, NB)]


def phase_load(nc, g, x):
    s_const, s_zero, s_bones, s_tp, s_cp = (g.sem(n) for n in
        ("const_ready", "fills_ready", "block_ones_ready", "x_transposed", "xt_copied"))
    s_xl = [g.sem(f"x_loaded{i}") for i in range(3)]
    s_small = g.sem("small_loaded")
    with ExitStack() as ctx:
        xt = ctx.enter_context(nc.sbuf_tensor("x_rows", [P, NT + 1, D], F32))
        mt = ctx.enter_context(nc.sbuf_tensor("mem_rows", [P, 2, D], F32))
        rows = [(xt[:, t, :], P) for t in range(NT)] + [(xt[0:NB, NT, :], NB)] + [(mt[:, m, :], P) for m in range(2)]
        outs = [g.XT[:, :, t * P:(t + 1) * P] for t in range(NT)] + [g.XT[:, :, SEQ:T]] + \
               [g.MT[:, :, m * P:(m + 1) * P] for m in range(2)]
        land = [s_xl[0]] * NT + [s_xl[1]] + [s_xl[2]] * 2
        block = ctx.enter_context(nc.Block())

        @block.sync
        def _(sp):
            sp.dma_start(xt[:, 0:NT, :], x["x_prompt"].rearrange("b (t p) d -> p (b t) d", p=P)).then_inc(s_xl[0], 16)
            sp.dma_start(xt[0:NB, NT, :], x["x_sample"].rearrange("b o d -> (b o) d")).then_inc(s_xl[1], 16)
            sp.dma_start(mt[:, :, :], x["mem_prompt"].rearrange("b (t p) d -> p (b t) d", p=P)).then_inc(s_xl[2], 16)
            small = [(g.A_bc, x["gdn_A_log"]), (g.dt_bc, x["gdn_dt_bias"]), (g.sbb_bc, x["sb_logit_bias"]),
                     (g.rb_bc, x["router_bias"])]
            for dst, src in small:
                sp.dma_start(dst[:, :], src.partition_broadcast(P)).then_inc(s_small, 16)
            for half in range(2):
                sp.dma_start(g.nw_col[half * HD:(half + 1) * HD, :], x["gdn_norm_w"].rearrange("(p o) -> p o", o=1)).then_inc(s_small, 16)
            sp.wait_ge(s_small, 16 * (len(small) + 2))

        @block.gpsimd
        def _(pool):
            for z in (g.ident[:, :], g.LM[:, :, :]):
                pool.memset(z, 0.0).then_inc(s_zero, 1)
            for z, v in ((g.ones, 1.0), (g.nones, -1.0), (g.UT, 1.0), (g.UTs, 1.0), (g.TRI, -1.0)):
                pool.memset(z[:, :], v).then_inc(s_zero, 1)
            for z, v in ((g.one_c, 1.0), (g.eps_l2, L2_EPS), (g.eps_ln, LN_EPS), (g.S[:, :, :], 0.0)):
                pool.memset(z, v).then_inc(s_zero, 1)
            pool.wait_ge(s_zero, 11)
            pool.affine_select(out=g.ident[:, :], in_=g.ident[:, :], compare_op=ALU.not_equal, fill=1.0,
                               base=0, pattern=[[-1, P]], channel_multiplier=1).then_inc(s_const, 1)
            pool.affine_select(out=g.UT[:, :], in_=g.UT[:, :], compare_op=ALU.is_ge, fill=0.0,
                               base=0, pattern=[[1, P]], channel_multiplier=-1).then_inc(s_const, 1)
            pool.affine_select(out=g.UTs[:, :], in_=g.UTs[:, :], compare_op=ALU.is_gt, fill=0.0,
                               base=0, pattern=[[1, P]], channel_multiplier=-1).then_inc(s_const, 1)
            pool.affine_select(out=g.TRI[:, :], in_=g.TRI[:, :], compare_op=ALU.is_ge, fill=0.0,
                               base=0, pattern=[[-1, P]], channel_multiplier=1).then_inc(s_const, 1)
            for n in range(7):
                s = 1 << n
                v = g.LM[:, n, :].rearrange("p (b h s) -> p b h s", h=2, s=s)[:, :, 1, :]
                nb = P // (2 * s)
                pool.memset(v, 1.0).then_inc(s_zero, 1)
                pool.wait_ge(s_zero, 12 + 3 * n)
                pool.affine_select(out=v, in_=v, compare_op=ALU.is_ge, fill=0.0, base=0,
                                   pattern=[[-2 * s, nb], [0, s]], channel_multiplier=1).then_inc(s_zero, 1)
                pool.wait_ge(s_zero, 13 + 3 * n)
                pool.affine_select(out=v, in_=v, compare_op=ALU.is_ge, fill=0.0, base=s - 1,
                                   pattern=[[2 * s, nb], [0, s]], channel_multiplier=-1).then_inc(s_zero, 1)
            pool.iota(g.iota_p[:, :], pattern=[[0, 1]], base=0, channel_multiplier=1).then_inc(s_const, 1)
            pool.iota(g.iota_e[:, :], pattern=[[CAP, NE]], base=0, channel_multiplier=0).then_inc(s_const, 1)

        @block.tensor
        def _(pe):
            pe.wait_ge(s_const, 1)
            for n, (src, m) in enumerate(rows):
                pe.wait_ge(land[n], 16)
                if n >= 2:
                    pe.wait_ge(s_cp, n - 1)
                for k in range(KC):
                    ins = nc.tensor.transpose(g.PS[:, 2 * (n % 2) + k // 4, (k % 4) * P:(k % 4) * P + m],
                                              src[:, k::KC], g.ident[0:m, 0:m])
                ins.then_inc(s_tp, 1)

        @block.vector
        def _(dve):
            nc.vector.memset(g.bones[:, :], 0.0).then_inc(s_bones, 1)
            dve.wait_ge(s_bones, 1)
            for half in range(2):
                q = slice(half * HD, (half + 1) * HD)
                nc.vector.memset(g.bones[q, q], 1.0).then_inc(s_bones, 1)
            for n, (_, m) in enumerate(rows):
                dve.wait_ge(s_tp, n + 1)
                src = g.PS[:, 2 * (n % 2):2 * (n % 2) + 2, :].rearrange("p b (k m) -> p (b k) m", m=P)[:, :, 0:m]
                nc.vector.tensor_copy(outs[n], src).then_inc(s_cp, 1)


def proj_cols(nc, g, src, col0, out0, n_slots, name, sigmoid=False):
    s_w = [g.sem(f"{name}_w{i}_loaded") for i in range(2)]
    s_mm, s_free = g.sem(f"{name}_chunk_done"), g.sem(f"{name}_banks_free")
    wv = src.rearrange("(p k) n -> p k n", k=KC)
    with ExitStack() as ctx:
        W = [ctx.enter_context(nc.sbuf_tensor(f"{name}_w{i}", [P, KC, 256], F32)) for i in range(2)]
        block = ctx.enter_context(nc.Block())

        @block.sync
        def _(sp):
            with sp.Fori(0, n_slots // 2) as i:
                for b in range(2):
                    sp.wait_ge(s_free, i * 4 + 2 * b + 1)
                    sp.dma_start(W[b][:, :, :], wv[:, :, bass.ds(i * 512 + col0 + b * 256, 256)]).then_inc(s_w[b], 16)

        @block.tensor
        def _(pe):
            with pe.Fori(0, n_slots // 2) as i:
                for b in range(2):
                    pe.wait_ge(s_w[b], i * 16 + 16)
                    for c in range(2):
                        pe.wait_ge(s_free, i * 4 + 2 * b + c + 2)
                        for h in range(2):
                            for k in range(KC):
                                ins = nc.tensor.matmul(g.PS[:, 2 * c + h, 0:TH], W[b][:, k, c * P:(c + 1) * P],
                                                       g.XT[:, k, h * TH:(h + 1) * TH], start=k == 0, stop=k == KC - 1)
                        ins.then_inc(s_mm, 1)

        target = lambda i, n: g.PT[:, bass.ds(i * 4 + out0 + n, 1), :].rearrange("p o (h t) -> p (o h) t", h=2)

        def copies(dve):
            dve.sem_inc(s_free, 3)
            with dve.Fori(0, n_slots // 2) as i:
                for n in range(4):
                    dve.wait_ge(s_mm, i * 4 + n + 1)
                    nc.vector.tensor_copy(target(i, n), g.PS[:, 2 * (n % 2):2 * (n % 2) + 2, 0:TH]).then_inc(s_free, 1)

        def sigmoids(act):
            act.sem_inc(s_free, 3)
            with act.Fori(0, n_slots // 2) as i:
                for n in range(4):
                    act.wait_ge(s_mm, i * 4 + n + 1)
                    nc.scalar.activation(target(i, n), g.PS[:, 2 * (n % 2):2 * (n % 2) + 2, 0:TH], ACT.Sigmoid).then_inc(s_free, 1)

        block.scalar(sigmoids) if sigmoid else block.vector(copies)


def phase_small(nc, g, x, y):
    s_w = [g.sem(f"small_w{i}_loaded") for i in range(3)]
    s_mm, s_cp, s_mkt, s_mktc, s_out = (g.sem(n) for n in
        ("small_mm_done", "small_copied", "mem_kt_done", "mem_kt_copied", "mem_kv_stored"))
    with ExitStack() as ctx:
        wba = ctx.enter_context(nc.sbuf_tensor("w_ba", [P, KC, 16], F32))
        wm = ctx.enter_context(nc.sbuf_tensor("w_mem", [P, 2, KC, MH * P], F32))
        mk = ctx.enter_context(nc.sbuf_tensor("mem_k", [P, 2, MH * P], F32))
        block = ctx.enter_context(nc.Block())

        @block.sync
        def _(sp):
            with nc.allow_non_contiguous_dma(reason="16 columns of w_in"):
                sp.dma_start(wba[:, :, :], x["w_in"].rearrange("(p k) n -> p k n", k=KC)[:, :, BA0:BA0 + 16]).then_inc(s_w[0], 16)
            sp.dma_start(wm[:, 0, :, :], x["w_mem_k"].rearrange("(p k) n -> p k n", k=KC)).then_inc(s_w[1], 16)
            sp.dma_start(wm[:, 1, :, :], x["w_mem_v"].rearrange("(p k) n -> p k n", k=KC)).then_inc(s_w[2], 16)
            for j, (dst, src) in enumerate(((y["mem_k_prompt"], mk), (y["mem_v_prompt"], g.MV))):
                sp.wait_ge(s_cp, 3 + 2 * j)
                sp.dma_start(dst.rearrange("b (m p) h d -> p (b m) (h d)", p=P), src[:, :, :]).then_inc(s_out, 16)
            sp.wait_ge(s_out, 32)

        @block.tensor
        def _(pe):
            pe.wait_ge(s_w[0], 16)
            for h in range(2):
                for k in range(KC):
                    ins = nc.tensor.matmul(g.PS[0:16, h, 0:TH], wba[:, k, :], g.XT[:, k, h * TH:(h + 1) * TH],
                                           start=k == 0, stop=k == KC - 1)
            ins.then_inc(s_mm, 1)
            for j in range(2):
                pe.wait_ge(s_w[1 + j], 16)
                for m in range(2):
                    for k in range(KC):
                        ins = nc.tensor.matmul(g.PS[:, 2 + 2 * j + m, :], g.MT[:, k, m * P:(m + 1) * P], wm[:, j, k, :],
                                               start=k == 0, stop=k == KC - 1)
                    ins.then_inc(s_mm, 1)
            pe.wait_ge(s_cp, 3)
            for h in range(MH):
                for m in range(2):
                    ins = nc.tensor.transpose(g.PS[:, 6 + h // 2, (h % 2) * NM + m * P:(h % 2) * NM + (m + 1) * P],
                                              mk[:, m, h * P:(h + 1) * P], g.ident[:, :])
            ins.then_inc(s_mkt, 1)

        @block.vector
        def _(dve):
            dve.wait_ge(s_mm, 1)
            nc.vector.tensor_copy(g.BA[:, :].rearrange("p (h t) -> p h t", h=2), g.PS[0:16, 0:2, 0:TH]).then_inc(s_cp, 1)
            for j, dst in enumerate((mk, g.MV)):
                for m in range(2):
                    dve.wait_ge(s_mm, 2 + 2 * j + m)
                    nc.vector.tensor_copy(dst[:, m, :], g.PS[:, 2 + 2 * j + m, :]).then_inc(s_cp, 1)
            dve.wait_ge(s_mkt, 1)
            nc.vector.tensor_copy(g.MKT[:, :, :], g.PS[:, 6:8, :].rearrange("p b (h m) -> p (b h) m", m=NM)).then_inc(s_mktc, 1)


def phase_rows(nc, g, x, y):
    s_cw, s_tp, s_cp, s_out, s_v = (g.sem(n) for n in
        ("conv_w_loaded", "rows_transposed", "rows_copied", "rows_stored", "rows_v_copied"))
    with ExitStack() as ctx:
        krows = ctx.enter_context(nc.sbuf_tensor("k_rows", [P, NT, SBW], F32))
        crow = ctx.enter_context(nc.sbuf_tensor("conv_rows", [3, 1536], F32))
        cw = ctx.enter_context(nc.sbuf_tensor("conv_w_rows", [4, 1536], F32))
        jobs = []
        for src0, dst in ((CK, krows), (CV, g.VT)):
            for t in range(NT):
                jobs.append(([(j * P, g.PT[:, src0 + j, t * P:(t + 1) * P], P, P) for j in range(4)],
                             dst[:, t, :], lambda b: g.PS[:, b, :]))
        for j in range(3):
            jobs.append(([(i * P, g.PT[:, CG + 4 * j + i, SEQ - 3:SEQ], P, 3) for i in range(4)],
                         crow[:, j * 512:(j + 1) * 512], lambda b: g.PS[0:3, b, :]))
        for j in range(8):
            col = j * 512 if j < 7 else MQ0
            jobs.append(([(i * P, g.PT[:, 4 * j + i, SEQ:T], P, NB) for i in range(4)],
                         g.XS[:, col:col + 512], lambda b: g.PS[0:NB, b, :]))
        jobs.append(([(0, g.BA[:, SEQ:T], 16, NB)], g.XS[:, BA0:BA0 + 16], lambda b: g.PS[0:NB, b, 0:16]))
        jobs.append(([(4 * j, cw[:, j * P:(j + 1) * P], 4, P) for j in range(12)],
                     g.CW[:, :, :], lambda b: g.PS[:, b, 0:48].rearrange("p (c k) -> p c k", k=4)))
        block = ctx.enter_context(nc.Block())

        @block.sync
        def _(sp):
            sp.dma_start(cw[:, :], x["conv_w"]).then_inc(s_cw, 16)
            sp.dma_start(y["conv_sample"][:, 0:2, :], x["state_gdn_conv"][:, 1:3, :]).then_inc(s_out, 16)
            sp.wait_ge(s_cp, 4)
            sp.dma_start(y["sb_k_prompt"].rearrange("b (t p) h d -> p (b t) (h d)", p=P), krows[:, :, :]).then_inc(s_out, 16)
            sp.wait_ge(s_cp, 8)
            sp.dma_start(y["sb_v_prompt"].rearrange("b (t p) h d -> p (b t) (h d)", p=P), g.VT[:, :, :]).then_inc(s_out, 16)
            sp.wait_ge(s_cp, 11)
            sp.dma_start(y["conv_prompt"].rearrange("b r n -> (b r) n"), crow[:, :]).then_inc(s_out, 16)
            sp.wait_ge(s_cp, 19)
            sp.dma_start(y["conv_sample"].rearrange("b r n -> b (r n)")[:, 2 * 1536:3 * 1536], g.XS[:, 1536:3072]).then_inc(s_out, 16)
            sp.dma_start(y["sb_k_sample"].rearrange("b o h d -> b (o h d)"), g.XS[:, 512:1024]).then_inc(s_out, 16)
            sp.dma_start(y["sb_v_sample"].rearrange("b o h d -> b (o h d)"), g.XS[:, 1024:1536]).then_inc(s_out, 16)
            sp.wait_ge(s_out, 16 * 7)

        @block.tensor
        def _(pe):
            for n, (parts, _, _) in enumerate(jobs):
                if n >= 4:
                    pe.wait_ge(s_cp, n - 3)
                if n == len(jobs) - 1:
                    pe.wait_ge(s_cw, 16)
                for col, src, k, m in parts:
                    w = src.shape[-1]
                    ins = nc.tensor.transpose(g.PS[0:w, n % 4, col:col + k], src, g.ident[0:k, 0:k])
                ins.then_inc(s_tp, 1)

        @block.vector
        def _(dve):
            for n, (_, dst, src) in enumerate(jobs):
                dve.wait_ge(s_tp, n + 1)
                nc.vector.tensor_copy(dst, src(n % 4)).then_inc(s_cp, 1)


def phase_sb(nc, g):
    OFF, W = [0, 512, 1024, 896], [512, 384, 256, 128]
    NC_ = 1280
    s_z, s_zs, s_ab, s_lg, s_sp, s_spm, s_cum, s_w, s_a, s_am, s_av, s_ot = (g.sem(n) for n in
        ("sb_z_done", "sb_z_copied", "sb_abs_ready", "sb_log_ready", "sb_softplus_ready", "sb_softplus_masked",
         "sb_cum_done", "sb_w_ready", "sb_a_ready", "sb_a_masked", "sb_av_done", "sb_o_copied"))
    s_al = g.sem("sb_act_link")
    with ExitStack() as ctx:
        zs, sp_, a_ = (ctx.enter_context(nc.sbuf_tensor(n, [P, 2, NC_], F32)) for n in ("sb_zs", "sb_sp", "sb_a"))
        ab = ctx.enter_context(nc.sbuf_tensor("sb_ab", [P, NC_], F32))
        Z = g.PS[:, 0:3, :].rearrange("p b n -> p (b n)")[:, 0:NC_]
        C = g.PS[:, 3:6, :].rearrange("p b n -> p (b n)")[:, 0:NC_]
        block = ctx.enter_context(nc.Block())

        @block.tensor
        def _(pe):
            def scores(h):
                c, r = h // 2, HD * (h % 2)
                if h >= 1:
                    pe.wait_ge(s_zs, h)
                for b in range(4):
                    ins = nc.tensor.matmul(Z[:, OFF[b]:OFF[b] + W[b]], g.PT[r:r + HD, CK + c, b * P:(b + 1) * P],
                                           g.PT[r:r + HD, CQ + c, b * P:SEQ], start=True, stop=True)
                ins.then_inc(s_z, 1)

            def cumulate(h):
                pe.wait_ge(s_spm, 4 * (h + 1))
                if h >= 1:
                    pe.wait_ge(s_w, h)
                for b in (0, 1, 3, 2):
                    for m in range(b, 4):
                        lo = (m - b) * P
                        ins = nc.tensor.matmul(C[:, OFF[b] + lo:OFF[b] + W[b]], (g.TRI if m == b else g.nones)[:, :],
                                               sp_[:, h % 2, OFF[m]:OFF[m] + W[m]], start=m == b, stop=m == 3)
                ins.then_inc(s_cum, 1)

            def values(h):
                c, r = h // 2, HD * (h % 2)
                pe.wait_ge(s_am, 4 * (h + 1))
                if h >= 4 and h % 2 == 0:
                    pe.wait_ge(s_ot, h // 2 - 1)
                for b in range(4):
                    ins = nc.tensor.matmul(g.PS[r:r + HD, 6 + c % 2, b * P:SEQ], g.VT[:, b, h * HD:(h + 1) * HD],
                                           a_[:, h % 2, OFF[b]:OFF[b] + W[b]], start=b == 0, stop=b == 3)
                ins.then_inc(s_av, 1)

            scores(0)
            for s in range(H + 2):
                if s + 1 < H:
                    scores(s + 1)
                if s < H:
                    cumulate(s)
                if s >= 2:
                    values(s - 2)

        @block.scalar
        def _(act):
            link = Link(act, s_al)

            def weights(h):
                act.wait_ge(s_w, h + 1)
                nc.scalar.activation(a_[:, h % 2, :], a_[:, h % 2, :], ACT.Exp).then_inc(s_a, 1)

            for h in range(H):
                act.wait_ge(s_z, h + 1)
                if h >= 2:
                    act.wait_ge(s_w, h - 1)
                nc.scalar.activation(zs[:, h % 2, :], Z, ACT.Identity, scale=HD ** -0.5,
                                     bias=g.sbb_bc[:, h:h + 1]).then_inc(s_zs, 1)
                act.wait_ge(s_ab, h + 1)
                link(nc.scalar.activation(ab[:, :], ab[:, :], ACT.Exp))
                nc.scalar.activation(ab[:, :], ab[:, :], ACT.Ln, bias=g.one_c).then_inc(s_lg, 1)
                if h >= 1:
                    weights(h - 1)
            weights(H - 1)

        @block.vector
        def _(dve):
            def add(h):
                dve.wait_ge(s_cum, h + 1)
                if h >= 2:
                    dve.wait_ge(s_av, h - 1)
                nc.vector.tensor_tensor(a_[:, h % 2, :], C, zs[:, h % 2, :], ALU.add).then_inc(s_w, 1)

            def copy_out(c):
                dve.wait_ge(s_av, 2 * c + 2)
                nc.vector.tensor_copy(g.OT[:, c, 0:SEQ], g.PS[:, 6 + c % 2, :]).then_inc(s_ot, 1)

            for h in range(H):
                dve.wait_ge(s_zs, h + 1)
                if h >= 1:
                    dve.wait_ge(s_sp, h)
                nc.vector.scalar_tensor_tensor(out=ab[:, :], in0=zs[:, h % 2, :], scalar=-1.0, in1=zs[:, h % 2, :],
                                               op0=ALU.mult, op1=ALU.min).then_inc(s_ab, 1)
                dve.wait_ge(s_lg, h + 1)
                if h >= 2:
                    dve.wait_ge(s_cum, h - 1)
                nc.vector.scalar_tensor_tensor(out=sp_[:, h % 2, :], in0=zs[:, h % 2, :], scalar=0.0, in1=ab[:, :],
                                               op0=ALU.max, op1=ALU.add).then_inc(s_sp, 1)
                if h >= 1:
                    add(h - 1)
                if h >= 4 and h % 2 == 0:
                    copy_out(h // 2 - 2)
            add(H - 1)
            copy_out(2)
            copy_out(3)

        @block.gpsimd
        def _(pool):
            def mask(buf, h, sem):
                for b in range(4):
                    v = buf[:, h % 2, OFF[b]:OFF[b] + P]
                    pool.affine_select(out=v, in_=v, compare_op=ALU.is_gt, fill=0.0, base=0,
                                       pattern=[[1, P]], channel_multiplier=-1).then_inc(sem, 1)

            for h in range(H):
                pool.wait_ge(s_sp, h + 1)
                mask(sp_, h, s_spm)
                if h >= 1:
                    pool.wait_ge(s_a, h)
                    mask(a_, h - 1, s_am)
            pool.wait_ge(s_a, H)
            mask(a_, H - 1, s_am)


def phase_mem(nc, g):
    SC = P ** -0.5
    s_s, s_mx, s_e, s_p, s_pt, s_ptc, s_o, s_oc = (g.sem(n) for n in
        ("mem_s_done", "mem_max_ready", "mem_exp_ready", "mem_p_ready", "mem_pt_done", "mem_pt_copied",
         "mem_o_done", "mem_o_copied"))
    s_dl, s_se = g.sem("mem_dve_link"), g.sem("mem_sum_ready")
    with ExitStack() as ctx:
        pr = ctx.enter_context(nc.sbuf_tensor("mem_pr", [P, 2, NT, NM], F32))
        pt = ctx.enter_context(nc.sbuf_tensor("mem_pt", [P, 2, SEQ], F32))
        mx, sm = (ctx.enter_context(nc.sbuf_tensor(n, [P, MH, NT], F32)) for n in ("mem_mx", "mem_sm"))
        block = ctx.enter_context(nc.Block())
        S_ = lambda h: g.PS[:, 2 * (h % 2):2 * (h % 2) + 2, :].rearrange("p b (t m) -> p (b t) m", m=NM)

        @block.tensor
        def _(pe):
            def scores(h):
                if h >= 2:
                    pe.wait_ge(s_e, 4 * (h - 1))
                for t in range(NT):
                    ins = nc.tensor.matmul(S_(h)[:, t, :], g.PT[:, CM + h, t * P:(t + 1) * P], g.MKT[:, h, :],
                                           start=True, stop=True)
                ins.then_inc(s_s, 1)

            scores(0)
            for h in range(MH):
                if h + 1 < MH:
                    scores(h + 1)
                pe.wait_ge(s_p, h + 1)
                if h >= 1:
                    pe.wait_ge(s_ptc, h)
                for m in range(2):
                    for t in range(NT):
                        ins = nc.tensor.transpose(g.PS[:, 4 + m, t * P:(t + 1) * P], pr[:, h % 2, t, m * P:(m + 1) * P],
                                                  g.ident[:, :])
                ins.then_inc(s_pt, 1)
                pe.wait_ge(s_ptc, h + 1)
                if h >= 2:
                    pe.wait_ge(s_oc, h - 1)
                for m in range(2):
                    ins = nc.tensor.matmul(g.PS[:, 6 + h % 2, :], g.MV[:, m, h * P:(h + 1) * P], pt[:, m, :],
                                           start=m == 0, stop=m == 1)
                ins.then_inc(s_o, 1)

        @block.scalar
        def _(act):
            for h in range(MH):
                act.wait_ge(s_mx, h + 1)
                if h >= 2:
                    act.wait_ge(s_pt, h - 1)
                for t in range(NT):
                    nc.scalar.activation(pr[:, h % 2, t, :], S_(h)[:, t, :], ACT.Exp, bias=mx[:, h, t:t + 1],
                                         scale=SC, accum_out=sm[:, h, t:t + 1]).then_inc(s_e, 1)

        @block.vector
        def _(dve):
            link = Link(dve, s_dl)

            def maxima(h):
                dve.wait_ge(s_s, h + 1)
                link(nc.vector.tensor_reduce(mx[:, h, :], S_(h), AX.X, ALU.max))
                nc.vector.tensor_scalar(mx[:, h, :], mx[:, h, :], -SC, None, ALU.mult).then_inc(s_mx, 1)

            maxima(0)
            for h in range(MH):
                dve.wait_ge(s_e, 4 * (h + 1))
                link(nc.vector.reciprocal(sm[:, h, :], sm[:, h, :]))
                nc.vector.tensor_tensor(pr[:, h % 2, :, :], pr[:, h % 2, :, :],
                                        sm[:, h, :].unsqueeze(2).to_broadcast([P, NT, NM]), ALU.mult).then_inc(s_p, 1)
                if h + 1 < MH:
                    maxima(h + 1)
                dve.wait_ge(s_pt, h + 1)
                if h >= 1:
                    dve.wait_ge(s_o, h)
                nc.vector.tensor_copy(pt[:, :, :], g.PS[:, 4:6, :]).then_inc(s_ptc, 1)
                dve.wait_ge(s_o, h + 1)
                nc.vector.tensor_copy(g.OT[:, 8 + h, 0:SEQ], g.PS[:, 6 + h % 2, :]).then_inc(s_oc, 1)


def phase_gdn_prep(nc, g):
    NTH = NT * H
    s_cv, s_si, s_sq, s_ss, s_rs, s_qk, s_tp, s_cp = (g.sem(n) for n in
        ("conv_sum_ready", "silu_ready", "square_ready", "sumsq_done", "rnorm_ready", "qk_normed", "kv_transposed", "kv_copied"))
    s_dl, s_al = g.sem("prep_dve_link"), g.sem("prep_act_link")
    s_bt, s_xa, s_lg, s_g, s_gc, s_gs, s_gt, s_eg, s_beta, s_eA = (g.sem(n) for n in
        ("ba_transposed", "decay_in_ready", "decay_log_ready", "decay_ready", "decay_sums_done", "decay_sums_copied",
         "decay_row_done", "decay_exp_ready", "beta_ready", "exp_a_ready"))
    with ExitStack() as ctx:
        sb = lambda n, s: ctx.enter_context(nc.sbuf_tensor(n, s, F32))
        tmp, sq, rs = sb("conv_tmp", [P, 2, SEQ]), sb("norm_sq", [P, 2, SEQ]), sb("norm_rs", [P, 2, SEQ])
        bt, xa, t1, gg = sb("bt", [P, NT, 16]), sb("decay_xa", [P, NTH]), sb("decay_t1", [P, NTH]), sb("decay_g", [P, NTH])
        tot, ea = sb("decay_tot", [P, NTH]), sb("exp_a", [P, H])
        th = lambda v: v.rearrange("p (t h) -> p t h", h=H)
        src = lambda c: g.PT[:, CG + c, 0:SEQ]
        block = ctx.enter_context(nc.Block())

        @block.vector
        def _(dve):
            link = Link(dve, s_dl)
            dve.wait_ge(s_bt, 1)
            link(nc.vector.tensor_copy(bt[:, :, :], g.PS[:, 7, 0:64].rearrange("p (t c) -> p t c", c=16)))
            link(nc.vector.tensor_tensor(th(xa[:, :]), bt[:, :, H:2 * H],
                                         g.dt_bc[:, :].unsqueeze(1).to_broadcast([P, NT, H]), ALU.add))
            nc.vector.scalar_tensor_tensor(out=t1[:, :], in0=xa[:, :], scalar=-1.0, in1=xa[:, :],
                                           op0=ALU.mult, op1=ALU.min).then_inc(s_xa, 1)
            dve.wait_ge(s_lg, 1)
            link(nc.vector.scalar_tensor_tensor(out=gg[:, :], in0=xa[:, :], scalar=0.0, in1=t1[:, :],
                                                op0=ALU.max, op1=ALU.add))
            dve.wait_ge(s_eA, 1)
            link(nc.vector.tensor_tensor(th(gg[:, :]), th(gg[:, :]), ea[:, :].unsqueeze(1).to_broadcast([P, NT, H]), ALU.mult))
            nc.vector.tensor_scalar(gg[:, :], gg[:, :], -1.0, None, ALU.mult).then_inc(s_g, 1)
            dve.wait_ge(s_gc, 2)
            nc.vector.tensor_copy(g.GC[:, :], g.PS[:, 7, 64:96]).then_inc(s_gs, 1)
            link(nc.vector.tensor_copy(tot[:, :], g.PS[:, 7, 96:128]))
            link(nc.vector.tensor_tensor(g.TAIL[:, :], tot[:, :], g.PS[:, 7, 64:96], ALU.subtract))
            for half in range(2):
                q = slice(half * HD, (half + 1) * HD)
                nc.vector.tensor_copy(g.EGL[q, :, :], th(tot[q, :])[:, :, half::2]).then_inc(s_gs, 1)
            dve.wait_ge(s_gt, 1)
            nc.vector.tensor_copy(g.GCT[:, :], g.PS[0:NTH, 6, 0:P]).then_inc(s_gs, 1)

            for c in range(12):
                if c >= 2:
                    dve.wait_ge(s_si, c - 1)
                b = tmp[:, c % 2, :]
                link(nc.vector.tensor_scalar(b, src(c), g.CW[:, c, 3:4], None, ALU.mult))
                for k in (2, 1, 0):
                    o = 3 - k
                    ins = nc.vector.scalar_tensor_tensor(out=b[:, o:SEQ], in0=g.PT[:, CG + c, 0:SEQ - o], scalar=g.CW[:, c, k:k + 1],
                                                         in1=b[:, o:SEQ], op0=ALU.mult, op1=ALU.add)
                    if k:
                        link(ins)
                ins.then_inc(s_cv, 1)
            for c in range(8):
                dve.wait_ge(s_rs, c + 1)
                nc.vector.scalar_tensor_tensor(out=src(c), in0=src(c), scalar=HD ** -0.5 if c < 4 else 1.0, in1=rs[:, c % 2, :],
                                               op0=ALU.mult, op1=ALU.mult).then_inc(s_qk, 1)
            for n in range(2 * NT):
                dve.wait_ge(s_tp, n + 1)
                dst = g.VTM if n < NT else g.KTM
                nc.vector.tensor_copy(dst[:, n % NT, :], g.PS[:, 2 + n % 4, :]).then_inc(s_cp, 1)

        @block.scalar
        def _(act):
            link = Link(act, s_al)
            nc.scalar.activation(ea[:, :], g.A_bc[:, :], ACT.Exp).then_inc(s_eA, 1)
            act.wait_ge(s_xa, 1)
            link(nc.scalar.activation(t1[:, :], t1[:, :], ACT.Exp))
            nc.scalar.activation(t1[:, :], t1[:, :], ACT.Ln, bias=g.one_c).then_inc(s_lg, 1)
            act.wait_ge(s_gs, 4)
            nc.scalar.activation(g.EGC[:, :], g.GC[:, :], ACT.Exp).then_inc(s_eg, 1)
            nc.scalar.activation(g.TAIL[:, :], g.TAIL[:, :], ACT.Exp).then_inc(s_eg, 1)
            nc.scalar.activation(g.EGL[:, :, :], g.EGL[:, :, :], ACT.Exp).then_inc(s_eg, 1)
            nc.scalar.activation(g.BETA[:, :].rearrange("p (t h) -> p t h", h=H), bt[:, :, 0:H], ACT.Sigmoid).then_inc(s_beta, 1)
            for c in range(12):
                act.wait_ge(s_cv, c + 1)
                nc.scalar.activation(src(c), tmp[:, c % 2, :], ACT.Silu).then_inc(s_si, 1)
            for c in range(4):
                nc.scalar.activation(g.PT[:, CZ + c, :], g.PT[:, CZ + c, :], ACT.Silu).then_inc(s_beta, 1)
            act.wait_ge(s_si, 12)

            def square(c):
                if c >= 2:
                    act.wait_ge(s_ss, c - 1)
                nc.scalar.activation(sq[:, c % 2, :], src(c), ACT.Square).then_inc(s_sq, 1)

            square(0)
            for c in range(8):
                if c < 7:
                    square(c + 1)
                act.wait_ge(s_ss, c + 1)
                if c >= 2:
                    act.wait_ge(s_qk, c - 1)
                link(nc.scalar.activation(rs[:, c % 2, :], g.PS[:, c % 2, :], ACT.Ln, bias=g.eps_l2))
                nc.scalar.activation(rs[:, c % 2, :], rs[:, c % 2, :], ACT.Exp, scale=-0.5).then_inc(s_rs, 1)

        @block.tensor
        def _(pe):
            for t in range(NT):
                ins = nc.tensor.transpose(g.PS[:, 7, t * 16:(t + 1) * 16], g.BA[:, t * P:(t + 1) * P], g.ident[0:16, 0:16])
            ins.then_inc(s_bt, 1)
            pe.wait_ge(s_g, 1)
            nc.tensor.matmul(g.PS[:, 7, 64:96], g.UT[:, :], gg[:, :], start=True, stop=True).then_inc(s_gc, 1)
            nc.tensor.matmul(g.PS[:, 7, 96:128], g.ones[:, :], gg[:, :], start=True, stop=True).then_inc(s_gc, 1)
            pe.wait_ge(s_gs, 1)
            nc.tensor.transpose(g.PS[0:NTH, 6, 0:P], g.GC[:, :], g.ident[:, :]).then_inc(s_gt, 1)

            def rows(n):
                pe.wait_ge(s_si, 12) if n < NT else pe.wait_ge(s_qk, 8)
                if n >= 4:
                    pe.wait_ge(s_cp, n - 3)
                c0 = CG + (8 if n < NT else 4)
                t = n % NT
                for j in range(4):
                    ins = nc.tensor.transpose(g.PS[:, 2 + n % 4, j * P:(j + 1) * P], g.PT[:, c0 + j, t * P:(t + 1) * P], g.ident[:, :])
                ins.then_inc(s_tp, 1)

            for c in range(8):
                pe.wait_ge(s_sq, c + 1)
                if c >= 2:
                    pe.wait_ge(s_rs, c - 1)
                nc.tensor.matmul(g.PS[:, c % 2, :], g.bones[:, :], sq[:, c % 2, :], start=True, stop=True).then_inc(s_ss, 1)
            for n in range(2 * NT):
                rows(n)


def phase_gdn(nc, g, y):
    names = ("kkqk_done", "diff_ready", "decay_ready", "mt_ready", "qk_ready", "qk_masked", "ms_ready", "ms0_ready", "ms0_transposed", "ms0_used",
             "x_ready", "y_done", "y_copied", "xy_done", "kx_ready", "w_done", "w_copied", "vn_done", "vn_ready",
             "os_done", "ov_done", "sd_done", "s_ready", "o_ready", "osq_ready", "orms_ready", "on_ready", "ot_done", "ot_copied", "link", "alink", "stored", "r_done")
    s = {n: g.sem("gdn_" + n) for n in names}
    LV = 6
    slot = lambda h: (h % 2) * 4 + h // 2
    head_of = lambda sl: 2 * (sl % 4) + sl // 4
    with ExitStack() as ctx:
        sb = lambda n, sh: ctx.enter_context(nc.sbuf_tensor("gdn_" + n, sh, F32))
        E, MT, QK, X, XT, Y = (sb(n, [P, H, P]) for n in ("E", "MT", "QK", "X", "XT", "Y"))
        MS = [sb(f"MS{i}", [P, H, P]) for i in range(2)]
        KE, KTL, VN, O = (sb(n, [P, SBW]) for n in ("KE", "KTL", "VN", "O"))
        NW = sb("NW", [P, 4, P])
        OSQ, ORS, SD = sb("OSQ", [P, SBW]), sb("ORS", [P, H]), sb("SD", [P, 4, HD])
        two = lambda b: g.PS[:, b:b + 2, :].rearrange("p b (h i) -> p (b h) i", i=P)
        heads = lambda v: v.rearrange("p (h e) -> p h e", h=H)
        bc = lambda v, w: v.unsqueeze(2).to_broadcast([v.shape[0], v.shape[1], w])
        mask_bc = lambda m, n=H: m.unsqueeze(1).to_broadcast([P, n, P])
        quarter = lambda b: g.PS[:, b, 0:4 * HD].rearrange("p (c e) -> p c e", e=HD)
        OS, VP = (lambda o: quarter(4 if o else 7)), (lambda o: quarter(5 if o else 6))
        block = ctx.enter_context(nc.Block())

        @block.tensor
        def _(pe):
            for t in range(NT):
                cols = slice(t * P, (t + 1) * P)
                L = t * (2 * LV + 2)
                if t:
                    pe.wait_ge(s["x_ready"], L)
                    pe.wait_ge(s["s_ready"], 2 * t)
                    pe.wait_ge(s["ot_copied"], t)
                for h in range(H):
                    c, r = h // 2, HD * (h % 2)
                    k = g.PT[r:r + HD, CG + 4 + c, cols]
                    nc.tensor.matmul(two(0)[:, slot(h), :], k, k, start=True, stop=True)
                    nc.tensor.matmul(two(2)[:, slot(h), :], k, g.PT[r:r + HD, CG + c, cols], start=True, stop=True)
                    row = t * H + h
                    ins = nc.tensor.matmul(two(4)[:, slot(h), :], g.ident[0:NT * H, row:row + 1].to_broadcast([NT * H, P]),
                                           g.GCT[:, :], start=True, stop=True)
                ins.then_inc(s["kkqk_done"], 1)
                pe.wait_ge(s["ms0_ready"], t + 1)
                for h in range(H):
                    ins = nc.tensor.transpose(two(0)[:, h, :], MS[1][:, h, :], g.ident[:, :])
                ins.then_inc(s["ms0_transposed"], 1)
                with pe.Fori(0, LV // 2) as i:
                    for p in range(2):
                        pe.wait_ge(s["ms_ready"], i * 2 + (t * LV + p + 1))
                        for a in range(2):
                            pe.wait_ge(s["x_ready"], i * 4 + (L + 2 * p + a + 1))
                            for h in range(4 * a, 4 * a + 4):
                                ins = nc.tensor.matmul(two(0)[:, h, :], MS[p][:, h, :], X[:, h, :], start=True, stop=True)
                            ins.then_inc(s["y_done"], 1)
                        for a in range(2):
                            pe.wait_ge(s["y_copied"], i * 4 + (2 * LV * t + 2 * p + a + 4))
                            for h in range(4 * a, 4 * a + 4):
                                nc.tensor.matmul(two(2)[:, h, :], XT[:, h, :], Y[:, h, :], start=True, stop=True)
                            for h in range(4 * a, 4 * a + 4):
                                ins = nc.tensor.matmul(two(4)[:, h, :], Y[:, h, :], XT[:, h, :], start=True, stop=True)
                            ins.then_inc(s["xy_done"], 1)
                pe.wait_ge(s["kx_ready"], 2 * t + 1)
                for a in range(2):
                    pe.wait_ge(s["x_ready"], L + 2 * LV + a + 1)
                    for h in range(4 * a, 4 * a + 4):
                        c = h % 4
                        ins = nc.tensor.matmul(two(0)[:, h, :], KE[:, c * P:(c + 1) * P], XT[:, h, :], start=True, stop=True)
                ins.then_inc(s["w_done"], 1)
                if t:
                    pe.wait_ge(s["s_ready"], 2 * t)
                pe.wait_ge(s["qk_masked"], t + 1)
                for h in range(H):
                    c, r = h // 2, HD * (h % 2)
                    ins = nc.tensor.matmul(OS(h % 2)[:, c, :], g.PT[r:r + HD, CG + c, cols], g.S[r:r + HD, c, :],
                                           start=True, stop=True)
                ins.then_inc(s["os_done"], 1)
                pe.wait_ge(s["w_copied"], 2 * t + 2)
                for h in range(H):
                    c, r = h // 2, HD * (h % 2)
                    nc.tensor.matmul(VP(h % 2)[:, c, :], XT[:, slot(h), :], g.VTM[:, t, h * HD:(h + 1) * HD], start=True, stop=False)
                    ins = nc.tensor.matmul(VP(h % 2)[:, c, :], NW[r:r + HD, c, :], g.S[r:r + HD, c, :],
                                           start=False, stop=True)
                ins.then_inc(s["vn_done"], 1)
                pe.wait_ge(s["vn_ready"], 2 * t + 2)
                pe.wait_ge(s["kx_ready"], 2 * t + 2)
                for c in range(4):
                    ins = nc.tensor.matmul(g.PS[:, 3, c * P:(c + 1) * P], KTL[:, c * P:(c + 1) * P], VN[:, c * P:(c + 1) * P],
                                           start=True, stop=True)
                ins.then_inc(s["sd_done"], 1)
                for h in range(H):
                    ins = nc.tensor.matmul(g.PS[:, 2, h * HD:(h + 1) * HD], QK[:, slot(h), :], VN[:, h * HD:(h + 1) * HD], start=True, stop=True)
                ins.then_inc(s["ov_done"], 1)
                pe.wait_ge(s["on_ready"], t + 1)
                for c in range(4):
                    ins = nc.tensor.transpose(g.PS[:, 0, c * P:(c + 1) * P], O[:, c * P:(c + 1) * P], g.ident[:, :])
                ins.then_inc(s["ot_done"], 1)

        @block.vector
        def _(dve):
            link = Link(dve, s["link"])
            for t in range(NT):
                st = slice(t * H, (t + 1) * H)
                L = t * (2 * LV + 2)
                dve.wait_ge(s["kkqk_done"], t + 1)
                for sl in range(H):
                    h = head_of(sl)
                    ins = nc.vector.tensor_scalar(E[:, sl, :], two(4)[:, sl, :], g.GC[:, t * H + h:t * H + h + 1], 0.0,
                                                  ALU.subtract, ALU.min)
                ins.then_inc(s["diff_ready"], 1)
                dve.wait_ge(s["decay_ready"], t + 1)
                for sl in range(H):
                    h = head_of(sl)
                    ins = nc.vector.scalar_tensor_tensor(out=MT[:, sl, :], in0=two(0)[:, sl, :], scalar=g.BETA[:, t * H + h:t * H + h + 1],
                                                         in1=E[:, sl, :], op0=ALU.mult, op1=ALU.mult)
                ins.then_inc(s["mt_ready"], 1)
                dve.wait_ge(s["mt_ready"], t + 1)
                nc.vector.tensor_tensor(MS[1][:, :, :], MT[:, :, :], mask_bc(g.LM[:, 0, :]), ALU.mult).then_inc(s["ms0_ready"], 1)
                nc.vector.tensor_tensor(QK[:, :, :], two(2), E[:, :, :], ALU.mult).then_inc(s["qk_ready"], 1)
                dve.wait_ge(s["ms0_ready"], t + 1)
                nc.vector.tensor_tensor(XT[:, :, :], mask_bc(g.ident[:, :]), MS[1][:, :, :], ALU.subtract).then_inc(s["ms0_used"], 1)
                dve.wait_ge(s["ms0_transposed"], t + 1)
                for a in range(2):
                    q = slice(4 * a, 4 * a + 4)
                    nc.vector.tensor_tensor(X[:, q, :], mask_bc(g.ident[:, :], 4), two(0)[:, q, :], ALU.subtract).then_inc(s["x_ready"], 1)
                with dve.Fori(0, LV // 2) as i:
                    for p in range(2):
                        for a in range(2):
                            q = slice(4 * a, 4 * a + 4)
                            dve.wait_ge(s["xy_done"], i * 4 + (2 * LV * t + 2 * p + a + 1))
                            nc.vector.tensor_tensor(XT[:, q, :], XT[:, q, :], two(4)[:, q, :], ALU.subtract)
                            nc.vector.tensor_tensor(X[:, q, :], X[:, q, :], two(2)[:, q, :], ALU.subtract).then_inc(s["x_ready"], 1)
                dve.wait_ge(s["w_done"], t + 1)
                for half in range(2):
                    q = slice(half * HD, (half + 1) * HD)
                    nc.vector.tensor_scalar(NW[q, :, :], two(0)[q, 4 * half:4 * half + 4, :], -1.0, None, ALU.mult).then_inc(s["w_copied"], 1)
                dve.wait_ge(s["vn_done"], t + 1)
                for o in range(2):
                    nc.vector.tensor_tensor(heads(VN[:, :])[:, o::2, :], VP(o), bc(g.BETA[:, st][:, o::2], HD), ALU.mult).then_inc(s["vn_ready"], 1)
                dve.wait_ge(s["os_done"], t + 1)
                link(nc.vector.tensor_tensor(SD[:, :, :], g.S[:, :, :], bc(g.EGL[:, t, :], HD), ALU.mult))
                dve.wait_ge(s["sd_done"], t + 1)
                for half in range(2):
                    q = slice(half * HD, (half + 1) * HD)
                    nc.vector.tensor_tensor(g.S[q, :, :], SD[q, :, :],
                                            g.PS[q, 3, :].rearrange("p (c e) -> p c e", e=P)[:, :, half * HD:(half + 1) * HD],
                                            ALU.add).then_inc(s["s_ready"], 1)
                if t:
                    dve.wait_ge(s["ot_done"], t)
                for o in range(2):
                    link(nc.vector.tensor_tensor(heads(O[:, :])[:, o::2, :], OS(o), bc(g.EGC[:, st][:, o::2], HD), ALU.mult))
                dve.wait_ge(s["ov_done"], t + 1)
                nc.vector.tensor_tensor(O[:, :], O[:, :], g.PS[:, 2, :], ALU.add).then_inc(s["o_ready"], 1)
                dve.wait_ge(s["osq_ready"], t + 1)
                nc.vector.tensor_reduce(ORS[:, :], heads(OSQ[:, :]), AX.X, ALU.add).then_inc(s["o_ready"], 1)
                dve.wait_ge(s["orms_ready"], t + 1)
                nc.vector.tensor_tensor(heads(O[:, :]), heads(O[:, :]), bc(ORS[:, :], HD), ALU.mult).then_inc(s["on_ready"], 1)
                dve.wait_ge(s["ot_done"], t + 1)
                nc.vector.scalar_tensor_tensor(out=g.OT[:, 4:8, t * P:(t + 1) * P], in0=g.PS[:, 0, :].rearrange("p (c i) -> p c i", c=4),
                                               scalar=g.nw_col[:, 0:1], in1=g.PT[:, CZ:CZ + 4, t * P:(t + 1) * P],
                                               op0=ALU.mult, op1=ALU.mult).then_inc(s["ot_copied"], 1)

        @block.scalar
        def _(act):
            link = Link(act, s["alink"])
            act.sem_inc(s["y_copied"], 3)
            for t in range(NT):
                act.wait_ge(s["diff_ready"], t + 1)
                nc.scalar.activation(E[:, :, :], E[:, :, :], ACT.Exp).then_inc(s["decay_ready"], 1)
                with act.Fori(0, LV // 2) as i:
                    for n in range(4):
                        act.wait_ge(s["y_done"], i * 4 + (2 * LV * t + n + 1))
                        q = slice(4 * (n % 2), 4 * (n % 2) + 4)
                        nc.scalar.activation(Y[:, q, :], two(0)[:, q, :], ACT.Copy).then_inc(s["y_copied"], 1)
                act.wait_ge(s["o_ready"], 2 * t + 1)
                nc.scalar.activation(OSQ[:, :], O[:, :], ACT.Square).then_inc(s["osq_ready"], 1)
                act.wait_ge(s["o_ready"], 2 * t + 2)
                link(nc.scalar.activation(ORS[:, :], ORS[:, :], ACT.Ln, bias=g.eps_l2, scale=1.0 / HD))
                nc.scalar.activation(ORS[:, :], ORS[:, :], ACT.Exp, scale=-0.5).then_inc(s["orms_ready"], 1)

        @block.gpsimd
        def _(pool):
            for t in range(NT):
                st = slice(t * H, (t + 1) * H)
                if t:
                    pool.wait_ge(s["w_done"], t)
                    pool.wait_ge(s["sd_done"], t)
                pool.tensor_tensor(heads(KE[:, :]), heads(g.KTM[:, t, :]), bc(g.EGC[:, st], HD), ALU.mult).then_inc(s["kx_ready"], 1)
                pool.tensor_tensor(heads(KTL[:, :]), heads(g.KTM[:, t, :]), bc(g.TAIL[:, st], HD), ALU.mult).then_inc(s["kx_ready"], 1)
                pool.wait_ge(s["mt_ready"], t + 1)
                with pool.Fori(0, LV // 2) as i:
                    for p in range(2):
                        if p:
                            pool.wait_ge(s["ms0_transposed"], t + 1)
                            pool.wait_ge(s["ms0_used"], t + 1)
                        pool.wait_ge(s["y_copied"], i * 4 + (2 * LV * t + 2 * p + 1))
                        pool.tensor_tensor(MS[p][:, :, :], MT[:, :, :],
                                           g.LM[:, bass.ds(i * 2 + p + 1, 1), :].to_broadcast([P, H, P]), ALU.mult).then_inc(s["ms_ready"], 1)
                pool.wait_ge(s["qk_ready"], t + 1)
                if t:
                    pool.wait_ge(s["ov_done"], t)
                pool.tensor_tensor(QK[:, :, :], QK[:, :, :], mask_bc(g.UT[:, :]), ALU.mult).then_inc(s["qk_masked"], 1)

        @block.sync
        def _(sp):
            sp.wait_ge(s["s_ready"], 2 * NT)
            for half in range(2):
                sp.dma_start(y["state_prompt"][0, half::2, :, :].rearrange("c d e -> d c e"),
                             g.S[half * HD:(half + 1) * HD, :, :]).then_inc(s["stored"], 16)
            sp.wait_ge(s["stored"], 32)


def phase_sample(nc, g, x, y):
    SC = P ** -0.5
    names = ("table_loaded", "state_loaded", "conv_loaded", "qb_done", "mqb_done", "sb_scores", "mem_scores", "sb_w_in", "sb_lg",
             "sb_sp", "sb_cum", "sb_w", "sb_a", "sb_av", "mem_t", "mem_max", "mem_exp", "mem_p", "mem_pt", "mem_ptc", "mem_o",
             "conv_t", "conv_sum", "conv_r", "conv_silu", "n_sq", "n_ss", "n_rs", "qkv_ready", "b_sig", "d_in", "d_lg", "d_ea",
             "d_g", "d_eg", "gates_ready", "z_silu", "sc_out", "sc_in", "s_new", "o_ready", "o_sq", "o_ss", "o_rs", "on_ready", "o_t",
             "nw_loaded", "stored", "link", "alink", "prod", "v_used")
    s = {n: g.sem("smp_" + n) for n in names}
    s_kv = [g.sem(f"smp_kv{i}_loaded") for i in range(4)]
    BH = NB * H
    with ExitStack() as ctx:
        sb = lambda n, sh, d=F32: ctx.enter_context(nc.sbuf_tensor("smp_" + n, sh, d))
        scr = nc.dram_tensor("scratch_rows", [4, NB, H, HD], F32)
        scr2 = nc.dram_tensor("scratch_gates", [2, NB, H], F32)
        KV = [g.PT[:, c:c + PG, 0:SBW] for c in (0, 4, 8, 24)]
        tab = sb("table", [1, NB * PG], I32)
        prod = sb("prod", [P, PG * SBW])
        zd, sd = sb("zd", [P, PG, NB, H]), sb("sd", [P, 2, NB, MH])
        t1, spd, ad = sb("t1", [P, PG * NB * H]), sb("spd", [P, PG * NB * H]), sb("ad", [P, PG, NB, H])
        pm, pmt = sb("pm", [NB * MH, NM]), sb("pmt", [P, 2, NB * MH])
        st1, st2 = sb("st1", [NB * MH, 1]), sb("st2", [NB * MH, 1])
        crow = sb("crow", [3 * NB, 1536])
        cf, ct = sb("cf", [P, 12, NB]), sb("ct", [P, 12, NB])
        xc, sqr, nrm = sb("xc", [NB, 4 * SBW]), sb("sqr", [NB, 2 * SBW]), sb("nrm", [NB, 2 * H])
        da, dt, gates = sb("da", [NB, H]), sb("dt", [NB, H]), sb("gates", [NB, 2, H])
        S0 = sb("S0", [BH, HD, HD])
        rows, gt = sb("rows", [BH, 4, HD]), sb("gt", [BH, 2])
        ks, vn, o2, osq, ors = (sb(n, [BH, w]) for n, w in (("ks", HD), ("vn", HD), ("o2", 2 * HD), ("osq", HD), ("ors", 1)))
        nw = sb("nw", [BH, HD])
        pr = prod[0:BH, 0:HD * HD // 2]
        flat = lambda v: v.rearrange("p a b c -> p (a b c)")
        block = ctx.enter_context(nc.Block())

        @block.sync
        def _(sp):
            sp.dma_start(tab[:, :], x["page_table"].rearrange("(o b) n -> o (b n)", o=1)).then_inc(s["table_loaded"], 16)
            sp.dma_start(crow[:, :], x["state_gdn_conv"].rearrange("b k n -> (b k) n")).then_inc(s["conv_loaded"], 16)
            sp.dma_start(S0[:, :, :], x["state_gdn"].rearrange("b h d e -> (b h) d e")).then_inc(s["state_loaded"], 16)
            sp.dma_start(nw[:, :], x["gdn_norm_w"].partition_broadcast(BH)).then_inc(s["nw_loaded"], 16)
            sp.wait_ge(s["table_loaded"], 16)
            for kind, cache in ((0, x["cache_sb_k"]), (1, x["cache_sb_v"])):
                for b in range(NB):
                    n = kind * NB + b
                    if n >= 4:
                        sp.wait_ge(s["prod"], n - 3) if n - 4 < NB else sp.wait_ge(s["v_used"], n - 4 - NB + 1)
                    for p in range(PG):
                        page = sp.value_load(tab[0:1, b * PG + p:b * PG + p + 1], min_val=0, max_val=N_POOL - 1)
                        sp.dma_start(KV[n % 4][:, p, :], cache[bass.ds(page, 1)].rearrange("a t h d -> t (a h d)")).then_inc(s_kv[n % 4], 16)
            for kind, cache in ((2, x["cache_mem_k"]), (3, x["cache_mem_v"])):
                for b in range(NB):
                    n = kind * NB + b
                    m = n - 4
                    sp.wait_ge(s["v_used"], m - NB + 1) if m < 2 * NB else (sp.wait_ge(s["prod"], m - NB + 1) if m < 3 * NB else sp.wait_ge(s["v_used"], m - 2 * NB + 1))
                    sp.dma_start(KV[n % 4][:, 0:2, :], cache[b].rearrange("(m p) h d -> p m (h d)", p=P)).then_inc(s_kv[n % 4], 16)
            sp.wait_ge(s["s_new"], 2)
            sp.dma_start(y["state_sample"].rearrange("b h d e -> (b h) d e"), S0[:, :, :]).then_inc(s["stored"], 16)
            sp.wait_ge(s["stored"], 16)

        def kv_total(n):
            total = 0
            for m in range(n % 4, n + 1, 4):
                total += 16 * (PG if m < 2 * NB else 1)
            return total

        @block.gpsimd
        def _(pool):
            pool.wait_ge(s["qkv_ready"], 3)
            pool.wait_ge(s["z_silu"], 1)
            pool.dma_start(scr[:, :, :, :].rearrange("j b h e -> b j (h e)"), xc[:, :].rearrange("b (j n) -> b j n", j=4)).then_inc(s["sc_out"], 16)
            pool.wait_ge(s["gates_ready"], 2)
            pool.dma_start(scr2[:, :, :].rearrange("j b h -> b j h"), gates[:, :, :]).then_inc(s["sc_out"], 16)
            pool.wait_ge(s["sc_out"], 32)
            for j in range(4):
                pool.dma_start(rows[:, j, :], scr[j].rearrange("b h e -> (b h) e")).then_inc(s["sc_in"], 16)
            with nc.allow_non_contiguous_dma(reason="64 gates"):
                for j in range(2):
                    pool.dma_start(gt[:, j:j + 1], scr2[j].rearrange("b (h o) -> (b h) o", o=1)).then_inc(s["sc_in"], 16)

        @block.tensor
        def _(pe):
            pe.wait_ge(s["conv_loaded"], 16)
            for c in range(12):
                ins = nc.tensor.transpose(g.PS[:, 5, c * 24:(c + 1) * 24], crow[:, c * P:(c + 1) * P], g.ident[0:24, 0:24])
            ins.then_inc(s["conv_t"], 1)
            for b in range(NB):
                if b >= 2:
                    pe.wait_ge(s["prod"], b - 1)
                nc.tensor.matmul(g.PS[:, b % 2, :], g.ident[0:NB, b:b + 1].to_broadcast([NB, P]), g.XS[:, 0:SBW],
                                 start=True, stop=True).then_inc(s["qb_done"], 1)
                if b == 0:
                    pe.wait_ge(s["conv_sum"], 1)
                    for c in range(12):
                        ins = nc.tensor.transpose(g.PS[0:NB, 2 + c // 4, (c % 4) * P:(c % 4 + 1) * P], cf[:, c, :], g.ident[:, :])
                    ins.then_inc(s["conv_r"], 1)
            pe.wait_ge(s["sb_sp"], 1)
            for p in range(PG):
                for m in range(p, PG):
                    ins = nc.tensor.matmul(g.PS[:, 5, p * 64:(p + 1) * 64], (g.TRI if m == p else g.nones)[:, :],
                                           spd[:, m * 64:(m + 1) * 64], start=m == p, stop=m == PG - 1)
            ins.then_inc(s["sb_cum"], 1)
            pe.wait_ge(s["sb_a"], 1)
            for b in range(NB):
                n = NB + b
                pe.wait_ge(s_kv[n % 4], kv_total(n))
                for c in range(4):
                    for p in range(PG):
                        col = (b * 4 + c) * 2
                        ins = nc.tensor.matmul(g.PS[:, 6, col:col + 2], KV[n % 4][:, p, c * P:(c + 1) * P], ad[:, p, b, 2 * c:2 * c + 2],
                                               start=p == 0, stop=p == PG - 1)
                ins.then_inc(s["v_used"], 1)
            for b in range(NB):
                if b >= 2:
                    pe.wait_ge(s["prod"], NB + b - 1)
                else:
                    pe.wait_ge(s["prod"], NB)
                nc.tensor.matmul(g.PS[:, b % 2, :], g.ident[0:NB, b:b + 1].to_broadcast([NB, P]), g.XS[:, MQ0:MQ0 + SBW],
                                 start=True, stop=True).then_inc(s["mqb_done"], 1)
            pe.wait_ge(s["mem_scores"], 1)
            for m in range(2):
                ins = nc.tensor.transpose(g.PS[0:NB * MH, 7, m * P:(m + 1) * P], sd[:, m, :, :].rearrange("p b h -> p (b h)"), g.ident[:, :])
            ins.then_inc(s["mem_t"], 1)
            pe.wait_ge(s["mem_p"], 1)
            for m in range(2):
                ins = nc.tensor.transpose(g.PS[:, 5, m * 32:(m + 1) * 32], pm[:, m * P:(m + 1) * P], g.ident[0:32, 0:32])
            ins.then_inc(s["mem_pt"], 1)
            pe.wait_ge(s["mem_ptc"], 1)
            for b in range(NB):
                n = 3 * NB + b
                pe.wait_ge(s_kv[n % 4], kv_total(n))
                for h in range(MH):
                    for m in range(2):
                        ins = nc.tensor.matmul(g.PS[:, 7, 256 + h * NB + b:256 + h * NB + b + 1], KV[n % 4][:, m, h * P:(h + 1) * P],
                                               pmt[:, m, b * MH + h:b * MH + h + 1], start=m == 0, stop=m == 1)
                ins.then_inc(s["v_used"], 1)
            pe.wait_ge(s["on_ready"], 2)
            nc.tensor.transpose(g.PS[:, 4, 0:BH], o2[:, :], g.ident[0:BH, 0:BH]).then_inc(s["o_t"], 1)

        @block.vector
        def _(dve):
            link = Link(dve, s["link"])
            dve.wait_ge(s["conv_t"], 1)
            old = g.PS[:, 5, 0:288].rearrange("p (c b k) -> p c b k", c=12, k=3)
            tap = lambda k: g.CW[:, :, k:k + 1].to_broadcast([P, 12, NB])
            link(nc.vector.tensor_tensor(cf[:, :, :], g.PT[:, CG:CG + 12, SEQ:T], tap(3), ALU.mult))
            for k in range(3):
                link(nc.vector.tensor_tensor(ct[:, :, :], old[:, :, :, k], tap(k), ALU.mult))
                ins = nc.vector.tensor_tensor(cf[:, :, :], cf[:, :, :], ct[:, :, :], ALU.add)
                if k < 2:
                    link(ins)
            ins.then_inc(s["conv_sum"], 1)
            link(nc.vector.tensor_tensor(da[:, :], g.XS[:, BA0 + H:BA0 + 2 * H], g.dt_bc[0:NB, :], ALU.add))
            nc.vector.scalar_tensor_tensor(out=dt[:, :], in0=da[:, :], scalar=-1.0, in1=da[:, :], op0=ALU.mult, op1=ALU.min).then_inc(s["d_in"], 1)
            dve.wait_ge(s["d_lg"], 2)
            link(nc.vector.scalar_tensor_tensor(out=dt[:, :], in0=da[:, :], scalar=0.0, in1=dt[:, :], op0=ALU.max, op1=ALU.add))
            nc.vector.scalar_tensor_tensor(out=dt[:, :], in0=dt[:, :], scalar=-1.0, in1=nrm[:, 0:H], op0=ALU.mult, op1=ALU.mult).then_inc(s["d_g"], 1)

            for b in range(NB):
                dve.wait_ge(s_kv[b % 4], kv_total(b))
                dve.wait_ge(s["qb_done"], b + 1)
                pv = prod[:, :].rearrange("p (g n) -> p g n", g=PG)
                nc.vector.tensor_tensor(pv, KV[b % 4], g.PS[:, b % 2, :].unsqueeze(1).to_broadcast([P, PG, SBW]), ALU.mult).then_inc(s["prod"], 1)
                dve.wait_ge(s["prod"], b + 1)
                link(nc.vector.tensor_reduce(zd[:, :, b, :], pv.rearrange("p g (h d) -> p g h d", d=HD), AX.X, ALU.add))
                if b == 1:
                    dve.wait_ge(s["n_sq"], 1)
                    nc.vector.tensor_reduce(nrm[:, :], sqr[:, :].rearrange("p (h d) -> p h d", d=HD), AX.X, ALU.add).then_inc(s["n_ss"], 1)
                if b == 2:
                    dve.wait_ge(s["n_rs"], 1)
                    v = xc[:, 0:2 * SBW].rearrange("p (h d) -> p h d", d=HD)
                    link(nc.vector.tensor_tensor(v, v, nrm[:, :].unsqueeze(2).to_broadcast([NB, 2 * H, HD]), ALU.mult))
                    nc.vector.tensor_scalar(xc[:, 0:SBW], xc[:, 0:SBW], HD ** -0.5, None, ALU.mult).then_inc(s["qkv_ready"], 3)
            link(nc.vector.scalar_tensor_tensor(out=zd[:, :, :, :].rearrange("p g b h -> p (g b) h"),
                                                in0=zd[:, :, :, :].rearrange("p g b h -> p (g b) h"), scalar=HD ** -0.5,
                                                in1=g.sbb_bc[:, :].unsqueeze(1).to_broadcast([P, PG * NB, H]), op0=ALU.mult, op1=ALU.add))
            nc.vector.scalar_tensor_tensor(out=t1[:, :], in0=flat(zd[:, :, :, :]), scalar=-1.0, in1=flat(zd[:, :, :, :]),
                                           op0=ALU.mult, op1=ALU.min).then_inc(s["sb_w_in"], 1)
            dve.wait_ge(s["sb_lg"], 1)
            nc.vector.scalar_tensor_tensor(out=spd[:, :], in0=flat(zd[:, :, :, :]), scalar=0.0, in1=t1[:, :],
                                           op0=ALU.max, op1=ALU.add).then_inc(s["sb_sp"], 1)

            def delta(part):
                kb = lambda q: rows[:, 1, q].unsqueeze(2).to_broadcast([BH, HD // 2, HD])
                qb = lambda q: rows[:, 0, q].unsqueeze(2).to_broadcast([BH, HD // 2, HD])
                prv = pr.rearrange("p (d e) -> p d e", e=HD)
                halves = [slice(0, HD // 2), slice(HD // 2, HD)]
                if part == 0:
                    dve.wait_ge(s["state_loaded"], 16)
                    dve.wait_ge(s["sc_in"], 16 * 6)
                    for i, q in enumerate(halves):
                        link(nc.vector.tensor_tensor(prv, S0[:, q, :], kb(q), ALU.mult))
                        link(nc.vector.tensor_reduce(ks[:, :] if i == 0 else vn[:, :], prv.rearrange("p d e -> p e d"), AX.X, ALU.add))
                    link(nc.vector.tensor_tensor(ks[:, :], ks[:, :], vn[:, :], ALU.add))
                    link(nc.vector.tensor_scalar(ks[:, :], ks[:, :], gt[:, 1:2], None, ALU.mult))
                    link(nc.vector.tensor_tensor(ks[:, :], rows[:, 2, :], ks[:, :], ALU.subtract))
                    link(nc.vector.tensor_scalar(vn[:, :], ks[:, :], gt[:, 0:1], None, ALU.mult))
                    for i, q in enumerate(halves):
                        link(nc.vector.tensor_tensor(prv, vn[:, :].unsqueeze(1).to_broadcast([BH, HD // 2, HD]), kb(q), ALU.mult))
                        nc.vector.scalar_tensor_tensor(out=S0[:, q, :], in0=S0[:, q, :], scalar=gt[:, 1:2], in1=prv,
                                                       op0=ALU.mult, op1=ALU.add).then_inc(s["s_new"], 1)
                        dve.wait_ge(s["s_new"], i + 1)
                else:
                    for i, q in enumerate(halves):
                        link(nc.vector.tensor_tensor(prv, S0[:, q, :], qb(q), ALU.mult))
                        link(nc.vector.tensor_reduce(ks[:, :] if i == 0 else vn[:, :], prv.rearrange("p d e -> p e d"), AX.X, ALU.add))
                    nc.vector.tensor_tensor(o2[:, 0:HD], ks[:, :], vn[:, :], ALU.add).then_inc(s["o_ready"], 1)
                    dve.wait_ge(s["o_sq"], 1)
                    nc.vector.tensor_reduce(ors[:, :], osq[:, :], AX.X, ALU.add).then_inc(s["o_ss"], 1)
                    dve.wait_ge(s["o_rs"], 1)
                    dve.wait_ge(s["nw_loaded"], 16)
                    link(nc.vector.tensor_scalar(o2[:, 0:HD], o2[:, 0:HD], ors[:, 0:1], None, ALU.mult))
                    link(nc.vector.tensor_tensor(o2[:, 0:HD], o2[:, 0:HD], nw[:, :], ALU.mult))
                    nc.vector.tensor_tensor(o2[:, 0:HD], o2[:, 0:HD], rows[:, 3, :], ALU.mult).then_inc(s["on_ready"], 1)
                    dve.wait_ge(s["on_ready"], 1)
                    nc.vector.tensor_copy(o2[:, HD:2 * HD], o2[:, 0:HD]).then_inc(s["on_ready"], 1)

            dve.wait_ge(s["sb_cum"], 1)
            nc.vector.tensor_tensor(flat(ad[:, :, :, :]), g.PS[:, 5, 0:256], flat(zd[:, :, :, :]), ALU.add).then_inc(s["sb_w"], 1)
            delta(0)
            dve.wait_ge(s["v_used"], NB)
            o = g.PS[:, 6, 0:64].rearrange("p (b c e) -> p c b e", b=NB, c=4)
            for half in range(2):
                q = slice(half * HD, (half + 1) * HD)
                nc.vector.tensor_copy(g.OT[q, 0:4, SEQ:T], o[q, :, :, half])
            for b in range(NB):
                n = 2 * NB + b
                dve.wait_ge(s_kv[n % 4], kv_total(n))
                dve.wait_ge(s["mqb_done"], b + 1)
                pv = prod[:, 0:2 * SBW].rearrange("p (g n) -> p g n", g=2)
                nc.vector.tensor_tensor(pv, KV[n % 4][:, 0:2, :], g.PS[:, b % 2, :].unsqueeze(1).to_broadcast([P, 2, SBW]), ALU.mult).then_inc(s["prod"], 1)
                dve.wait_ge(s["prod"], NB + b + 1)
                ins = nc.vector.tensor_reduce(sd[:, :, b, :], pv.rearrange("p g (h d) -> p g h d", d=P), AX.X, ALU.add)
                if b < NB - 1:
                    link(ins)
            ins.then_inc(s["mem_scores"], 1)
            dve.wait_ge(s["mem_scores"], 1)
            delta(1)
            dve.wait_ge(s["mem_t"], 1)
            link(nc.vector.tensor_reduce(st1[:, :], g.PS[0:32, 7, 0:NM], AX.X, ALU.max))
            nc.vector.tensor_scalar(st1[:, :], st1[:, :], -SC, None, ALU.mult).then_inc(s["mem_max"], 1)
            dve.wait_ge(s["mem_exp"], 1)
            link(nc.vector.reciprocal(st2[:, :], st2[:, :]))
            nc.vector.tensor_scalar(pm[:, :], pm[:, :], st2[:, 0:1], None, ALU.mult).then_inc(s["mem_p"], 1)
            dve.wait_ge(s["mem_pt"], 1)
            nc.vector.tensor_copy(pmt[:, :, :], g.PS[:, 5, 0:64].rearrange("p (m j) -> p m j", m=2)).then_inc(s["mem_ptc"], 1)
            dve.wait_ge(s["v_used"], 2 * NB)
            nc.vector.tensor_copy(g.OT[:, 8:12, SEQ:T], g.PS[:, 7, 256:288].rearrange("p (h b) -> p h b", h=MH))
            dve.wait_ge(s["o_t"], 1)
            ot = g.PS[:, 4, 0:BH].rearrange("p (b h) -> p h b", b=NB)
            for half in range(2):
                q = slice(half * HD, (half + 1) * HD)
                nc.vector.tensor_copy(g.OT[q, 4:8, SEQ:T], ot[q, half::2, :])

        @block.scalar
        def _(act):
            link = Link(act, s["alink"])
            nc.scalar.activation(nrm[:, 0:H], g.A_bc[0:NB, :], ACT.Exp).then_inc(s["d_lg"], 1)
            act.wait_ge(s["d_in"], 1)
            link(nc.scalar.activation(dt[:, :], dt[:, :], ACT.Exp))
            nc.scalar.activation(dt[:, :], dt[:, :], ACT.Ln, bias=g.one_c[0:NB]).then_inc(s["d_lg"], 1)
            act.wait_ge(s["d_g"], 1)
            nc.scalar.activation(gates[:, 1, :], dt[:, :], ACT.Exp).then_inc(s["gates_ready"], 1)
            nc.scalar.activation(gates[:, 0, :], g.XS[:, BA0:BA0 + H], ACT.Sigmoid).then_inc(s["gates_ready"], 1)
            act.wait_ge(s["conv_r"], 1)
            link(nc.scalar.activation(xc[:, 0:3 * SBW], g.PS[0:NB, 2:5, :].rearrange("p b n -> p (b n)"), ACT.Silu))
            nc.scalar.activation(xc[:, 3 * SBW:4 * SBW], g.XS[:, 3072:3584], ACT.Silu).then_inc(s["z_silu"], 1)
            nc.scalar.activation(sqr[:, :], xc[:, 0:2 * SBW], ACT.Square).then_inc(s["n_sq"], 1)
            act.wait_ge(s["n_ss"], 1)
            link(nc.scalar.activation(nrm[:, :], nrm[:, :], ACT.Ln, bias=g.eps_l2[0:NB]))
            nc.scalar.activation(nrm[:, :], nrm[:, :], ACT.Exp, scale=-0.5).then_inc(s["n_rs"], 1)
            act.wait_ge(s["sb_w_in"], 1)
            link(nc.scalar.activation(t1[:, :], t1[:, :], ACT.Exp))
            nc.scalar.activation(t1[:, :], t1[:, :], ACT.Ln, bias=g.one_c).then_inc(s["sb_lg"], 1)
            act.wait_ge(s["sb_w"], 1)
            nc.scalar.activation(flat(ad[:, :, :, :]), flat(ad[:, :, :, :]), ACT.Exp).then_inc(s["sb_a"], 1)
            act.wait_ge(s["o_ready"], 1)
            nc.scalar.activation(osq[:, :], o2[:, 0:HD], ACT.Square).then_inc(s["o_sq"], 1)
            act.wait_ge(s["o_ss"], 1)
            link(nc.scalar.activation(ors[:, :], ors[:, :], ACT.Ln, bias=g.eps_l2[0:BH], scale=1.0 / HD))
            nc.scalar.activation(ors[:, :], ors[:, :], ACT.Exp, scale=-0.5).then_inc(s["o_rs"], 1)
            act.wait_ge(s["mem_max"], 1)
            nc.scalar.activation(pm[:, :], g.PS[0:32, 7, 0:NM], ACT.Exp, bias=st1[:, 0:1], scale=SC, accum_out=st2[:, 0:1]).then_inc(s["mem_exp"], 1)


def phase_merge(nc, g, x):
    s_w = [g.sem(f"br_w{i}_loaded") for i in range(3)]
    s_mm, s_m, s_l = g.sem("branch_done"), g.sem("branch_gated"), g.sem("branch_link")
    with ExitStack() as ctx:
        W = [ctx.enter_context(nc.sbuf_tensor(f"br_w{i}", [P, 4, D], F32)) for i in range(3)]
        tmp = ctx.enter_context(nc.sbuf_tensor("br_tmp", [P, 2, TH], F32))
        block = ctx.enter_context(nc.Block())

        @block.sync
        def _(sp):
            for i, w in enumerate((x["w_br_sb"], x["w_br_gdn"], x["w_br_mem"])):
                sp.dma_start(W[i][:, :, :], w.rearrange("(c p) n -> p c n", p=P)).then_inc(s_w[i], 16)

        @block.tensor
        def _(pe):
            for n in range(24):
                j, br = n // 3, n % 3
                if n < 3:
                    pe.wait_ge(s_w[br], 16)
                if n >= 3:
                    pe.wait_ge(s_m, n - 2)
                for h in range(2):
                    for c in range(4):
                        ins = nc.tensor.matmul(g.PS[:, 2 * (n % 3) + h, 0:TH], W[br][:, c, j * P:(j + 1) * P],
                                               g.OT[:, 4 * br + c, h * TH:(h + 1) * TH], start=c == 0, stop=c == 3)
                ins.then_inc(s_mm, 1)

        @block.vector
        def _(dve):
            link = Link(dve, s_l)
            for n in range(24):
                j, br = n // 3, n % 3
                half = lambda v: v.rearrange("p (h t) -> p h t", h=2)
                m = half(g.PT[:, 24 + j, :])
                dve.wait_ge(s_mm, n + 1)
                if br:
                    dve.wait_ge(s_m, n)
                nc.vector.tensor_tensor(tmp[:, :, :] if br else m, g.PS[:, 2 * (n % 3):2 * (n % 3) + 2, 0:TH],
                                        half(g.PT[:, 8 * br + j, :]), ALU.mult).then_inc(s_l if br else s_m, 1)
                if br:
                    link.n += 1
                    dve.wait_ge(s_l, link.n)
                    nc.vector.tensor_tensor(m, m, tmp[:, :, :], ALU.add).then_inc(s_m, 1)


def layer_norm_rows(nc, dve, link, src, dst, stats, agg, rstd, gain, shift, m, s_var, s_rstd, count):
    for h in range(2):
        ins = nc.vector.bn_stats(stats[0:m, h, :], src[:, h * 512:(h + 1) * 512])
    link(ins)
    nc.vector.bn_aggr(agg[0:m, :], stats[0:m, :, :]).then_inc(s_var, 1)
    dve.wait_ge(s_rstd, count)
    link(nc.vector.tensor_scalar(dst, src, agg[0:m, 0:1], rstd[0:m, 0:1], ALU.subtract, ALU.mult))
    link(nc.vector.tensor_tensor(dst, dst, gain[0:m, :], ALU.mult))
    return nc.vector.tensor_tensor(dst, dst, shift[0:m, :], ALU.add)


def phase_out(nc, g, x):
    s_w, s_mm, s_pre, s_var, s_rstd, s_h, s_tp, s_cp, s_st, s_l, s_al = (g.sem(n) for n in
        ("wo_loaded", "wo_done", "residual_ready", "ln1_var_ready", "ln1_rstd_ready", "h_ready", "h_transposed", "ht_copied",
         "h_stored", "out_link", "out_act_link"))
    s_in = [g.sem(f"out_in{i}_loaded") for i in range(4)]
    tiles = tok_tiles()
    with ExitStack() as ctx:
        sb = lambda n, sh: ctx.enter_context(nc.sbuf_tensor("out_" + n, sh, F32))
        W, xr = sb("wo", [P, KC, D]), sb("x", [P, 2, D])
        gain, shift, stats, agg, rstd = sb("gain", [P, D]), sb("shift", [P, D]), sb("stats", [P, 2, 6]), sb("agg", [P, 2]), sb("rstd", [P, 1])
        block = ctx.enter_context(nc.Block())

        @block.sync
        def _(sp):
            sp.dma_start(W[:, :, :], x["w_o"].rearrange("(c p) n -> p c n", p=P)).then_inc(s_w, 16)
            sp.dma_start(gain[:, :], x["ln1_g"].partition_broadcast(P)).then_inc(s_in[2], 16)
            sp.dma_start(shift[:, :], x["ln1_b"].partition_broadcast(P)).then_inc(s_in[3], 16)
            for t, (t0, m) in enumerate(tiles):
                if t >= 2:
                    sp.wait_ge(s_pre, t - 1)
                src = x["x_prompt"][0, t0:t0 + m, :] if t < NT else x["x_sample"].rearrange("b o d -> (b o) d")
                sp.dma_start(xr[0:m, t % 2, :], src).then_inc(s_in[t % 2], 16)
            for t, (t0, m) in enumerate(tiles):
                sp.wait_ge(s_h, t + 1)
                sp.dma_start(g.h_dram[t0:t0 + m, :], g.H[0:m, t, :]).then_inc(s_st, 16)
            sp.wait_ge(s_st, 16 * 5)

        @block.tensor
        def _(pe):
            pe.wait_ge(s_w, 16)

            def product(t):
                t0, m = tiles[t]
                if t >= 2:
                    pe.wait_ge(s_pre, t - 1)
                for h in range(2):
                    for k in range(KC):
                        ins = nc.tensor.matmul(g.PS[0:m, 2 * (t % 2) + h, :], g.PT[:, 24 + k, t0:t0 + m], W[:, k, h * 512:(h + 1) * 512],
                                               start=k == 0, stop=k == KC - 1)
                ins.then_inc(s_mm, 1)

            def transposes(t):
                t0, m = tiles[t]
                pe.wait_ge(s_h, t + 1)
                if t >= 2:
                    pe.wait_ge(s_cp, t - 1)
                for k in range(KC):
                    ins = nc.tensor.transpose(g.PS[:, 4 + 2 * (t % 2) + k // 4, (k % 4) * P:(k % 4) * P + m], g.H[0:m, t, k::KC],
                                              g.ident[0:m, 0:m])
                ins.then_inc(s_tp, 1)

            for t in range(5):
                product(t)
                if t >= 2:
                    transposes(t - 2)
            transposes(3)
            transposes(4)

        @block.scalar
        def _(act):
            link = Link(act, s_al)

            def copy_ht(t):
                t0, m = tiles[t]
                act.wait_ge(s_tp, t + 1)
                src = g.PS[:, 4 + 2 * (t % 2):6 + 2 * (t % 2), :].rearrange("p b (k m) -> p (b k) m", m=P)[:, :, 0:m]
                nc.scalar.activation(g.XT[:, :, t0:t0 + m], src, ACT.Copy).then_inc(s_cp, 1)

            for t, (t0, m) in enumerate(tiles):
                act.wait_ge(s_var, t + 1)
                link(nc.scalar.activation(rstd[0:m, :], agg[0:m, 1:2], ACT.Ln, bias=g.eps_ln[0:m]))
                nc.scalar.activation(rstd[0:m, :], rstd[0:m, :], ACT.Exp, scale=-0.5).then_inc(s_rstd, 1)
                if t >= 1:
                    copy_ht(t - 1)
            copy_ht(4)

        @block.vector
        def _(dve):
            link = Link(dve, s_l)
            dve.wait_ge(s_in[2], 16)
            dve.wait_ge(s_in[3], 16)
            for t, (t0, m) in enumerate(tiles):
                dve.wait_ge(s_mm, t + 1)
                dve.wait_ge(s_in[t % 2], 16 * (t // 2 + 1))
                h = g.H[0:m, t, :]
                nc.vector.scalar_tensor_tensor(out=h, in0=xr[0:m, t % 2, :], scalar=ALPHA,
                                               in1=g.PS[0:m, 2 * (t % 2):2 * (t % 2) + 2, :].rearrange("p b n -> p (b n)"),
                                               op0=ALU.mult, op1=ALU.add).then_inc(s_pre, 1)
                dve.wait_ge(s_pre, t + 1)
                layer_norm_rows(nc, dve, link, h, h, stats, agg, rstd, gain, shift, m, s_var, s_rstd, t + 1).then_inc(s_h, 1)


def phase_route(nc, g, x):
    names = ("w_loaded", "init", "tok0", "logits_done", "scores_ready", "chosen", "ranks_done", "dest_ready", "over_ready", "over_t", "table_cleared",
             "scattered", "table_in", "table_t", "slots_ready", "link", "gu_done", "sg_ready", "su_ready", "sh_ready",
             "ht_done", "ht_copied", "y_done", "y_copied", "sw_loaded")
    s = {n: g.sem("rt_" + n) for n in names}
    tiles = tok_tiles()
    with ExitStack() as ctx:
        sb = lambda n, sh, d=F32: ctx.enter_context(nc.sbuf_tensor("rt_" + n, sh, d))
        wr = sb("wr", [P, KC, NE])
        wgu, wd = sb("wgu", [P, 2, KC, DE]), sb("wd", [P, 2, D])
        SC, BI, M, DP, T1 = (sb(n, [P, 5, NE]) for n in ("SC", "BI", "M", "DP", "T1"))
        M8 = sb("M8", [P, 5, NG, 8])
        gs, cnt = sb("gs", [P, 5, NG]), sb("cnt", [P, 5, NG])
        A, B = sb("A", [P, 5, NG, NG]), sb("B", [P, 5, NG, NG])
        low, lowi = sb("low", [P, NG, NG]), sb("lowi", [P, NG, NG], I32)
        m8, den = sb("m8", [P, 5, 8]), sb("den", [P, 5])
        cn, ex, inc, ofs, ie, one64 = (sb(n, [P, NE]) for n in ("cn", "ex", "inc", "ofs", "ie", "one64"))
        oe, ip = sb("oe", [P, 2]), sb("ip", [P, 1])
        tok, dk = sb("tok", [P, 5, TOPK]), sb("dk", [P, 5, 8])
        toki = sb("toki", [P, 5, TOPK], I32)
        didx = sb("didx", [P, 5, TOPK], I32)
        free = sb("free", [NBLK, CAP])
        tabr = sb("tabr", [NBLK, CAP])
        sg, su, sh, sht = sb("sg", [P, DE]), sb("su", [P, DE]), sb("sh", [P, 2, DE]), sb("sht", [P, 2, P])
        block = ctx.enter_context(nc.Block())

        @block.sync
        def _(sp):
            sp.dma_start(wr[:, :, :], x["w_router"].rearrange("(p k) n -> p k n", k=KC)).then_inc(s["w_loaded"], 16)
            for j, w in enumerate((x["w_sh_gate"], x["w_sh_up"])):
                sp.dma_start(wgu[:, j, :, :], w.rearrange("(p k) f -> p k f", k=KC)).then_inc(s["sw_loaded"], 16)
            sp.dma_start(wd[:, :, :], x["w_sh_down"].rearrange("(p j) n -> p j n", j=2)).then_inc(s["sw_loaded"], 16)
            sp.wait_ge(s["init"], 3)
            sp.dma_start(g.slot_dram.rearrange("(b p) o -> b (p o)", p=CAP), free[:, :]).then_inc(s["table_cleared"], 16)
            sp.wait_ge(s["scattered"], 16 * 40)
            sp.dma_start(tabr[:, :], g.slot_dram.rearrange("(b p) o -> b (p o)", p=CAP)).then_inc(s["table_in"], 16)

        @block.tensor
        def _(pe):
            pe.wait_ge(s["w_loaded"], 16)
            for t, (t0, m) in enumerate(tiles):
                for k in range(KC):
                    ins = nc.tensor.matmul(g.PS[0:m, 0, t * NE:(t + 1) * NE], g.XT[:, k, t0:t0 + m], wr[:, k, :],
                                           start=k == 0, stop=k == KC - 1)
            ins.then_inc(s["logits_done"], 1)

            def gate_up(t):
                t0, m = tiles[t]
                if t >= 2:
                    pe.wait_ge(s["su_ready"], t - 1)
                for k in range(KC):
                    ins = nc.tensor.matmul(g.PS[0:m, 3 + t % 2, :], g.XT[:, k, t0:t0 + m], wgu[:, :, k, :], start=k == 0, stop=k == KC - 1)
                ins.then_inc(s["gu_done"], 1)

            def down(t):
                t0, m = tiles[t]
                pe.wait_ge(s["sh_ready"], t + 1)
                for j in range(2):
                    ins = nc.tensor.transpose(g.PS[:, 5, j * P:j * P + m], sh[0:m, t % 2, j::2], g.ident[0:m, 0:m])
                ins.then_inc(s["ht_done"], 1)
                pe.wait_ge(s["ht_copied"], t + 1)
                if t >= 1:
                    pe.wait_ge(s["y_copied"], t)
                for h in range(2):
                    for j in range(2):
                        ins = nc.tensor.matmul(g.PS[0:m, 6 + h, :], sht[:, j, 0:m], wd[:, j, h * 512:(h + 1) * 512], start=j == 0, stop=j == 1)
                ins.then_inc(s["y_done"], 1)

            pe.wait_ge(s["sw_loaded"], 48)
            gate_up(0)
            gate_up(1)
            down(0)
            pe.wait_ge(s["chosen"], 1)
            for t in range(5):
                kt = tiles[t][1]
                nc.tensor.matmul(g.PS[:, 1, t * NE:(t + 1) * NE], g.UTs[0:kt, :], M[0:kt, t, :], start=True, stop=t == 0)
                for j in range(t):
                    nc.tensor.matmul(g.PS[:, 1, t * NE:(t + 1) * NE], g.ones[:, :], M[:, j, :], start=False, stop=j == t - 1)
            for t in range(5):
                kt = tiles[t][1]
                ins = nc.tensor.matmul(g.PS[:, 2, 0:NE], g.ones[0:kt, :], M[0:kt, t, :], start=t == 0, stop=t == 4)
            ins.then_inc(s["ranks_done"], 1)
            gate_up(2)
            down(1)
            pe.wait_ge(s["over_ready"], 1)
            nc.tensor.transpose(g.PS[0:1, 2, 256:256 + 64], oe[0:64, 0:1], g.ident[0:64, 0:64]).then_inc(s["over_t"], 1)
            gate_up(3)
            down(2)
            gate_up(4)
            down(3)
            down(4)
            pe.wait_ge(s["table_in"], 16)
            nc.tensor.transpose(g.PS[:, 0, 0:NBLK], tabr[:, :], g.ident[0:NBLK, 0:NBLK]).then_inc(s["table_t"], 1)

        @block.scalar
        def _(act):
            act.wait_ge(s["logits_done"], 1)
            act.wait_ge(s["init"], 1)
            nc.scalar.activation(SC[:, 0:4, :], g.PS[:, 0, 0:4 * NE].rearrange("p (t e) -> p t e", e=NE), ACT.Sigmoid).then_inc(s["scores_ready"], 1)
            nc.scalar.activation(SC[0:NB, 4, :], g.PS[0:NB, 0, 4 * NE:5 * NE], ACT.Sigmoid).then_inc(s["scores_ready"], 1)
            for t, (t0, m) in enumerate(tiles):
                act.wait_ge(s["gu_done"], t + 1)
                if t >= 1:
                    act.wait_ge(s["sh_ready"], t)
                nc.scalar.activation(sg[0:m, :], g.PS[0:m, 3 + t % 2, 0:DE], ACT.Silu).then_inc(s["sg_ready"], 1)
                nc.scalar.activation(su[0:m, :], g.PS[0:m, 3 + t % 2, DE:2 * DE], ACT.Copy).then_inc(s["su_ready"], 1)
                act.wait_ge(s["ht_done"], t + 1)
                nc.scalar.activation(sht[:, :, 0:m], g.PS[:, 5, 0:2 * P].rearrange("p (j m) -> p j m", j=2)[:, :, 0:m], ACT.Copy).then_inc(s["ht_copied"], 1)
                act.wait_ge(s["y_done"], t + 1)
                nc.scalar.activation(g.ACC[0:m, t, :], g.PS[0:m, 6:8, :].rearrange("p b n -> p (b n)"), ACT.Copy).then_inc(s["y_copied"], 1)

        @block.gpsimd
        def _(pool):
            pool.memset(SC[:, 4, :], 0.5).then_inc(s["init"], 1)
            pool.memset(one64[:, :], 1.0).then_inc(s["init"], 1)
            pool.memset(free[:, :], float(T * TOPK)).then_inc(s["init"], 1)
            pool.iota(lowi[:, :, :], pattern=[[1, NG], [-1, NG]], base=0, channel_multiplier=0).then_inc(s["tok0"], 1)
            pool.iota(toki[:, :, :], pattern=[[P * TOPK, 5], [1, TOPK]], base=0, channel_multiplier=TOPK).then_inc(s["tok0"], 1)
            for t, (t0, m) in enumerate(tiles):
                pool.wait_ge(s["sg_ready"], t + 1)
                pool.wait_ge(s["su_ready"], t + 1)
                if t >= 2:
                    pool.wait_ge(s["ht_done"], t - 1)
                pool.tensor_tensor(sh[0:m, t % 2, :], sg[0:m, :], su[0:m, :], ALU.mult).then_inc(s["sh_ready"], 1)
            pool.wait_ge(s["dest_ready"], 1)
            pool.wait_ge(s["table_cleared"], 16)
            for t, (t0, m) in enumerate(tiles):
                for k in range(8):
                    pool.indirect_dma_start(out=g.slot_dram, out_offset=bass.IndirectOffsetOnAxis(ap=didx[0:m, t, k:k + 1], axis=0),
                                            in_=tok[0:m, t, k:k + 1], in_offset=None).then_inc(s["scattered"], 16)

        @block.vector
        def _(dve):
            link = Link(dve, s["link"])
            V = nc.vector
            dve.wait_ge(s["tok0"], 2)
            V.tensor_copy(tok[:, :, :], toki[:, :, :])
            V.tensor_copy(ip[:, :], g.iota_p[:, :])
            V.tensor_copy(ie[:, :], g.iota_e[:, :])
            link(V.tensor_copy(low[:, :, :], lowi[:, :, :]))
            link(V.tensor_scalar(low[:, :, :], low[:, :, :], 0.0, None, ALU.is_gt))
            dve.wait_ge(s["scores_ready"], 2)
            link(V.tensor_tensor(BI[:, :, :], SC[:, :, :], g.rb_bc[:, :].unsqueeze(1).to_broadcast([P, 5, NE]), ALU.add))
            for t in range(5):
                for q in range(NG):
                    ins = V.max(M8[:, t, q, :], BI[:, t, q * 8:(q + 1) * 8])
            link(ins)
            link(V.tensor_tensor(gs[:, :, :], M8[:, :, :, 0], M8[:, :, :, 1], ALU.add))
            gi, gj = gs[:, :, :].unsqueeze(3).to_broadcast([P, 5, NG, NG]), gs[:, :, :].unsqueeze(2).to_broadcast([P, 5, NG, NG])
            V.tensor_tensor(A[:, :, :, :], gj, gi, ALU.is_gt)
            link(V.tensor_tensor(B[:, :, :, :], gj, gi, ALU.is_equal))
            link(V.tensor_tensor(B[:, :, :, :], B[:, :, :, :], low[:, :, :].unsqueeze(1).to_broadcast([P, 5, NG, NG]), ALU.mult))
            link(V.tensor_tensor(A[:, :, :, :], A[:, :, :, :], B[:, :, :, :], ALU.add))
            link(V.tensor_reduce(cnt[:, :, :], A[:, :, :, :], AX.X, ALU.add))
            link(V.tensor_scalar(cnt[:, :, :], cnt[:, :, :], 4.0, None, ALU.is_lt))
            e8 = lambda v: v.rearrange("p t (q e) -> p (t q) e", e=8)
            g8 = lambda v: v.rearrange("p t q -> p (t q)").unsqueeze(2).to_broadcast([P, 5 * NG, 8])
            link(V.tensor_tensor(e8(BI[:, :, :]), e8(BI[:, :, :]), g8(cnt[:, :, :]), ALU.mult))
            link(V.tensor_scalar(cnt[:, :, :], cnt[:, :, :], BIG, -BIG, ALU.mult, ALU.add))
            link(V.tensor_tensor(e8(BI[:, :, :]), e8(BI[:, :, :]), g8(cnt[:, :, :]), ALU.add))
            for t in range(5):
                ins = V.max(m8[:, t, :], BI[:, t, :])
            link(ins)
            for t in range(5):
                ins = V.match_replace(T1[:, t, :], m8[:, t, :], BI[:, t, :], -3.0 * BIG)
            link(ins)
            V.tensor_tensor(M[:, :, :], T1[:, :, :], BI[:, :, :], ALU.is_lt).then_inc(s["chosen"], 1)
            dve.wait_ge(s["chosen"], 1)
            link(V.tensor_tensor(SC[:, :, :], SC[:, :, :], M[:, :, :], ALU.mult))
            link(V.tensor_reduce(den[:, :], SC[:, :, :], AX.X, ALU.add))
            link(V.reciprocal(den[:, :], den[:, :]))
            link(V.tensor_scalar(den[:, :], den[:, :], ROUTE_SCALE, None, ALU.mult))
            link(V.tensor_tensor(SC[:, :, :], SC[:, :, :], den[:, :].unsqueeze(2).to_broadcast([P, 5, NE]), ALU.mult))
            dve.wait_ge(s["ranks_done"], 1)
            link(V.tensor_copy(cn[:, :], g.PS[:, 2, 0:NE]))
            link(V.tensor_scalar(ex[:, :], cn[:, :], float(CAP), None, ALU.is_gt))
            for q in range(2, (T - 1) // CAP + 1):
                link(V.scalar_tensor_tensor(out=ex[:, :], in0=cn[:, :], scalar=float(q * CAP), in1=ex[:, :], op0=ALU.is_gt, op1=ALU.add))
            dve.wait_ge(s["init"], 2)
            link(V.tensor_tensor_scan(inc[:, :], one64[:, :], ex[:, :], 0.0, ALU.mult, ALU.add))
            link(V.tensor_tensor(ofs[:, :], inc[:, :], ex[:, :], ALU.subtract))
            link(V.tensor_scalar(ofs[:, :], ofs[:, :], float(CAP), float(CAP * (NE - 1)), ALU.mult, ALU.add))
            link(V.tensor_tensor(ofs[:, :], ofs[:, :], ie[:, :], ALU.subtract))
            R = g.PS[:, 1, 0:5 * NE].rearrange("p (t e) -> p t e", e=NE)
            wide = lambda v: v.unsqueeze(1).to_broadcast([P, 5, NE])
            link(V.tensor_scalar(T1[:, :, :], R, float(CAP), None, ALU.is_ge))
            link(V.tensor_tensor(T1[:, :, :], T1[:, :, :], wide(ofs[:, :]), ALU.mult))
            link(V.tensor_tensor(T1[:, :, :], T1[:, :, :], R, ALU.add))
            link(V.tensor_tensor(T1[:, :, :], T1[:, :, :], wide(ie[:, :]), ALU.add))
            link(V.scalar_tensor_tensor(out=DP[:, :, :], in0=T1[:, :, :], scalar=1.0, in1=M[:, :, :], op0=ALU.add, op1=ALU.mult))
            for t in range(5):
                ins = V.max(dk[:, t, :], DP[:, t, :])
            link(ins)
            V.tensor_scalar(didx[:, :, :], dk[:, :, :], -1.0, None, ALU.add).then_inc(s["dest_ready"], 1)
            link(V.tensor_scalar(T1[:, 0, :], inc[:, :], ip[:, 0:1], 0.0, ALU.is_le, ALU.add, accum_out=oe[:, 0:1]))
            V.tensor_scalar(oe[:, 0:1], oe[:, 0:1], float(NE - 1), None, ALU.min).then_inc(s["over_ready"], 1)
            V.tensor_copy(g.over[0:1, 64:65], inc[0:1, NE - 1:NE])
            dve.wait_ge(s["over_t"], 1)
            V.tensor_copy(g.over[0:1, 0:64], g.PS[0:1, 2, 256:256 + 64])
            for t in range(5):
                for k in range(8):
                    ins = V.scalar_tensor_tensor(out=T1[:, t, :], in0=DP[:, t, :], scalar=dk[:, t, k:k + 1], in1=SC[:, t, :],
                                                 op0=ALU.is_equal, op1=ALU.mult, accum_out=g.wk[:, t, k:k + 1])
                    link(ins)
            dve.wait_ge(s["table_t"], 1)
            link(V.tensor_copy(g.slots[:, 1, :], g.PS[:, 0, 0:NBLK]))
            V.tensor_scalar(g.slots[:, 0, :], g.slots[:, 1, :], 3, None, ALU.logical_shift_right).then_inc(s["slots_ready"], 1)


def phase_moe(nc, g, x):
    NW = 4
    names = ("xt_done", "xt_copied", "gu_done", "silu_ready", "h_ready", "ht_done", "ht_copied", "y_done", "y_copied",
             "o_gathered", "o_w", "o_xt", "o_xtc", "o_gu", "o_silu", "o_h", "o_ht", "o_htc", "o_y", "o_yc", "o_stored", "icol", "icol_seen",
             "y_free", "o_free", "x_zeroed")
    s = {n: g.sem("moe_" + n) for n in names}
    s_x = [g.sem(f"moe_x{i}_gathered") for i in range(NW)]
    s_gu = [g.sem(f"moe_gu{i}_loaded") for i in range(NW)]
    s_d = [g.sem(f"moe_d{i}_loaded") for i in range(NW)]
    s_y = [g.sem(f"moe_y{i}_stored") for i in range(2)]
    with ExitStack() as ctx:
        sb = lambda n, sh: ctx.enter_context(nc.sbuf_tensor("moe_" + n, sh, F32))
        WG, WD = [sb(f"wgu{i}", [P, 2, KC, DE]) for i in range(NW)], [sb(f"wd{i}", [P, 2, D]) for i in range(NW)]
        xg, xt = [sb(f"x{i}", [P, D]) for i in range(NW)], [sb(f"xt{i}", [P, KC, P]) for i in range(2)]
        sg, hh, ht = [sb(f"sg{i}", [P, DE]) for i in range(2)], [sb(f"h{i}", [P, DE]) for i in range(2)], [sb(f"ht{i}", [P, 2, P]) for i in range(2)]
        yy = [sb(f"y{i}", [P, D]) for i in range(2)]
        icol = [ctx.enter_context(nc.sbuf_tensor(f"moe_icol{i}", [P, 2], I32)) for i in range(NW)]
        block = ctx.enter_context(nc.Block())
        pair = lambda b: g.PS[:, b:b + 2, :].rearrange("p b n -> p (b n)")
        BODY = NE // NW - 1

        def load_gate_up(sp, e, b, sem):
            sp.dma_start(WG[b][:, 0, :, :], x["w_exp_gate"][e].rearrange("o (p k) f -> p (o k) f", k=KC)).then_inc(sem, 16)
            sp.dma_start(WG[b][:, 1, :, :], x["w_exp_up"][e].rearrange("o (p k) f -> p (o k) f", k=KC)).then_inc(sem, 16)

        def load_down(sp, e, b, sem):
            sp.dma_start(WD[b][:, :, :], x["w_exp_down"][e].rearrange("o (p j) n -> p (o j) n", j=2)).then_inc(sem, 16)

        @block.sync
        def _(sp):
            for b in range(NW):
                load_gate_up(sp, slice(b, b + 1), b, s_gu[b])
                load_down(sp, slice(b, b + 1), b, s_d[b])
            with sp.Fori(0, BODY) as i:
                for b in range(NW):
                    sp.wait_ge(s["gu_done"], i * NW + b + 1)
                    load_gate_up(sp, bass.ds(i * NW + NW + b, 1), b, s_gu[b])
                    sp.wait_ge(s["y_done"], i * NW + b + 1)
                    load_down(sp, bass.ds(i * NW + NW + b, 1), b, s_d[b])
            total = sp.value_load(g.over[0:1, NE:NE + 1], min_val=0, max_val=NOV)
            sp.wait_ge(s["y_done"], NE)
            sp.sem_inc(s["o_y"], 1)
            with sp.If(total > 0):
                with sp.Fori(0, NOV) as i:
                    with sp.If(total > i):
                        e = sp.value_load(g.over[0:1, bass.ds(i, 1)], min_val=0, max_val=NE - 1)
                        sp.wait_ge(s["o_y"], i + 1)
                        load_gate_up(sp, bass.ds(e, 1), 0, s["o_w"])
                        load_down(sp, bass.ds(e, 1), 0, s["o_w"])

        @block.gpsimd
        def _(pool):
            def take_column(col, u, count):
                pool.tensor_copy(icol[u][:, :], g.slots[:, :, col].rearrange("p w o -> p (w o)")).then_inc(s["icol"], 1)
                pool.wait_ge(s["icol"], count)
                pool.sem_inc(s["icol_seen"], 1)

            def gather(u, sem):
                pool.indirect_dma_start(out=xg[u][:, :], out_offset=None, in_=g.h_dram,
                                        in_offset=bass.IndirectOffsetOnAxis(ap=icol[u][:, 0:1], axis=0),
                                        bounds_check=T - 1, oob_is_err=False).then_inc(sem, 16)

            def scatter(u, b, sem):
                pool.sem_inc(s["icol_seen"], 1)
                pool.indirect_dma_start(out=g.y_dram, out_offset=bass.IndirectOffsetOnAxis(ap=icol[u][:, 1:2], axis=0),
                                        in_=yy[b][:, :], in_offset=None,
                                        bounds_check=T * TOPK - 1, oob_is_err=False).then_inc(sem, 16)

            for u in range(NW):
                pool.memset(xg[u][:, :], 0.0).then_inc(s["x_zeroed"], 1)
            pool.wait_ge(s["x_zeroed"], NW)
            for u in range(NW):
                take_column(slice(u, u + 1), u, u + 1)
                gather(u, s_x[u])
            with pool.Fori(0, BODY) as i:
                for u in range(NW):
                    pool.wait_ge(s["y_copied"], i * NW + u + 2)
                    scatter(u, u % 2, s_y[u % 2])
                    pool.wait_ge(s_y[u % 2], i * 16 * NW // 2 + 16 * (u // 2 + 1))
                    pool.sem_inc(s["y_free"], 1)
                    take_column(bass.ds(i * NW + NW + u, 1), u, i * NW + NW + u + 1)
                    gather(u, s_x[u])
            for u in range(NW):
                pool.wait_ge(s["y_copied"], BODY * NW + u + 2)
                scatter(u, u % 2, s_y[u % 2])
                pool.wait_ge(s_y[u % 2], 16 * (BODY * NW // 2 + u // 2 + 1))
                pool.sem_inc(s["y_free"], 1)
            total = pool.value_load(g.over[0:1, NE:NE + 1], min_val=0, max_val=NOV)
            with pool.If(total > 0):
                with pool.Fori(0, NOV) as i:
                    with pool.If(total > i):
                        take_column(bass.ds(i + NE, 1), 0, i + NE + 1)
                        gather(0, s["o_gathered"])
                        pool.wait_ge(s["o_yc"], i + 2)
                        scatter(0, 0, s["o_stored"])
                        pool.wait_ge(s["o_stored"], i * 16 + 16)
                        pool.sem_inc(s["o_free"], 1)

        @block.tensor
        def _(pe):
            def rows_transpose(b):
                for k in range(KC):
                    ins = nc.tensor.transpose(g.PS[:, k // 4, (k % 4) * P:(k % 4 + 1) * P], xg[b][:, k::KC], g.ident[:, :])
                return ins

            def gate_up_products(b, w):
                for k in range(KC):
                    ins = nc.tensor.matmul(g.PS[:, 2 + b, :], xt[b][:, k, :], WG[w][:, :, k, :], start=k == 0, stop=k == KC - 1)
                return ins

            def h_transpose(b):
                for j in range(2):
                    ins = nc.tensor.transpose(g.PS[:, 4, j * P:(j + 1) * P], hh[b][:, j::2], g.ident[:, :])
                return ins

            def down_products(b, w):
                for h in range(2):
                    for j in range(2):
                        ins = nc.tensor.matmul(g.PS[:, 5 + h, :], ht[b][:, j, :], WD[w][:, j, h * 512:(h + 1) * 512], start=j == 0, stop=j == 1)
                return ins

            def rows_t(i, u):
                pe.wait_ge(s_x[u % NW], i * 16 + 16 * (u // NW + 1))
                pe.wait_ge(s["xt_copied"], i * NW + u + 1)
                rows_transpose(u % NW).then_inc(s["xt_done"], 1)

            def gate_up(i, u):
                pe.wait_ge(s_gu[u % NW], i * 32 + 32 * (u // NW + 1))
                pe.wait_ge(s["xt_copied"], i * NW + u + 2)
                pe.wait_ge(s["h_ready"], i * NW + u + 1)
                gate_up_products(u % 2, u % NW).then_inc(s["gu_done"], 1)

            def h_t(i, u):
                pe.wait_ge(s["h_ready"], i * NW + u + 3)
                h_transpose(u % 2).then_inc(s["ht_done"], 1)

            def down(i, u):
                pe.wait_ge(s_d[u % NW], i * 16 + 16 * (u // NW + 1))
                pe.wait_ge(s["ht_copied"], i * NW + u + 1)
                pe.wait_ge(s["y_copied"], i * NW + u + 1)
                down_products(u % 2, u % NW).then_inc(s["y_done"], 1)

            rows_t(0, 0)
            gate_up(0, 0)
            rows_t(0, 1)
            with pe.Fori(0, BODY) as i:
                for u in range(NW):
                    h_t(i, u)
                    gate_up(i, u + 1)
                    rows_t(i, u + 2)
                    down(i, u)
            for u in range(NW):
                h_t(BODY, u)
                if u + 1 < NW:
                    gate_up(BODY, u + 1)
                if u + 2 < NW:
                    rows_t(BODY, u + 2)
                down(BODY, u)
            total = pe.value_load(g.over[0:1, NE:NE + 1], min_val=0, max_val=NOV)
            pe.wait_ge(s["y_copied"], NE + 1)
            with pe.If(total > 0):
                with pe.Fori(0, NOV) as i:
                    with pe.If(total > i):
                        pe.wait_ge(s["o_gathered"], i * 16 + 16)
                        rows_transpose(0).then_inc(s["o_xt"], 1)
                        pe.wait_ge(s["o_xtc"], i + 1)
                        pe.wait_ge(s["o_w"], i * 48 + 48)
                        gate_up_products(0, 0).then_inc(s["o_gu"], 1)
                        pe.wait_ge(s["o_h"], i + 1)
                        h_transpose(0).then_inc(s["o_ht"], 1)
                        pe.wait_ge(s["o_htc"], i + 1)
                        pe.wait_ge(s["o_yc"], i + 1)
                        down_products(0, 0).then_inc(s["o_y"], 1)

        @block.scalar
        def _(act):
            def silu(i, u):
                act.wait_ge(s["gu_done"], i * NW + u + 1)
                act.wait_ge(s["h_ready"], i * NW + u + 1)
                nc.scalar.activation(sg[u % 2][:, :], g.PS[:, 2 + u % 2, 0:DE], ACT.Silu).then_inc(s["silu_ready"], 1)

            def rows_out(i, u):
                act.wait_ge(s["y_done"], i * NW + u + 1)
                act.wait_ge(s["y_free"], i * NW + u + 1)
                nc.scalar.activation(yy[u % 2][:, :], pair(5), ACT.Copy).then_inc(s["y_copied"], 1)

            act.sem_inc(s["y_free"], 2)
            act.sem_inc(s["y_copied"], 1)
            act.sem_inc(s["o_yc"], 1)
            act.sem_inc(s["o_free"], 1)
            silu(0, 0)
            with act.Fori(0, BODY) as i:
                for u in range(NW):
                    silu(i, u + 1)
                    rows_out(i, u)
            for u in range(NW):
                if u + 1 < NW:
                    silu(BODY, u + 1)
                rows_out(BODY, u)
            total = act.value_load(g.over[0:1, NE:NE + 1], min_val=0, max_val=NOV)
            act.wait_ge(s["y_free"], NE + 2)
            with act.If(total > 0):
                with act.Fori(0, NOV) as i:
                    with act.If(total > i):
                        act.wait_ge(s["o_gu"], i + 1)
                        nc.scalar.activation(sg[0][:, :], g.PS[:, 2, 0:DE], ACT.Silu).then_inc(s["o_silu"], 1)
                        act.wait_ge(s["o_y"], i + 2)
                        act.wait_ge(s["o_free"], i + 1)
                        nc.scalar.activation(yy[0][:, :], pair(5), ACT.Copy).then_inc(s["o_yc"], 1)

        @block.vector
        def _(dve):
            copy_rows = lambda b: nc.vector.tensor_copy(xt[b][:, :, :].rearrange("p k m -> p (k m)"), pair(0))
            copy_ht = lambda b: nc.vector.tensor_copy(ht[b][:, :, :].rearrange("p j m -> p (j m)"), g.PS[:, 4, 0:2 * P])
            gate = lambda b: nc.vector.tensor_tensor(hh[b][:, :], sg[b][:, :], g.PS[:, 2 + b, DE:2 * DE], ALU.mult)

            def rows_copy(i, u):
                dve.wait_ge(s["xt_done"], i * NW + u + 1)
                if not isinstance(i, int) or i * NW + u >= 2:
                    dve.wait_ge(s["gu_done"], i * NW + u - 1)
                copy_rows(u % 2).then_inc(s["xt_copied"], 1)

            def gated(i, u):
                dve.wait_ge(s["silu_ready"], i * NW + u + 1)
                if not isinstance(i, int) or i * NW + u >= 2:
                    dve.wait_ge(s["ht_done"], i * NW + u - 1)
                gate(u % 2).then_inc(s["h_ready"], 1)

            def ht_copy(i, u):
                dve.wait_ge(s["ht_done"], i * NW + u + 1)
                if not isinstance(i, int) or i * NW + u >= 2:
                    dve.wait_ge(s["y_done"], i * NW + u - 1)
                copy_ht(u % 2).then_inc(s["ht_copied"], 1)

            def step(i, u):
                ht_copy(i, u)
                gated(i, u + 1)
                rows_copy(i, u + 2)

            dve.sem_inc(s["xt_copied"], 1)
            dve.sem_inc(s["h_ready"], 2)
            rows_copy(0, 0)
            rows_copy(0, 1)
            gated(0, 0)
            for u in range(NW):
                step(0, u)
            with dve.Fori(1, BODY) as i:
                for u in range(NW):
                    step(i, u)
            for u in range(NW):
                ht_copy(BODY, u)
                if u + 1 < NW:
                    gated(BODY, u + 1)
                if u + 2 < NW:
                    rows_copy(BODY, u + 2)
            total = dve.value_load(g.over[0:1, NE:NE + 1], min_val=0, max_val=NOV)
            with dve.If(total > 0):
                with dve.Fori(0, NOV) as i:
                    with dve.If(total > i):
                        dve.wait_ge(s["o_xt"], i + 1)
                        copy_rows(0).then_inc(s["o_xtc"], 1)
                        dve.wait_ge(s["o_silu"], i + 1)
                        gate(0).then_inc(s["o_h"], 1)
                        dve.wait_ge(s["o_ht"], i + 1)
                        copy_ht(0).then_inc(s["o_htc"], 1)


def phase_final(nc, g, x, y):
    NR, K = 3, 4
    s_acc, s_var, s_rstd, s_y, s_st, s_l, s_al, s_used = (g.sem("fin_" + n) for n in
        ("acc_ready", "var_ready", "rstd_ready", "y_ready", "y_stored", "link", "act_link", "row_used"))
    s_r = [g.sem(f"fin_row{i}_loaded") for i in range(NR)]
    s_h = [g.sem(f"fin_h{i}_loaded") for i in range(2)]
    s_in = g.sem("fin_norm_loaded")
    tiles = tok_tiles()
    with ExitStack() as ctx:
        sb = lambda n, sh: ctx.enter_context(nc.sbuf_tensor("fin_" + n, sh, F32))
        row, hb = [sb(f"row{i}", [P, K, D]) for i in range(NR)], [sb(f"h{i}", [P, D]) for i in range(2)]
        gain, shift, stats, agg, rstd = sb("gain", [P, D]), sb("shift", [P, D]), sb("stats", [P, 2, 6]), sb("agg", [P, 2]), sb("rstd", [P, 1])
        block = ctx.enter_context(nc.Block())

        @block.sync
        def _(sp):
            sp.dma_start(gain[:, :], x["ln2_g"].partition_broadcast(P)).then_inc(s_in, 16)
            sp.dma_start(shift[:, :], x["ln2_b"].partition_broadcast(P)).then_inc(s_in, 16)
            for t, (t0, m) in enumerate(tiles):
                rows = g.y_dram[t0 * TOPK:(t0 + m) * TOPK, :].rearrange("(p k) d -> p k d", k=TOPK)
                for j in range(TOPK // K):
                    n = t * (TOPK // K) + j
                    if n >= NR:
                        sp.wait_ge(s_used, (n - NR + 1) * K)
                    sp.dma_start(row[n % NR][0:m, :, :], rows[:, j * K:(j + 1) * K, :]).then_inc(s_r[n % NR], 16)
                if t >= 2:
                    sp.wait_ge(s_acc, t - 1)
                sp.dma_start(hb[t % 2][0:m, :], g.h_dram[t0:t0 + m, :]).then_inc(s_h[t % 2], 16)
            for t, (t0, m) in enumerate(tiles):
                sp.wait_ge(s_y, t + 1)
                dst = y["y_prompt"][0, t0:t0 + m, :] if t < NT else y["y_sample"].rearrange("b o d -> (b o) d")
                sp.dma_start(dst, g.ACC[0:m, t, :]).then_inc(s_st, 16)
            sp.wait_ge(s_st, 16 * 5)

        @block.scalar
        def _(act):
            link = Link(act, s_al)
            for t, (t0, m) in enumerate(tiles):
                act.wait_ge(s_var, t + 1)
                link(nc.scalar.activation(rstd[0:m, :], agg[0:m, 1:2], ACT.Ln, bias=g.eps_ln[0:m]))
                nc.scalar.activation(rstd[0:m, :], rstd[0:m, :], ACT.Exp, scale=-0.5).then_inc(s_rstd, 1)

        @block.vector
        def _(dve):
            link = Link(dve, s_l)
            dve.wait_ge(s_in, 32)
            for t, (t0, m) in enumerate(tiles):
                acc = g.ACC[0:m, t, :]
                for k in range(TOPK):
                    n = (t * TOPK + k) // K
                    if k % K == 0:
                        dve.wait_ge(s_r[n % NR], 16 * (n // NR + 1))
                    nc.vector.scalar_tensor_tensor(out=acc, in0=row[n % NR][0:m, k % K, :], scalar=g.wk[0:m, t, k:k + 1], in1=acc,
                                                   op0=ALU.mult, op1=ALU.add).then_inc(s_used, 1)
                    dve.wait_ge(s_used, t * TOPK + k + 1)
                dve.wait_ge(s_h[t % 2], 16 * (t // 2 + 1))
                nc.vector.scalar_tensor_tensor(out=acc, in0=hb[t % 2][0:m, :], scalar=ALPHA, in1=acc,
                                               op0=ALU.mult, op1=ALU.add).then_inc(s_acc, 1)
                dve.wait_ge(s_acc, t + 1)
                layer_norm_rows(nc, dve, link, acc, acc, stats, agg, rstd, gain, shift, m, s_var, s_rstd, t + 1).then_inc(s_y, 1)


def build(nc, x, y, stop=99):
    g = Shared()
    phase_sems = []

    def sem(name):
        phase_sems.append(nc.alloc_semaphore(name=name))
        return phase_sems[-1]

    def end_phase():
        nc.clear_and_free_semaphores(phase_sems)
        nc.all_engine_barrier(sem_only=True)
        phase_sems.clear()

    g.sem = sem
    g.h_dram = nc.dram_tensor("scratch_h", [T, D], F32, kind="Internal").ap()
    g.y_dram = nc.dram_tensor("scratch_expert_rows", [T * TOPK, D], F32, kind="Internal").ap()
    g.slot_dram = nc.dram_tensor("scratch_slot_tokens", [NBLK * CAP, 1], F32, kind="Internal").ap()
    with ExitStack() as ctx:
        alloc = lambda c: lambda n, s, d=F32: c.enter_context(nc.sbuf_tensor(n, s, d))
        sb = alloc(ctx)
        g.PS = ctx.enter_context(nc.psum_tensor("PS", [P, 8, 512], F32))
        g.ident, g.UT, g.UTs, g.TRI, g.ones, g.nones, g.bones = (
            sb(n, [P, P]) for n in ("ident", "UT", "UTs", "TRI", "ones", "nones", "bones"))
        g.LM = sb("LM", [P, 7, P])
        g.one_c, g.eps_l2, g.eps_ln = (sb(n, [P, 1])[:, :] for n in ("one_c", "eps_l2", "eps_ln"))
        g.iota_p, g.iota_e = sb("iota_p", [P, 1], I32), sb("iota_e", [P, NE], I32)
        g.A_bc, g.dt_bc, g.sbb_bc, g.rb_bc = (sb(n, [P, w]) for n, w in
                                              (("A_bc", H), ("dt_bc", H), ("sbb_bc", H), ("rb_bc", NE)))
        g.nw_col = sb("nw_col", [P, 1])
        g.S = sb("S", [P, 4, HD])
        g.wk = sb("wk", [P, 5, TOPK])
        g.slots, g.over = sb("slots", [P, 2, NBLK], I32), sb("over", [1, NE + 1], I32)
        g.XT = sb("XT", [P, KC, T])
        with ExitStack() as mix:
            ms = alloc(mix)
            g.OT, g.PT = ms("OT", [P, 12, T]), ms("PT", [P, NCH, T])
            with ExitStack() as att:
                ab = alloc(att)
                g.BA, g.XS, g.CW = ab("BA", [16, T]), ab("XS", [NB, GT0]), ab("CW", [P, 12, 4])
                g.MKT, g.MV, g.VT = ab("MKT", [P, MH, NM]), ab("MV", [P, 2, MH * P]), ab("VT", [P, NT, SBW])
                with nc.sbuf_tensor("MT", [P, KC, NM], F32) as MT:
                    g.MT = MT
                    phase_load(nc, g, x)
                    end_phase()
                    if stop == 0: return
                    proj_cols(nc, g, x["w_in"], 0, 0, 14, "in_a")
                    end_phase()
                    proj_cols(nc, g, x["w_in"], MQ0, CM, 2, "in_m")
                    end_phase()
                    if stop == 1: return
                    phase_small(nc, g, x, y)
                    end_phase()
                phase_rows(nc, g, x, y)
                end_phase()
                if stop == 2: return
                phase_sb(nc, g)
                end_phase()
                if stop == 3: return
                phase_mem(nc, g)
                end_phase()
                if stop == 4: return
                with ExitStack() as gd:
                    gb = alloc(gd)
                    g.KTM, g.VTM = g.PT[:, 0:NT, 0:SBW], g.PT[:, NT:2 * NT, 0:SBW]
                    g.GC, g.EGC, g.TAIL, g.BETA = (gb(n, [P, NT * H]) for n in ("GC", "EGC", "TAIL", "BETA"))
                    g.EGL, g.GCT = gb("EGL", [P, NT, 4]), gb("GCT", [NT * H, P])
                    phase_gdn_prep(nc, g)
                    end_phase()
                    phase_gdn(nc, g, y)
                    end_phase()
                if stop == 5: return
                phase_sample(nc, g, x, y)
                end_phase()
                if stop == 6: return
            proj_cols(nc, g, x["w_in"], GT0, 0, 12, "in_g", sigmoid=True)
            end_phase()
            phase_merge(nc, g, x)
            end_phase()
            if stop == 7: return
            g.H = g.PT[:, 0:10, :].rearrange("p c t -> p (c t)")[:, 0:5 * D].rearrange("p (t d) -> p t d", d=D)
            phase_out(nc, g, x)
            end_phase()
            if stop == 8: return
        g.ACC = sb("ACC", [P, NT + 1, D])
        phase_route(nc, g, x)
        end_phase()
        if stop == 9: return
        phase_moe(nc, g, x)
        end_phase()
        if stop == 10: return
        phase_final(nc, g, x, y)


INPUTS = ("x_prompt", "x_sample", "cache_sb_k", "cache_sb_v", "page_table", "state_gdn", "state_gdn_conv", "cache_mem_k",
          "cache_mem_v", "mem_prompt", "w_in", "sb_logit_bias", "conv_w", "gdn_A_log", "gdn_dt_bias", "gdn_norm_w",
          "w_mem_k", "w_mem_v", "w_br_sb", "w_br_gdn", "w_br_mem", "w_o", "ln1_g", "ln1_b", "w_router", "router_bias",
          "w_exp_gate", "w_exp_up", "w_exp_down", "w_sh_gate", "w_sh_up", "w_sh_down", "ln2_g", "ln2_b")
OUTPUTS = (("y_prompt", (1, SEQ, D)), ("y_sample", (NB, 1, D)),
           ("sb_k_prompt", (1, SEQ, H, HD)), ("sb_v_prompt", (1, SEQ, H, HD)),
           ("state_prompt", (1, H, HD, HD)), ("conv_prompt", (1, 3, 3 * SBW)),
           ("mem_k_prompt", (1, NM, MH, P)), ("mem_v_prompt", (1, NM, MH, P)),
           ("sb_k_sample", (NB, 1, H, HD)), ("sb_v_sample", (NB, 1, H, HD)),
           ("state_sample", (NB, H, HD, HD)), ("conv_sample", (NB, 3, 3 * SBW)))


def kernel(**inputs):
    import concourse.bacc as bacc
    from concourse.bass_utils import run_bass_kernel_spmd

    nc = bacc.Bacc("TRN2", target_bir_lowering=False, num_devices=1)
    arrays = {"in_" + n: np.ascontiguousarray(inputs[n]) for n in INPUTS}
    x = {n: nc.dram_tensor("in_" + n, arrays["in_" + n].shape, mybir.dt.from_np(arrays["in_" + n].dtype),
                                             kind="ExternalInput").ap() for n in INPUTS}
    y = {n: nc.dram_tensor("out_" + n, shape, F32, kind="ExternalOutput").ap() for n, shape in OUTPUTS}
    build(nc, x, y)
    r = run_bass_kernel_spmd(nc, [arrays], core_ids=[0])
    return tuple(r.results[0]["out_" + n] for n, _ in OUTPUTS)
```

```python
import numpy as np
from contextlib import ExitStack

import concourse.bass as bass
import concourse.mybir as mybir

F32 = mybir.dt.float32
I32 = mybir.dt.int32
ALU = mybir.AluOpType
ACT = mybir.ActivationFunctionType
AX = mybir.AxisListType

P = 128
D = 1024
KC = D // P
SEQ = 512
NB = 8
T = SEQ + NB
TH = T // 2
NT = SEQ // P
H = 8
HD = 64
MH = 4
NM = 256
PAST = 512
PG = PAST // P
N_POOL = 40
SBW = H * HD
CQ, CK, CV, CG, CZ, CM = 0, 4, 8, 12, 24, 28
NCH = 32
GATE = list(range(8, 12)) + list(range(28, 32)) + list(range(16, 24)) + list(range(8))
MERGED = list(range(12, 16)) + list(range(24, 28))
G_PREP, G_SMP = 8, 8
BA0 = 3584
MQ0 = 3600
GT0 = 4112
NE = 64
NG = 8
DE = 256
TOPK = 8
CAP = 128
NOV = T * TOPK // CAP
NBLK = NE + NOV
NW = 4
ALPHA = 2.0 ** 0.25
LN_EPS = 1e-5
L2_EPS = 1e-6
ROUTE_SCALE = 2.5
BIG = 1e30


class Shared:
    pass


class Link:

    def __init__(self, eng, sem):
        self.eng, self.sem, self.n, self.off = eng, sem, 0, 0

    def __call__(self, ins):
        self.n += 1
        ins.then_inc(self.sem, 1)
        self.eng.wait_ge(self.sem, self.off + self.n)
        return ins

    def loop(self, i, per, base):
        self.off, self.n = i * per + base, 0

    def after(self, total):
        self.off, self.n = 0, total


def tok_tiles():
    return [(t * P, P) for t in range(NT)] + [(SEQ, NB)]


def exp_ln_table(nc):
    nc.scalar.preload_act_table_set("natural_log_exp_and_others")


def phase_load(nc, g, x):
    s_const, s_zero, s_bones, s_tp, s_cp = (g.sem(n) for n in
        ("const_ready", "fills_ready", "block_ones_ready", "x_transposed", "xt_copied"))
    s_xl = [g.sem(f"x_loaded{i}") for i in range(2 + NT)]
    s_small = g.sem("small_loaded")
    with ExitStack() as ctx:
        xt = ctx.enter_context(nc.sbuf_tensor("x_rows", [P, NT + 1, D], F32))
        mt = ctx.enter_context(nc.sbuf_tensor("mem_rows", [P, 2, D], F32))
        rows = [(xt[:, t, :], P) for t in range(NT)] + [(xt[0:NB, NT, :], NB)] + [(mt[:, m, :], P) for m in range(2)]
        outs = [g.XT[:, :, t * P:(t + 1) * P] for t in range(NT)] + [g.XT[:, :, SEQ:T]] + \
               [g.MT[:, :, m * P:(m + 1) * P] for m in range(2)]
        land = s_xl[2:] + [s_xl[0]] + [s_xl[1]] * 2
        block = ctx.enter_context(nc.Block())

        @block.sync
        def _(sp):
            for t in range(NT):
                sp.dma_start(xt[:, t, :], x["x_prompt"][0, t * P:(t + 1) * P, :]).then_inc(s_xl[2 + t], 16)
            sp.dma_start(xt[0:NB, NT, :], x["x_sample"].rearrange("b o d -> (b o) d")).then_inc(s_xl[0], 16)
            sp.dma_start(mt[:, :, :], x["mem_prompt"].rearrange("b (t p) d -> p (b t) d", p=P)).then_inc(s_xl[1], 16)
            small = [(g.A_bc, x["gdn_A_log"]), (g.dt_bc, x["gdn_dt_bias"]), (g.sbb_bc, x["sb_logit_bias"]),
                     (g.rb_bc, x["router_bias"])]
            for dst, src in small:
                sp.dma_start(dst[:, :], src.partition_broadcast(P)).then_inc(s_small, 16)
            for half in range(2):
                sp.dma_start(g.nw_col[half * HD:(half + 1) * HD, :], x["gdn_norm_w"].rearrange("(p o) -> p o", o=1)).then_inc(s_small, 16)
            sp.wait_ge(s_small, 16 * (len(small) + 2))

        @block.gpsimd
        def _(pool):
            for z in (g.ident[:, :], g.LM[:, :, :]):
                pool.memset(z, 0.0).then_inc(s_zero, 1)
            for z, v in ((g.ones, 1.0), (g.nones, -1.0), (g.UT, 1.0), (g.UTs, 1.0), (g.TRI, -1.0)):
                pool.memset(z[:, :], v).then_inc(s_zero, 1)
            for z, v in ((g.one_c, 1.0), (g.eps_l2, L2_EPS), (g.eps_ln, LN_EPS), (g.S[:, :, :], 0.0)):
                pool.memset(z, v).then_inc(s_zero, 1)
            pool.wait_ge(s_zero, 11)
            pool.affine_select(out=g.ident[:, :], in_=g.ident[:, :], compare_op=ALU.not_equal, fill=1.0,
                               base=0, pattern=[[-1, P]], channel_multiplier=1).then_inc(s_const, 1)
            pool.affine_select(out=g.UT[:, :], in_=g.UT[:, :], compare_op=ALU.is_ge, fill=0.0,
                               base=0, pattern=[[1, P]], channel_multiplier=-1).then_inc(s_const, 1)
            pool.affine_select(out=g.UTs[:, :], in_=g.UTs[:, :], compare_op=ALU.is_gt, fill=0.0,
                               base=0, pattern=[[1, P]], channel_multiplier=-1).then_inc(s_const, 1)
            pool.affine_select(out=g.TRI[:, :], in_=g.TRI[:, :], compare_op=ALU.is_ge, fill=0.0,
                               base=0, pattern=[[-1, P]], channel_multiplier=1).then_inc(s_const, 1)
            for n in range(7):
                s = 1 << n
                v = g.LM[:, n, :].rearrange("p (b h s) -> p b h s", h=2, s=s)[:, :, 1, :]
                nb = P // (2 * s)
                pool.memset(v, 1.0).then_inc(s_zero, 1)
                pool.wait_ge(s_zero, 12 + 3 * n)
                pool.affine_select(out=v, in_=v, compare_op=ALU.is_ge, fill=0.0, base=0,
                                   pattern=[[-2 * s, nb], [0, s]], channel_multiplier=1).then_inc(s_zero, 1)
                pool.wait_ge(s_zero, 13 + 3 * n)
                pool.affine_select(out=v, in_=v, compare_op=ALU.is_ge, fill=0.0, base=s - 1,
                                   pattern=[[2 * s, nb], [0, s]], channel_multiplier=-1).then_inc(s_zero, 1)
            pool.iota(g.iota_p[:, :], pattern=[[0, 1]], base=0, channel_multiplier=1).then_inc(s_const, 1)
            pool.iota(g.iota_e[:, :], pattern=[[CAP, NE]], base=0, channel_multiplier=0).then_inc(s_const, 1)

        @block.tensor
        def _(pe):
            pe.wait_ge(s_const, 1)
            for n, (src, m) in enumerate(rows):
                pe.wait_ge(land[n], 16)
                if n >= 2:
                    pe.wait_ge(s_cp, n - 1)
                for k in range(KC):
                    ins = nc.tensor.transpose(g.PS[:, 2 * (n % 2) + k // 4, (k % 4) * P:(k % 4) * P + m],
                                              src[:, k::KC], g.ident[0:m, 0:m])
                ins.then_inc(s_tp, 1)

        @block.vector
        def _(dve):
            nc.vector.memset(g.bones[:, :], 0.0).then_inc(s_bones, 1)
            dve.wait_ge(s_bones, 1)
            for half in range(2):
                q = slice(half * HD, (half + 1) * HD)
                nc.vector.memset(g.bones[q, q], 1.0).then_inc(s_bones, 1)
            for n, (_, m) in enumerate(rows):
                dve.wait_ge(s_tp, n + 1)
                src = g.PS[:, 2 * (n % 2):2 * (n % 2) + 2, :].rearrange("p b (k m) -> p (b k) m", m=P)[:, :, 0:m]
                nc.vector.tensor_copy(outs[n], src).then_inc(s_cp, 1)


def proj_cols(nc, g, src, segments, name, sigmoid=False, ahead=None):
    starts = [sum(n for _, _, n in segments[:j]) for j in range(len(segments))]
    s_w = [g.sem(f"{name}_w{i}_loaded") for i in range(2)]
    s_mm, s_free = g.sem(f"{name}_chunk_done"), g.sem(f"{name}_banks_free")
    wv = src.rearrange("(p k) n -> p k n", k=KC)
    with ExitStack() as ctx:
        W = [ctx.enter_context(nc.sbuf_tensor(f"{name}_w{i}", [P, KC, 256], F32)) for i in range(2)]
        block = ctx.enter_context(nc.Block())

        @block.sync
        def _(sp):
            for i0, (col0, _, n) in zip(starts, segments):
                with sp.Fori(0, n) as i:
                    for b in range(2):
                        sp.wait_ge(s_free, i * 4 + (4 * i0 + 2 * b + 1))
                        sp.dma_start(W[b][:, :, :], wv[:, :, bass.ds(i * 512 + col0 + b * 256, 256)]).then_inc(s_w[b], 16)
            if ahead:
                ahead(sp)

        @block.tensor
        def _(pe):
            with pe.Fori(0, sum(n for _, _, n in segments)) as i:
                for b in range(2):
                    pe.wait_ge(s_w[b], i * 16 + 16)
                    for c in range(2):
                        pe.wait_ge(s_free, i * 4 + 2 * b + c + 2)
                        for h in range(2):
                            for k in range(KC):
                                ins = nc.tensor.matmul(g.PS[:, 2 * c + h, 0:TH], W[b][:, k, c * P:(c + 1) * P],
                                                       g.XT[:, k, h * TH:(h + 1) * TH], start=k == 0, stop=k == KC - 1)
                        ins.then_inc(s_mm, 1)

        def out_of_banks(eng, func):
            eng.sem_inc(s_free, 3)
            for i0, (_, out0, n_pairs) in zip(starts, segments):
                with eng.Fori(0, n_pairs) as i:
                    for n in range(4):
                        eng.wait_ge(s_mm, i * 4 + (4 * i0 + n + 1))
                        func(g.PT[:, bass.ds(i * 4 + out0 + n, 1), :].rearrange("p o (h t) -> p (o h) t", h=2),
                             g.PS[:, 2 * (n % 2):2 * (n % 2) + 2, 0:TH]).then_inc(s_free, 1)

        def copies(dve):
            out_of_banks(dve, nc.vector.tensor_copy)

        def sigmoids(act):
            for v in (g.PT[:, 8:12, :], g.PT[:, 16:24, :], g.PT[:, 28:32, :]):
                nc.scalar.activation(v, v, ACT.Sigmoid)
            out_of_banks(act, lambda dst, banks: nc.scalar.activation(dst, banks, ACT.Sigmoid))

        block.scalar(sigmoids) if sigmoid else block.vector(copies)


def phase_small(nc, g, x, y):
    s_w = [g.sem(f"small_w{i}_loaded") for i in range(3)]
    s_mm, s_cp, s_mkt, s_mktc, s_out = (g.sem(n) for n in
        ("small_mm_done", "small_copied", "mem_kt_done", "mem_kt_copied", "mem_kv_stored"))
    with ExitStack() as ctx:
        wba = ctx.enter_context(nc.sbuf_tensor("w_ba", [P, KC, 16], F32))
        wm = ctx.enter_context(nc.sbuf_tensor("w_mem", [P, 2, KC, MH * P], F32))
        mk = ctx.enter_context(nc.sbuf_tensor("mem_k", [P, 2, MH * P], F32))
        block = ctx.enter_context(nc.Block())

        @block.sync
        def _(sp):
            with nc.allow_non_contiguous_dma(reason="16 columns of w_in"):
                sp.dma_start(wba[:, :, :], x["w_in"].rearrange("(p k) n -> p k n", k=KC)[:, :, BA0:BA0 + 16]).then_inc(s_w[0], 16)
            sp.dma_start(wm[:, 0, :, :], x["w_mem_k"].rearrange("(p k) n -> p k n", k=KC)).then_inc(s_w[1], 16)
            sp.dma_start(wm[:, 1, :, :], x["w_mem_v"].rearrange("(p k) n -> p k n", k=KC)).then_inc(s_w[2], 16)
            for j, (dst, src) in enumerate(((y["mem_k_prompt"], mk), (y["mem_v_prompt"], g.MV))):
                sp.wait_ge(s_cp, 3 + 2 * j)
                sp.dma_start(dst.rearrange("b (m p) h d -> p (b m) (h d)", p=P), src[:, :, :]).then_inc(s_out, 16)
            sp.wait_ge(s_out, 32)

        @block.tensor
        def _(pe):
            pe.wait_ge(s_w[0], 16)
            for h in range(2):
                for k in range(KC):
                    ins = nc.tensor.matmul(g.PS[0:16, h, 0:TH], wba[:, k, :], g.XT[:, k, h * TH:(h + 1) * TH],
                                           start=k == 0, stop=k == KC - 1)
            ins.then_inc(s_mm, 1)
            for j in range(2):
                pe.wait_ge(s_w[1 + j], 16)
                for m in range(2):
                    for k in range(KC):
                        ins = nc.tensor.matmul(g.PS[:, 2 + 2 * j + m, :], g.MT[:, k, m * P:(m + 1) * P], wm[:, j, k, :],
                                               start=k == 0, stop=k == KC - 1)
                    ins.then_inc(s_mm, 1)
            pe.wait_ge(s_cp, 3)
            for h in range(MH):
                for m in range(2):
                    ins = nc.tensor.transpose(g.PS[:, 6 + h // 2, (h % 2) * NM + m * P:(h % 2) * NM + (m + 1) * P],
                                              mk[:, m, h * P:(h + 1) * P], g.ident[:, :])
            ins.then_inc(s_mkt, 1)

        @block.vector
        def _(dve):
            dve.wait_ge(s_mm, 1)
            nc.vector.tensor_copy(g.BA[:, :].rearrange("p (h t) -> p h t", h=2), g.PS[0:16, 0:2, 0:TH]).then_inc(s_cp, 1)
            for j, dst in enumerate((mk, g.MV)):
                for m in range(2):
                    dve.wait_ge(s_mm, 2 + 2 * j + m)
                    nc.vector.tensor_copy(dst[:, m, :], g.PS[:, 2 + 2 * j + m, :]).then_inc(s_cp, 1)
            dve.wait_ge(s_mkt, 1)
            nc.vector.tensor_copy(g.MKT[:, :, :], g.PS[:, 6:8, :].rearrange("p b (h m) -> p (b h) m", m=NM)).then_inc(s_mktc, 1)


def phase_rows(nc, g, x, y):
    s_cw, s_tp, s_cp, s_out = (g.sem(n) for n in
        ("conv_w_loaded", "rows_transposed", "rows_copied", "rows_stored"))
    with ExitStack() as ctx:
        krows = ctx.enter_context(nc.sbuf_tensor("k_rows", [P, NT, SBW], F32))
        crow = ctx.enter_context(nc.sbuf_tensor("conv_rows", [3, 1536], F32))
        cw = ctx.enter_context(nc.sbuf_tensor("conv_w_rows", [4, 1536], F32))
        jobs = []
        for src0, dst in ((CK, krows), (CV, g.VT)):
            for t in range(NT):
                jobs.append(([(j * P, g.PT[:, src0 + j, t * P:(t + 1) * P], P, P) for j in range(4)],
                             dst[:, t, :], lambda b: g.PS[:, b, :]))
        for j in range(3):
            jobs.append(([(i * P, g.PT[:, CG + 4 * j + i, SEQ - 3:SEQ], P, 3) for i in range(4)],
                         crow[:, j * 512:(j + 1) * 512], lambda b: g.PS[0:3, b, :]))
        for j in range(8):
            col = j * 512 if j < 7 else MQ0
            jobs.append(([(i * P, g.PT[:, 4 * j + i, SEQ:T], P, NB) for i in range(4)],
                         g.XS[:, col:col + 512], lambda b: g.PS[0:NB, b, :]))
        jobs.append(([(0, g.BA[:, SEQ:T], 16, NB)], g.XS[:, BA0:BA0 + 16], lambda b: g.PS[0:NB, b, 0:16]))
        jobs.append(([(4 * j, cw[:, j * P:(j + 1) * P], 4, P) for j in range(12)],
                     g.CW[:, :, :], lambda b: g.PS[:, b, 0:48].rearrange("p (c k) -> p c k", k=4)))
        block = ctx.enter_context(nc.Block())

        @block.sync
        def _(sp):
            sp.dma_start(cw[:, :], x["conv_w"]).then_inc(s_cw, 16)
            sp.dma_start(y["conv_sample"][:, 0:2, :], x["state_gdn_conv"][:, 1:3, :]).then_inc(s_out, 16)
            sp.wait_ge(s_cp, 4)
            sp.dma_start(y["sb_k_prompt"].rearrange("b (t p) h d -> p (b t) (h d)", p=P), krows[:, :, :]).then_inc(s_out, 16)
            sp.wait_ge(s_cp, 8)
            sp.dma_start(y["sb_v_prompt"].rearrange("b (t p) h d -> p (b t) (h d)", p=P), g.VT[:, :, :]).then_inc(s_out, 16)
            sp.wait_ge(s_cp, 11)
            sp.dma_start(y["conv_prompt"].rearrange("b r n -> (b r) n"), crow[:, :]).then_inc(s_out, 16)
            sp.wait_ge(s_cp, 19)
            sp.dma_start(y["conv_sample"].rearrange("b r n -> b (r n)")[:, 2 * 1536:3 * 1536], g.XS[:, 1536:3072]).then_inc(s_out, 16)
            sp.dma_start(y["sb_k_sample"].rearrange("b o h d -> b (o h d)"), g.XS[:, 512:1024]).then_inc(s_out, 16)
            sp.dma_start(y["sb_v_sample"].rearrange("b o h d -> b (o h d)"), g.XS[:, 1024:1536]).then_inc(s_out, 16)
            sp.wait_ge(s_out, 16 * 7)

        @block.tensor
        def _(pe):
            for n, (parts, _, _) in enumerate(jobs):
                if n >= 4:
                    pe.wait_ge(s_cp, n - 3)
                if n == len(jobs) - 1:
                    pe.wait_ge(s_cw, 16)
                for col, src, k, m in parts:
                    w = src.shape[-1]
                    ins = nc.tensor.transpose(g.PS[0:w, n % 4, col:col + k], src, g.ident[0:k, 0:k])
                ins.then_inc(s_tp, 1)

        @block.vector
        def _(dve):
            for n, (_, dst, src) in enumerate(jobs):
                dve.wait_ge(s_tp, n + 1)
                nc.vector.tensor_copy(dst, src(n % 4)).then_inc(s_cp, 1)


def phase_sb(nc, g):
    OFF, W = [0, 512, 1024, 896], [512, 384, 256, 128]
    NC_ = 1280
    s_z, s_zs, s_ab, s_lg, s_sp, s_spm, s_cum, s_w, s_a, s_am, s_av, s_ot = (g.sem(n) for n in
        ("sb_z_done", "sb_z_copied", "sb_abs_ready", "sb_log_ready", "sb_softplus_ready", "sb_softplus_masked",
         "sb_cum_done", "sb_w_ready", "sb_a_ready", "sb_a_masked", "sb_av_done", "sb_o_copied"))
    s_al = g.sem("sb_act_link")
    with ExitStack() as ctx:
        zs, sp_, a_ = (ctx.enter_context(nc.sbuf_tensor(n, [P, 2, NC_], F32)) for n in ("sb_zs", "sb_sp", "sb_a"))
        ab = ctx.enter_context(nc.sbuf_tensor("sb_ab", [P, NC_], F32))
        Z = g.PS[:, 0:3, :].rearrange("p b n -> p (b n)")[:, 0:NC_]
        C = g.PS[:, 3:6, :].rearrange("p b n -> p (b n)")[:, 0:NC_]
        block = ctx.enter_context(nc.Block())

        @block.tensor
        def _(pe):
            def scores(h):
                c, r = h // 2, HD * (h % 2)
                if h >= 1:
                    pe.wait_ge(s_zs, h)
                for b in range(4):
                    ins = nc.tensor.matmul(Z[:, OFF[b]:OFF[b] + W[b]], g.PT[r:r + HD, CK + c, b * P:(b + 1) * P],
                                           g.PT[r:r + HD, CQ + c, b * P:SEQ], start=True, stop=True)
                ins.then_inc(s_z, 1)

            def cumulate(h):
                pe.wait_ge(s_spm, 4 * (h + 1))
                if h >= 1:
                    pe.wait_ge(s_w, h)
                for b in (0, 1, 3, 2):
                    for m in range(b, 4):
                        lo = (m - b) * P
                        ins = nc.tensor.matmul(C[:, OFF[b] + lo:OFF[b] + W[b]], (g.TRI if m == b else g.nones)[:, :],
                                               sp_[:, h % 2, OFF[m]:OFF[m] + W[m]], start=m == b, stop=m == 3)
                ins.then_inc(s_cum, 1)

            def values(h):
                c, r = h // 2, HD * (h % 2)
                pe.wait_ge(s_am, 4 * (h + 1))
                if h >= 4 and h % 2 == 0:
                    pe.wait_ge(s_ot, h // 2 - 1)
                for b in range(4):
                    ins = nc.tensor.matmul(g.PS[r:r + HD, 6 + c % 2, b * P:SEQ], g.VT[:, b, h * HD:(h + 1) * HD],
                                           a_[:, h % 2, OFF[b]:OFF[b] + W[b]], start=b == 0, stop=b == 3)
                ins.then_inc(s_av, 1)

            scores(0)
            for s in range(H + 2):
                if s + 1 < H:
                    scores(s + 1)
                if s < H:
                    cumulate(s)
                if s >= 2:
                    values(s - 2)

        @block.scalar
        def _(act):
            link = Link(act, s_al)

            def weights(h):
                act.wait_ge(s_w, h + 1)
                nc.scalar.activation(a_[:, h % 2, :], a_[:, h % 2, :], ACT.Exp).then_inc(s_a, 1)

            exp_ln_table(nc)
            for h in range(H):
                act.wait_ge(s_z, h + 1)
                if h >= 2:
                    act.wait_ge(s_w, h - 1)
                nc.scalar.activation(zs[:, h % 2, :], Z, ACT.Identity, scale=HD ** -0.5,
                                     bias=g.sbb_bc[:, h:h + 1]).then_inc(s_zs, 1)
                act.wait_ge(s_ab, h + 1)
                link(nc.scalar.activation(ab[:, :], ab[:, :], ACT.Exp))
                nc.scalar.activation(ab[:, :], ab[:, :], ACT.Ln, bias=g.one_c).then_inc(s_lg, 1)
                if h >= 1:
                    weights(h - 1)
            weights(H - 1)

        @block.vector
        def _(dve):
            def add(h):
                dve.wait_ge(s_cum, h + 1)
                if h >= 2:
                    dve.wait_ge(s_av, h - 1)
                nc.vector.tensor_tensor(a_[:, h % 2, :], C, zs[:, h % 2, :], ALU.add).then_inc(s_w, 1)

            def copy_out(c):
                dve.wait_ge(s_av, 2 * c + 2)
                nc.vector.tensor_copy(g.OT[:, c, 0:SEQ], g.PS[:, 6 + c % 2, :]).then_inc(s_ot, 1)

            for h in range(H):
                dve.wait_ge(s_zs, h + 1)
                if h >= 1:
                    dve.wait_ge(s_sp, h)
                nc.vector.scalar_tensor_tensor(out=ab[:, :], in0=zs[:, h % 2, :], scalar=-1.0, in1=zs[:, h % 2, :],
                                               op0=ALU.mult, op1=ALU.min).then_inc(s_ab, 1)
                dve.wait_ge(s_lg, h + 1)
                if h >= 2:
                    dve.wait_ge(s_cum, h - 1)
                nc.vector.scalar_tensor_tensor(out=sp_[:, h % 2, :], in0=zs[:, h % 2, :], scalar=0.0, in1=ab[:, :],
                                               op0=ALU.max, op1=ALU.add).then_inc(s_sp, 1)
                if h >= 1:
                    add(h - 1)
                if h >= 4 and h % 2 == 0:
                    copy_out(h // 2 - 2)
            add(H - 1)
            copy_out(2)
            copy_out(3)

        @block.gpsimd
        def _(pool):
            def mask(buf, h, sem):
                for b in range(4):
                    v = buf[:, h % 2, OFF[b]:OFF[b] + P]
                    pool.affine_select(out=v, in_=v, compare_op=ALU.is_gt, fill=0.0, base=0,
                                       pattern=[[1, P]], channel_multiplier=-1).then_inc(sem, 1)

            for h in range(H):
                pool.wait_ge(s_sp, h + 1)
                mask(sp_, h, s_spm)
                if h >= 1:
                    pool.wait_ge(s_a, h)
                    mask(a_, h - 1, s_am)
            pool.wait_ge(s_a, H)
            mask(a_, H - 1, s_am)


def phase_mem(nc, g):
    SC = P ** -0.5
    s_s, s_mx, s_e, s_p, s_pt, s_ptc, s_o, s_oc = (g.sem(n) for n in
        ("mem_s_done", "mem_max_ready", "mem_exp_ready", "mem_p_ready", "mem_pt_done", "mem_pt_copied",
         "mem_o_done", "mem_o_copied"))
    s_dl = g.sem("mem_dve_link")
    with ExitStack() as ctx:
        pr = ctx.enter_context(nc.sbuf_tensor("mem_pr", [P, 2, NT, NM], F32))
        pt = ctx.enter_context(nc.sbuf_tensor("mem_pt", [P, 2, SEQ], F32))
        mx, sm = (ctx.enter_context(nc.sbuf_tensor(n, [P, MH, NT], F32)) for n in ("mem_mx", "mem_sm"))
        block = ctx.enter_context(nc.Block())
        S_ = lambda h: g.PS[:, 2 * (h % 2):2 * (h % 2) + 2, :].rearrange("p b (t m) -> p (b t) m", m=NM)

        @block.tensor
        def _(pe):
            def scores(h):
                if h >= 2:
                    pe.wait_ge(s_e, 4 * (h - 1))
                for t in range(NT):
                    ins = nc.tensor.matmul(S_(h)[:, t, :], g.PT[:, CM + h, t * P:(t + 1) * P], g.MKT[:, h, :],
                                           start=True, stop=True)
                ins.then_inc(s_s, 1)

            scores(0)
            for h in range(MH):
                if h + 1 < MH:
                    scores(h + 1)
                pe.wait_ge(s_p, h + 1)
                if h >= 1:
                    pe.wait_ge(s_ptc, h)
                for m in range(2):
                    for t in range(NT):
                        ins = nc.tensor.transpose(g.PS[:, 4 + m, t * P:(t + 1) * P], pr[:, h % 2, t, m * P:(m + 1) * P],
                                                  g.ident[:, :])
                ins.then_inc(s_pt, 1)
                pe.wait_ge(s_ptc, h + 1)
                if h >= 2:
                    pe.wait_ge(s_oc, h - 1)
                for m in range(2):
                    ins = nc.tensor.matmul(g.PS[:, 6 + h % 2, :], g.MV[:, m, h * P:(h + 1) * P], pt[:, m, :],
                                           start=m == 0, stop=m == 1)
                ins.then_inc(s_o, 1)

        @block.scalar
        def _(act):
            for h in range(MH):
                act.wait_ge(s_mx, h + 1)
                if h >= 2:
                    act.wait_ge(s_pt, h - 1)
                for t in range(NT):
                    nc.scalar.activation(pr[:, h % 2, t, :], S_(h)[:, t, :], ACT.Exp, bias=mx[:, h, t:t + 1],
                                         scale=SC, accum_out=sm[:, h, t:t + 1]).then_inc(s_e, 1)

        @block.vector
        def _(dve):
            link = Link(dve, s_dl)

            def maxima(h):
                dve.wait_ge(s_s, h + 1)
                link(nc.vector.tensor_reduce(mx[:, h, :], S_(h), AX.X, ALU.max))
                nc.vector.tensor_scalar(mx[:, h, :], mx[:, h, :], -SC, None, ALU.mult).then_inc(s_mx, 1)

            maxima(0)
            for h in range(MH):
                dve.wait_ge(s_e, 4 * (h + 1))
                link(nc.vector.reciprocal(sm[:, h, :], sm[:, h, :]))
                nc.vector.tensor_tensor(pr[:, h % 2, :, :], pr[:, h % 2, :, :],
                                        sm[:, h, :].unsqueeze(2).to_broadcast([P, NT, NM]), ALU.mult).then_inc(s_p, 1)
                if h + 1 < MH:
                    maxima(h + 1)
                dve.wait_ge(s_pt, h + 1)
                if h >= 1:
                    dve.wait_ge(s_o, h)
                nc.vector.tensor_copy(pt[:, :, :], g.PS[:, 4:6, :]).then_inc(s_ptc, 1)
                dve.wait_ge(s_o, h + 1)
                nc.vector.tensor_copy(g.OT[:, 8 + h, 0:SEQ], g.PS[:, 6 + h % 2, :]).then_inc(s_oc, 1)


class GateFiller:

    def __init__(self, nc, g, x, name, first, count, bank):
        self.nc, self.g, self.first, self.count, self.bank = nc, g, first, count, bank
        self.w = x["w_in"].rearrange("(p k) n -> p k n", k=KC)
        self.loaded = [g.sem(f"{name}_gate_w{i}_loaded") for i in range(2)]
        self.done, self.copied = g.sem(name + "_gate_done"), g.sem(name + "_gate_copied")
        self.u = self.v = 0

    def load(self, eng):
        for n in range(self.count // 2):
            if n >= 2:
                eng.wait_ge(self.done, 4 * (n - 1))
            c = GT0 + self.first * P + n * 256
            eng.dma_start(self.g.GW[n % 2], self.w[:, :, c:c + 256]).then_inc(self.loaded[n % 2], 16)

    def products(self, pe, n):
        g = self.g
        for _ in range(n):
            u, c, h = self.u, self.u // 2, self.u % 2
            self.u += 1
            if u % 4 == 0:
                pe.wait_ge(self.loaded[c // 2 % 2], 16 * (c // 4 + 1))
            if u >= 2:
                pe.wait_ge(self.copied, u - 1)
            for k in range(KC):
                ins = self.nc.tensor.matmul(g.PS[:, self.bank + h, 0:TH], g.GW[c // 2 % 2][:, k, (c % 2) * P:(c % 2 + 1) * P],
                                            g.XT[:, k, h * TH:(h + 1) * TH], start=k == 0, stop=k == KC - 1)
            ins.then_inc(self.done, 1)

    def copies(self, act, n):
        g = self.g
        for _ in range(n):
            u, c, h = self.v, self.v // 2, self.v % 2
            self.v += 1
            act.wait_ge(self.done, u + 1)
            self.nc.scalar.activation(g.PT[:, GATE[self.first + c], h * TH:(h + 1) * TH], g.PS[:, self.bank + h, 0:TH],
                                      ACT.Copy).then_inc(self.copied, 1)


def phase_gdn_prep(nc, g, x):
    NTH = NT * H
    s_cv, s_si, s_sq, s_ss, s_rs, s_qk, s_tp, s_cp = (g.sem(n) for n in
        ("conv_sum_ready", "silu_ready", "square_ready", "sumsq_done", "rnorm_ready", "qk_normed", "kv_transposed", "kv_copied"))
    s_dl, s_al = g.sem("prep_dve_link"), g.sem("prep_act_link")
    s_bt, s_xa, s_lg, s_g, s_gc, s_gs, s_gt, s_eg, s_beta, s_eA = (g.sem(n) for n in
        ("ba_transposed", "decay_in_ready", "decay_log_ready", "decay_ready", "decay_sums_done", "decay_sums_copied",
         "decay_row_done", "decay_exp_ready", "beta_ready", "exp_a_ready"))
    with ExitStack() as ctx:
        sb = lambda n, s: ctx.enter_context(nc.sbuf_tensor(n, s, F32))
        tmp, sq, rs = sb("conv_tmp", [P, 2, SEQ]), sb("norm_sq", [P, 2, SEQ]), sb("norm_rs", [P, 2, SEQ])
        bt, xa, t1, gg = sb("bt", [P, NT, 16]), sb("decay_xa", [P, NTH]), sb("decay_t1", [P, NTH]), sb("decay_g", [P, NTH])
        tot, ea = sb("decay_tot", [P, NTH]), sb("exp_a", [P, H])
        th = lambda v: v.rearrange("p (t h) -> p t h", h=H)
        src = lambda c: g.PT[:, CG + c, 0:SEQ]
        filler = GateFiller(nc, g, x, "prep", 0, G_PREP, 4)
        block = ctx.enter_context(nc.Block())

        @block.vector
        def _(dve):
            link = Link(dve, s_dl)
            dve.wait_ge(s_bt, 1)
            link(nc.vector.tensor_copy(bt[:, :, :], g.PS[:, 7, 0:64].rearrange("p (t c) -> p t c", c=16)))
            link(nc.vector.tensor_tensor(th(xa[:, :]), bt[:, :, H:2 * H],
                                         g.dt_bc[:, :].unsqueeze(1).to_broadcast([P, NT, H]), ALU.add))
            nc.vector.scalar_tensor_tensor(out=t1[:, :], in0=xa[:, :], scalar=-1.0, in1=xa[:, :],
                                           op0=ALU.mult, op1=ALU.min).then_inc(s_xa, 1)
            dve.wait_ge(s_lg, 1)
            link(nc.vector.scalar_tensor_tensor(out=gg[:, :], in0=xa[:, :], scalar=0.0, in1=t1[:, :],
                                                op0=ALU.max, op1=ALU.add))
            dve.wait_ge(s_eA, 1)
            link(nc.vector.tensor_tensor(th(gg[:, :]), th(gg[:, :]), ea[:, :].unsqueeze(1).to_broadcast([P, NT, H]), ALU.mult))
            nc.vector.tensor_scalar(gg[:, :], gg[:, :], -1.0, None, ALU.mult).then_inc(s_g, 1)
            dve.wait_ge(s_gc, 2)
            nc.vector.tensor_copy(g.GC[:, :], g.PS[:, 7, 64:96]).then_inc(s_gs, 1)
            link(nc.vector.tensor_copy(tot[:, :], g.PS[:, 7, 96:128]))
            link(nc.vector.tensor_tensor(g.TAIL[:, :], tot[:, :], g.PS[:, 7, 64:96], ALU.subtract))
            for half in range(2):
                q = slice(half * HD, (half + 1) * HD)
                nc.vector.tensor_copy(g.EGL[q, :, :], th(tot[q, :])[:, :, half::2]).then_inc(s_gs, 1)
            dve.wait_ge(s_gt, 1)
            nc.vector.tensor_copy(g.GCT[:, :], g.PS[0:NTH, 6, 0:P]).then_inc(s_gs, 1)

            for c in range(12):
                if c >= 2:
                    dve.wait_ge(s_si, c - 1)
                b = tmp[:, c % 2, :]
                link(nc.vector.tensor_scalar(b, src(c), g.CW[:, c, 3:4], None, ALU.mult))
                for k in (2, 1, 0):
                    o = 3 - k
                    ins = nc.vector.scalar_tensor_tensor(out=b[:, o:SEQ], in0=g.PT[:, CG + c, 0:SEQ - o], scalar=g.CW[:, c, k:k + 1],
                                                         in1=b[:, o:SEQ], op0=ALU.mult, op1=ALU.add)
                    if k:
                        link(ins)
                ins.then_inc(s_cv, 1)
            for c in range(8):
                dve.wait_ge(s_rs, c + 1)
                nc.vector.scalar_tensor_tensor(out=src(c), in0=src(c), scalar=HD ** -0.5 if c < 4 else 1.0, in1=rs[:, c % 2, :],
                                               op0=ALU.mult, op1=ALU.mult).then_inc(s_qk, 1)
            for n in range(2 * NT):
                dve.wait_ge(s_tp, n + 1)
                dst = g.VTM if n < NT else g.KTM
                nc.vector.tensor_copy(dst[:, n % NT, :], g.PS[:, 2 + n % 4, :]).then_inc(s_cp, 1)

        @block.scalar
        def _(act):
            link = Link(act, s_al)
            exp_ln_table(nc)
            nc.scalar.activation(ea[:, :], g.A_bc[:, :], ACT.Exp).then_inc(s_eA, 1)
            act.wait_ge(s_xa, 1)
            link(nc.scalar.activation(t1[:, :], t1[:, :], ACT.Exp))
            nc.scalar.activation(t1[:, :], t1[:, :], ACT.Ln, bias=g.one_c).then_inc(s_lg, 1)
            act.wait_ge(s_gs, 4)
            nc.scalar.activation(g.EGC[:, :], g.GC[:, :], ACT.Exp).then_inc(s_eg, 1)
            nc.scalar.activation(g.TAIL[:, :], g.TAIL[:, :], ACT.Exp).then_inc(s_eg, 1)
            nc.scalar.activation(g.EGL[:, :, :], g.EGL[:, :, :], ACT.Exp).then_inc(s_eg, 1)
            nc.scalar.activation(g.BETA[:, :].rearrange("p (t h) -> p t h", h=H), bt[:, :, 0:H], ACT.Sigmoid).then_inc(s_beta, 1)
            for c in range(12):
                act.wait_ge(s_cv, c + 1)
                nc.scalar.activation(src(c), tmp[:, c % 2, :], ACT.Silu).then_inc(s_si, 1)
                if 1 <= c < 2 * G_PREP - 7 + 1:
                    filler.copies(act, 1)
            for c in range(4):
                nc.scalar.activation(g.PT[:, CZ + c, :], g.PT[:, CZ + c, :], ACT.Silu).then_inc(s_beta, 1)
            act.wait_ge(s_si, 12)

            def square(c):
                if c >= 2:
                    act.wait_ge(s_ss, c - 1)
                nc.scalar.activation(sq[:, c % 2, :], src(c), ACT.Square).then_inc(s_sq, 1)

            exp_ln_table(nc)
            square(0)
            for c in range(8):
                if c < 7:
                    square(c + 1)
                act.wait_ge(s_ss, c + 1)
                if c >= 2:
                    act.wait_ge(s_qk, c - 1)
                link(nc.scalar.activation(rs[:, c % 2, :], g.PS[:, c % 2, :], ACT.Ln, bias=g.eps_l2))
                nc.scalar.activation(rs[:, c % 2, :], rs[:, c % 2, :], ACT.Exp, scale=-0.5).then_inc(s_rs, 1)
                if c < 7:
                    filler.copies(act, 1)

        @block.tensor
        def _(pe):
            for t in range(NT):
                ins = nc.tensor.transpose(g.PS[:, 7, t * 16:(t + 1) * 16], g.BA[:, t * P:(t + 1) * P], g.ident[0:16, 0:16])
            ins.then_inc(s_bt, 1)
            pe.wait_ge(s_g, 1)
            nc.tensor.matmul(g.PS[:, 7, 64:96], g.UT[:, :], gg[:, :], start=True, stop=True).then_inc(s_gc, 1)
            nc.tensor.matmul(g.PS[:, 7, 96:128], g.ones[:, :], gg[:, :], start=True, stop=True).then_inc(s_gc, 1)
            pe.wait_ge(s_gs, 1)
            nc.tensor.transpose(g.PS[0:NTH, 6, 0:P], g.GC[:, :], g.ident[:, :]).then_inc(s_gt, 1)
            filler.products(pe, 2 * G_PREP - 7)

            def rows(n):
                pe.wait_ge(s_si, 12) if n < NT else pe.wait_ge(s_qk, 8)
                if n == 2:
                    pe.wait_ge(filler.copied, 2 * G_PREP)
                if n >= 4:
                    pe.wait_ge(s_cp, n - 3)
                c0 = CG + (8 if n < NT else 4)
                t = n % NT
                for j in range(4):
                    ins = nc.tensor.transpose(g.PS[:, 2 + n % 4, j * P:(j + 1) * P], g.PT[:, c0 + j, t * P:(t + 1) * P], g.ident[:, :])
                ins.then_inc(s_tp, 1)

            for c in range(8):
                pe.wait_ge(s_sq, c + 1)
                if c >= 2:
                    pe.wait_ge(s_rs, c - 1)
                nc.tensor.matmul(g.PS[:, c % 2, :], g.bones[:, :], sq[:, c % 2, :], start=True, stop=True).then_inc(s_ss, 1)
                if c < 7:
                    filler.products(pe, 1)
            for n in range(2 * NT):
                rows(n)

        @block.gpsimd
        def _(pool):
            filler.load(pool)


def phase_gdn(nc, g, y):
    names = ("kkqk_done", "diff_ready", "decay_ready", "mt_ready", "qk_ready", "qk_masked", "ms_ready", "ms0_ready",
             "ms0_transposed", "ms0_used", "x_ready", "y_done", "y_copied", "xy_done", "kx_ready", "w_done",
             "w_copied", "vn_done", "vn_ready", "os_done", "ov_done", "sd_done", "s_ready", "o_ready", "osq_ready",
             "orms_ready", "on_ready", "ot_done", "ot_copied", "link", "alink", "stored")
    s = {n: g.sem("gdn_" + n) for n in names}
    LV = 6
    slot = lambda h: (h % 2) * 4 + h // 2
    head_of = lambda sl: 2 * (sl % 4) + sl // 4
    with ExitStack() as ctx:
        sb = lambda n, sh: ctx.enter_context(nc.sbuf_tensor("gdn_" + n, sh, F32))
        E, MT, QK, X, XT, Y = (sb(n, [P, H, P]) for n in ("E", "MT", "QK", "X", "XT", "Y"))
        MS = [sb(f"MS{i}", [P, H, P]) for i in range(2)]
        KE, KTL, VN, O = (sb(n, [P, SBW]) for n in ("KE", "KTL", "VN", "O"))
        NW = sb("NW", [P, 4, P])
        OSQ, ORS, SD = sb("OSQ", [P, SBW]), sb("ORS", [P, H]), sb("SD", [P, 4, HD])
        two = lambda b: g.PS[:, b:b + 2, :].rearrange("p b (h i) -> p (b h) i", i=P)
        heads = lambda v: v.rearrange("p (h e) -> p h e", h=H)
        bc = lambda v, w: v.unsqueeze(2).to_broadcast([v.shape[0], v.shape[1], w])
        mask_bc = lambda m, n=H: m.unsqueeze(1).to_broadcast([P, n, P])
        quarter = lambda b: g.PS[:, b, 0:4 * HD].rearrange("p (c e) -> p c e", e=HD)
        OS, VP = (lambda o: quarter(4 if o else 7)), (lambda o: quarter(5 if o else 6))
        block = ctx.enter_context(nc.Block())

        @block.tensor
        def _(pe):
            def transposes(t):
                pe.wait_ge(s["on_ready"], t + 1)
                for c in range(4):
                    ins = nc.tensor.transpose(g.PS[:, 7, c * P:(c + 1) * P], O[:, c * P:(c + 1) * P], g.ident[:, :])
                ins.then_inc(s["ot_done"], 1)

            for t in range(NT):
                cols = slice(t * P, (t + 1) * P)
                L = t * (2 * LV + 2)
                if t:
                    pe.wait_ge(s["x_ready"], L)
                    pe.wait_ge(s["s_ready"], 2 * t)
                    pe.wait_ge(s["o_ready"], 2 * t - 1)
                for h in range(H):
                    c, r = h // 2, HD * (h % 2)
                    k = g.PT[r:r + HD, CG + 4 + c, cols]
                    nc.tensor.matmul(two(0)[:, slot(h), :], k, k, start=True, stop=True)
                    nc.tensor.matmul(two(2)[:, slot(h), :], k, g.PT[r:r + HD, CG + c, cols], start=True, stop=True)
                    row = t * H + h
                    ins = nc.tensor.matmul(two(4)[:, slot(h), :], g.ident[0:NT * H, row:row + 1].to_broadcast([NT * H, P]),
                                           g.GCT[:, :], start=True, stop=True)
                ins.then_inc(s["kkqk_done"], 1)
                if t:
                    transposes(t - 1)
                pe.wait_ge(s["ms0_ready"], t + 1)
                for h in range(H):
                    ins = nc.tensor.transpose(two(0)[:, h, :], MS[1][:, h, :], g.ident[:, :])
                ins.then_inc(s["ms0_transposed"], 1)
                with pe.Fori(0, LV // 2) as i:
                    for p in range(2):
                        pe.wait_ge(s["ms_ready"], i * 2 + (t * LV + p + 1))
                        for a in range(2):
                            pe.wait_ge(s["x_ready"], i * 4 + (L + 2 * p + a + 1))
                            for h in range(4 * a, 4 * a + 4):
                                ins = nc.tensor.matmul(two(0)[:, h, :], MS[p][:, h, :], X[:, h, :], start=True, stop=True)
                            ins.then_inc(s["y_done"], 1)
                        for a in range(2):
                            pe.wait_ge(s["y_copied"], i * 4 + (2 * LV * t + 2 * p + a + 4))
                            for h in range(4 * a, 4 * a + 4):
                                nc.tensor.matmul(two(2)[:, h, :], XT[:, h, :], Y[:, h, :], start=True, stop=True)
                            for h in range(4 * a, 4 * a + 4):
                                ins = nc.tensor.matmul(two(4)[:, h, :], Y[:, h, :], XT[:, h, :], start=True, stop=True)
                            ins.then_inc(s["xy_done"], 1)
                pe.wait_ge(s["kx_ready"], 2 * t + 1)
                for a in range(2):
                    pe.wait_ge(s["x_ready"], L + 2 * LV + a + 1)
                    for h in range(4 * a, 4 * a + 4):
                        c = h % 4
                        ins = nc.tensor.matmul(two(0)[:, h, :], KE[:, c * P:(c + 1) * P], XT[:, h, :], start=True, stop=True)
                ins.then_inc(s["w_done"], 1)
                if t:
                    pe.wait_ge(s["s_ready"], 2 * t)
                    pe.wait_ge(s["ot_copied"], t)
                pe.wait_ge(s["qk_masked"], t + 1)
                for h in range(H):
                    c, r = h // 2, HD * (h % 2)
                    ins = nc.tensor.matmul(OS(h % 2)[:, c, :], g.PT[r:r + HD, CG + c, cols], g.S[r:r + HD, c, :],
                                           start=True, stop=True)
                ins.then_inc(s["os_done"], 1)
                pe.wait_ge(s["w_copied"], 2 * t + 2)
                for h in range(H):
                    c, r = h // 2, HD * (h % 2)
                    nc.tensor.matmul(VP(h % 2)[:, c, :], XT[:, slot(h), :], g.VTM[:, t, h * HD:(h + 1) * HD], start=True, stop=False)
                    ins = nc.tensor.matmul(VP(h % 2)[:, c, :], NW[r:r + HD, c, :], g.S[r:r + HD, c, :],
                                           start=False, stop=True)
                ins.then_inc(s["vn_done"], 1)
                pe.wait_ge(s["vn_ready"], 2 * t + 2)
                pe.wait_ge(s["kx_ready"], 2 * t + 2)
                for c in range(4):
                    ins = nc.tensor.matmul(g.PS[:, 3, c * P:(c + 1) * P], KTL[:, c * P:(c + 1) * P], VN[:, c * P:(c + 1) * P],
                                           start=True, stop=True)
                ins.then_inc(s["sd_done"], 1)
                for h in range(H):
                    ins = nc.tensor.matmul(g.PS[:, 2, h * HD:(h + 1) * HD], QK[:, slot(h), :], VN[:, h * HD:(h + 1) * HD], start=True, stop=True)
                ins.then_inc(s["ov_done"], 1)
            transposes(NT - 1)

        @block.vector
        def _(dve):
            link = Link(dve, s["link"])
            for t in range(NT):
                st = slice(t * H, (t + 1) * H)
                L = t * (2 * LV + 2)
                dve.wait_ge(s["kkqk_done"], t + 1)
                for sl in range(H):
                    h = head_of(sl)
                    ins = nc.vector.tensor_scalar(E[:, sl, :], two(4)[:, sl, :], g.GC[:, t * H + h:t * H + h + 1], 0.0,
                                                  ALU.subtract, ALU.min)
                ins.then_inc(s["diff_ready"], 1)
                dve.wait_ge(s["decay_ready"], t + 1)
                for sl in range(H):
                    h = head_of(sl)
                    ins = nc.vector.scalar_tensor_tensor(out=MT[:, sl, :], in0=two(0)[:, sl, :], scalar=g.BETA[:, t * H + h:t * H + h + 1],
                                                         in1=E[:, sl, :], op0=ALU.mult, op1=ALU.mult)
                ins.then_inc(s["mt_ready"], 1)
                dve.wait_ge(s["mt_ready"], t + 1)
                nc.vector.tensor_tensor(MS[1][:, :, :], MT[:, :, :], mask_bc(g.LM[:, 0, :]), ALU.mult).then_inc(s["ms0_ready"], 1)
                nc.vector.tensor_tensor(QK[:, :, :], two(2), E[:, :, :], ALU.mult).then_inc(s["qk_ready"], 1)
                dve.wait_ge(s["ms0_ready"], t + 1)
                nc.vector.tensor_tensor(XT[:, :, :], mask_bc(g.ident[:, :]), MS[1][:, :, :], ALU.subtract).then_inc(s["ms0_used"], 1)
                dve.wait_ge(s["ms0_transposed"], t + 1)
                for a in range(2):
                    q = slice(4 * a, 4 * a + 4)
                    nc.vector.tensor_tensor(X[:, q, :], mask_bc(g.ident[:, :], 4), two(0)[:, q, :], ALU.subtract).then_inc(s["x_ready"], 1)
                with dve.Fori(0, LV // 2) as i:
                    for p in range(2):
                        for a in range(2):
                            q = slice(4 * a, 4 * a + 4)
                            dve.wait_ge(s["xy_done"], i * 4 + (2 * LV * t + 2 * p + a + 1))
                            nc.vector.tensor_tensor(XT[:, q, :], XT[:, q, :], two(4)[:, q, :], ALU.subtract)
                            nc.vector.tensor_tensor(X[:, q, :], X[:, q, :], two(2)[:, q, :], ALU.subtract).then_inc(s["x_ready"], 1)
                dve.wait_ge(s["w_done"], t + 1)
                for half in range(2):
                    q = slice(half * HD, (half + 1) * HD)
                    nc.vector.tensor_scalar(NW[q, :, :], two(0)[q, 4 * half:4 * half + 4, :], -1.0, None, ALU.mult).then_inc(s["w_copied"], 1)
                dve.wait_ge(s["vn_done"], t + 1)
                for o in range(2):
                    nc.vector.tensor_tensor(heads(VN[:, :])[:, o::2, :], VP(o), bc(g.BETA[:, st][:, o::2], HD), ALU.mult).then_inc(s["vn_ready"], 1)
                dve.wait_ge(s["os_done"], t + 1)
                link(nc.vector.tensor_tensor(SD[:, :, :], g.S[:, :, :], bc(g.EGL[:, t, :], HD), ALU.mult))
                dve.wait_ge(s["sd_done"], t + 1)
                for half in range(2):
                    q = slice(half * HD, (half + 1) * HD)
                    nc.vector.tensor_tensor(g.S[q, :, :], SD[q, :, :],
                                            g.PS[q, 3, :].rearrange("p (c e) -> p c e", e=P)[:, :, half * HD:(half + 1) * HD],
                                            ALU.add).then_inc(s["s_ready"], 1)
                if t:
                    dve.wait_ge(s["ot_done"], t)
                for o in range(2):
                    link(nc.vector.tensor_tensor(heads(O[:, :])[:, o::2, :], OS(o), bc(g.EGC[:, st][:, o::2], HD), ALU.mult))
                dve.wait_ge(s["ov_done"], t + 1)
                nc.vector.tensor_tensor(O[:, :], O[:, :], g.PS[:, 2, :], ALU.add).then_inc(s["o_ready"], 1)
                dve.wait_ge(s["osq_ready"], t + 1)
                nc.vector.tensor_reduce(ORS[:, :], heads(OSQ[:, :]), AX.X, ALU.add).then_inc(s["o_ready"], 1)
                dve.wait_ge(s["orms_ready"], t + 1)
                nc.vector.tensor_tensor(heads(O[:, :]), heads(O[:, :]), bc(ORS[:, :], HD), ALU.mult).then_inc(s["on_ready"], 1)
                dve.wait_ge(s["ot_done"], t + 1)
                nc.vector.scalar_tensor_tensor(out=g.OT[:, 4:8, t * P:(t + 1) * P], in0=g.PS[:, 7, :].rearrange("p (c i) -> p c i", c=4),
                                               scalar=g.nw_col[:, 0:1], in1=g.PT[:, CZ:CZ + 4, t * P:(t + 1) * P],
                                               op0=ALU.mult, op1=ALU.mult).then_inc(s["ot_copied"], 1)

        @block.scalar
        def _(act):
            link = Link(act, s["alink"])
            exp_ln_table(nc)
            act.sem_inc(s["y_copied"], 3)
            for t in range(NT):
                act.wait_ge(s["diff_ready"], t + 1)
                nc.scalar.activation(E[:, :, :], E[:, :, :], ACT.Exp).then_inc(s["decay_ready"], 1)
                with act.Fori(0, LV // 2) as i:
                    for n in range(4):
                        act.wait_ge(s["y_done"], i * 4 + (2 * LV * t + n + 1))
                        q = slice(4 * (n % 2), 4 * (n % 2) + 4)
                        nc.scalar.activation(Y[:, q, :], two(0)[:, q, :], ACT.Copy).then_inc(s["y_copied"], 1)
                act.wait_ge(s["o_ready"], 2 * t + 1)
                nc.scalar.activation(OSQ[:, :], O[:, :], ACT.Square).then_inc(s["osq_ready"], 1)
                act.wait_ge(s["o_ready"], 2 * t + 2)
                link(nc.scalar.activation(ORS[:, :], ORS[:, :], ACT.Ln, bias=g.eps_l2, scale=1.0 / HD))
                nc.scalar.activation(ORS[:, :], ORS[:, :], ACT.Exp, scale=-0.5).then_inc(s["orms_ready"], 1)

        @block.gpsimd
        def _(pool):
            for t in range(NT):
                st = slice(t * H, (t + 1) * H)
                if t:
                    pool.wait_ge(s["w_done"], t)
                    pool.wait_ge(s["sd_done"], t)
                pool.tensor_tensor(heads(KE[:, :]), heads(g.KTM[:, t, :]), bc(g.EGC[:, st], HD), ALU.mult).then_inc(s["kx_ready"], 1)
                pool.tensor_tensor(heads(KTL[:, :]), heads(g.KTM[:, t, :]), bc(g.TAIL[:, st], HD), ALU.mult).then_inc(s["kx_ready"], 1)
                pool.wait_ge(s["mt_ready"], t + 1)
                with pool.Fori(0, LV // 2) as i:
                    for p in range(2):
                        if p:
                            pool.wait_ge(s["ms0_transposed"], t + 1)
                            pool.wait_ge(s["ms0_used"], t + 1)
                        pool.wait_ge(s["y_copied"], i * 4 + (2 * LV * t + 2 * p + 1))
                        pool.tensor_tensor(MS[p][:, :, :], MT[:, :, :],
                                           g.LM[:, bass.ds(i * 2 + p + 1, 1), :].to_broadcast([P, H, P]), ALU.mult).then_inc(s["ms_ready"], 1)
                pool.wait_ge(s["qk_ready"], t + 1)
                if t:
                    pool.wait_ge(s["ov_done"], t)
                pool.tensor_tensor(QK[:, :, :], QK[:, :, :], mask_bc(g.UT[:, :]), ALU.mult).then_inc(s["qk_masked"], 1)

        @block.sync
        def _(sp):
            sp.wait_ge(s["s_ready"], 2 * NT)
            for half in range(2):
                sp.dma_start(y["state_prompt"][0, half::2, :, :].rearrange("c d e -> d c e"),
                             g.S[half * HD:(half + 1) * HD, :, :]).then_inc(s["stored"], 16)
            sp.wait_ge(s["stored"], 32)


def phase_sample(nc, g, x, y):
    SC = P ** -0.5
    names = ("table_loaded", "state_loaded", "conv_loaded", "qb_done", "mqb_done", "mem_scores", "sb_w_in", "sb_lg",
             "sb_sp", "sb_cum", "sb_w", "sb_a", "mem_t", "mem_max", "mem_exp", "mem_p", "mem_pt", "mem_ptc",
             "conv_t", "conv_sum", "conv_r", "n_sq", "n_ss", "n_rs", "qkv_ready", "d_in", "d_lg", "d_g",
             "gates_ready", "z_silu", "sc_out", "sc_in", "s_new", "o_ready", "o_sq", "o_ss", "o_rs", "on_ready",
             "o_t", "nw_loaded", "stored", "link", "alink", "prod", "v_used")
    s = {n: g.sem("smp_" + n) for n in names}
    s_kv = [g.sem(f"smp_kv{i}_loaded") for i in range(4)]
    BH = NB * H
    with ExitStack() as ctx:
        sb = lambda n, sh, d=F32: ctx.enter_context(nc.sbuf_tensor("smp_" + n, sh, d))
        scr = nc.dram_tensor("scratch_rows", [4, NB, H, HD], F32)
        scr2 = nc.dram_tensor("scratch_gates", [2, NB, H], F32)
        KV = [g.PT[:, c:c + PG, 0:SBW] for c in (0, 4, 12, 24)]
        tab = sb("table", [1, NB * PG], I32)
        prod = sb("prod", [P, PG * SBW])
        zd, sd = sb("zd", [P, PG, NB, H]), sb("sd", [P, 2, NB, MH])
        t1, spd, ad = sb("t1", [P, PG * NB * H]), sb("spd", [P, PG * NB * H]), sb("ad", [P, PG, NB, H])
        pm, pmt = sb("pm", [NB * MH, NM]), sb("pmt", [P, 2, NB * MH])
        st1, st2 = sb("st1", [NB * MH, 1]), sb("st2", [NB * MH, 1])
        crow = sb("crow", [3 * NB, 1536])
        cf, ct = sb("cf", [P, 12, NB]), sb("ct", [P, 12, NB])
        xc, sqr, nrm = sb("xc", [NB, 4 * SBW]), sb("sqr", [NB, 2 * SBW]), sb("nrm", [NB, 2 * H])
        da, dt, gates = sb("da", [NB, H]), sb("dt", [NB, H]), sb("gates", [NB, 2, H])
        S0 = sb("S0", [BH, HD, HD])
        rows, gt = sb("rows", [BH, 4, HD]), sb("gt", [BH, 2])
        ks, vn, o2, osq, ors = (sb(n, [BH, w]) for n, w in (("ks", HD), ("vn", HD), ("o2", 2 * HD), ("osq", HD), ("ors", 1)))
        nw = sb("nw", [BH, HD])
        filler = GateFiller(nc, g, x, "smp", G_PREP, G_SMP, 2)
        pr = prod[0:BH, 0:HD * HD // 2]
        flat = lambda v: v.rearrange("p a b c -> p (a b c)")
        block = ctx.enter_context(nc.Block())

        @block.sync
        def _(sp):
            sp.dma_start(tab[:, :], x["page_table"].rearrange("(o b) n -> o (b n)", o=1)).then_inc(s["table_loaded"], 16)
            sp.dma_start(crow[:, :], x["state_gdn_conv"].rearrange("b k n -> (b k) n")).then_inc(s["conv_loaded"], 16)
            sp.dma_start(S0[:, :, :], x["state_gdn"].rearrange("b h d e -> (b h) d e")).then_inc(s["state_loaded"], 16)
            sp.dma_start(nw[:, :], x["gdn_norm_w"].partition_broadcast(BH)).then_inc(s["nw_loaded"], 16)
            sp.wait_ge(s["table_loaded"], 16)
            for kind, cache in ((0, x["cache_sb_k"]), (1, x["cache_sb_v"])):
                for b in range(NB):
                    n = kind * NB + b
                    if n >= 4:
                        sp.wait_ge(s["prod"], n - 3) if n - 4 < NB else sp.wait_ge(s["v_used"], n - 4 - NB + 1)
                    for p in range(PG):
                        page = sp.value_load(tab[0:1, b * PG + p:b * PG + p + 1], min_val=0, max_val=N_POOL - 1)
                        sp.dma_start(KV[n % 4][:, p, :], cache[bass.ds(page, 1)].rearrange("a t h d -> t (a h d)")).then_inc(s_kv[n % 4], 16)
            for kind, cache in ((2, x["cache_mem_k"]), (3, x["cache_mem_v"])):
                for b in range(NB):
                    n = kind * NB + b
                    m = n - 4
                    sp.wait_ge(s["v_used"], m - NB + 1) if m < 2 * NB else (sp.wait_ge(s["prod"], m - NB + 1) if m < 3 * NB else sp.wait_ge(s["v_used"], m - 2 * NB + 1))
                    sp.dma_start(KV[n % 4][:, 0:2, :], cache[b].rearrange("(m p) h d -> p m (h d)", p=P)).then_inc(s_kv[n % 4], 16)
            sp.wait_ge(s["s_new"], 2)
            sp.dma_start(y["state_sample"].rearrange("b h d e -> (b h) d e"), S0[:, :, :]).then_inc(s["stored"], 16)
            sp.wait_ge(s["stored"], 16)

        def kv_total(n):
            total = 0
            for m in range(n % 4, n + 1, 4):
                total += 16 * (PG if m < 2 * NB else 1)
            return total

        @block.gpsimd
        def _(pool):
            filler.load(pool)

        @block.tensor
        def _(pe):
            pe.wait_ge(s["conv_loaded"], 16)
            for c in range(12):
                ins = nc.tensor.transpose(g.PS[:, 5, c * 24:(c + 1) * 24], crow[:, c * P:(c + 1) * P], g.ident[0:24, 0:24])
            ins.then_inc(s["conv_t"], 1)
            for b in range(NB):
                if b >= 2:
                    pe.wait_ge(s["prod"], b - 1)
                nc.tensor.matmul(g.PS[:, b % 2, :], g.ident[0:NB, b:b + 1].to_broadcast([NB, P]), g.XS[:, 0:SBW],
                                 start=True, stop=True).then_inc(s["qb_done"], 1)
                if b == 0:
                    pe.wait_ge(s["conv_sum"], 1)
                    for c in range(12):
                        ins = nc.tensor.transpose(g.PS[0:NB, 2 + c // 4, (c % 4) * P:(c % 4 + 1) * P], cf[:, c, :], g.ident[:, :])
                    ins.then_inc(s["conv_r"], 1)
                else:
                    if b == 1:
                        pe.wait_ge(s["z_silu"], 1)
                    filler.products(pe, 1)
            filler.products(pe, 1)
            pe.wait_ge(s["sb_sp"], 1)
            for p in range(PG):
                for m in range(p, PG):
                    ins = nc.tensor.matmul(g.PS[:, 5, p * 64:(p + 1) * 64], (g.TRI if m == p else g.nones)[:, :],
                                           spd[:, m * 64:(m + 1) * 64], start=m == p, stop=m == PG - 1)
            ins.then_inc(s["sb_cum"], 1)
            filler.products(pe, 1)
            pe.wait_ge(s["sb_a"], 1)
            for b in range(NB):
                n = NB + b
                pe.wait_ge(s_kv[n % 4], kv_total(n))
                for c in range(4):
                    for p in range(PG):
                        col = (b * 4 + c) * 2
                        ins = nc.tensor.matmul(g.PS[:, 6, col:col + 2], KV[n % 4][:, p, c * P:(c + 1) * P], ad[:, p, b, 2 * c:2 * c + 2],
                                               start=p == 0, stop=p == PG - 1)
                ins.then_inc(s["v_used"], 1)
            filler.products(pe, 3)
            pe.wait_ge(s["on_ready"], 2)
            nc.tensor.transpose(g.PS[:, 4, 0:BH], o2[:, :], g.ident[0:BH, 0:BH]).then_inc(s["o_t"], 1)
            for b in range(NB):
                if b >= 2:
                    pe.wait_ge(s["prod"], NB + b - 1)
                else:
                    pe.wait_ge(s["prod"], NB)
                nc.tensor.matmul(g.PS[:, b % 2, :], g.ident[0:NB, b:b + 1].to_broadcast([NB, P]), g.XS[:, MQ0:MQ0 + SBW],
                                 start=True, stop=True).then_inc(s["mqb_done"], 1)
                if b % 4 == 3:
                    filler.products(pe, 1)
            pe.wait_ge(s["mem_scores"], 1)
            for m in range(2):
                ins = nc.tensor.transpose(g.PS[0:NB * MH, 7, m * P:(m + 1) * P], sd[:, m, :, :].rearrange("p b h -> p (b h)"), g.ident[:, :])
            ins.then_inc(s["mem_t"], 1)
            filler.products(pe, 1)
            pe.wait_ge(s["mem_p"], 1)
            for m in range(2):
                ins = nc.tensor.transpose(g.PS[:, 5, m * 32:(m + 1) * 32], pm[:, m * P:(m + 1) * P], g.ident[0:32, 0:32])
            ins.then_inc(s["mem_pt"], 1)
            filler.products(pe, 1)
            pe.wait_ge(s["mem_ptc"], 1)
            for b in range(NB):
                n = 3 * NB + b
                pe.wait_ge(s_kv[n % 4], kv_total(n))
                for h in range(MH):
                    for m in range(2):
                        ins = nc.tensor.matmul(g.PS[:, 7, 256 + h * NB + b:256 + h * NB + b + 1], KV[n % 4][:, m, h * P:(h + 1) * P],
                                               pmt[:, m, b * MH + h:b * MH + h + 1], start=m == 0, stop=m == 1)
                ins.then_inc(s["v_used"], 1)

        @block.vector
        def _(dve):
            link = Link(dve, s["link"])
            dve.wait_ge(s["conv_t"], 1)
            old = g.PS[:, 5, 0:288].rearrange("p (c b k) -> p c b k", c=12, k=3)
            tap = lambda k: g.CW[:, :, k:k + 1].to_broadcast([P, 12, NB])
            link(nc.vector.tensor_tensor(cf[:, :, :], g.PT[:, CG:CG + 12, SEQ:T], tap(3), ALU.mult))
            for k in range(3):
                link(nc.vector.tensor_tensor(ct[:, :, :], old[:, :, :, k], tap(k), ALU.mult))
                ins = nc.vector.tensor_tensor(cf[:, :, :], cf[:, :, :], ct[:, :, :], ALU.add)
                if k < 2:
                    link(ins)
            ins.then_inc(s["conv_sum"], 1)
            link(nc.vector.tensor_tensor(da[:, :], g.XS[:, BA0 + H:BA0 + 2 * H], g.dt_bc[0:NB, :], ALU.add))
            nc.vector.scalar_tensor_tensor(out=dt[:, :], in0=da[:, :], scalar=-1.0, in1=da[:, :], op0=ALU.mult, op1=ALU.min).then_inc(s["d_in"], 1)
            dve.wait_ge(s["d_lg"], 2)
            link(nc.vector.scalar_tensor_tensor(out=dt[:, :], in0=da[:, :], scalar=0.0, in1=dt[:, :], op0=ALU.max, op1=ALU.add))
            nc.vector.scalar_tensor_tensor(out=dt[:, :], in0=dt[:, :], scalar=-1.0, in1=nrm[:, 0:H], op0=ALU.mult, op1=ALU.mult).then_inc(s["d_g"], 1)

            for b in range(NB):
                dve.wait_ge(s_kv[b % 4], kv_total(b))
                dve.wait_ge(s["qb_done"], b + 1)
                pv = prod[:, :].rearrange("p (g n) -> p g n", g=PG)
                nc.vector.tensor_tensor(pv, KV[b % 4], g.PS[:, b % 2, :].unsqueeze(1).to_broadcast([P, PG, SBW]), ALU.mult).then_inc(s["prod"], 1)
                dve.wait_ge(s["prod"], b + 1)
                link(nc.vector.tensor_reduce(zd[:, :, b, :], pv.rearrange("p g (h d) -> p g h d", d=HD), AX.X, ALU.add))
                if b == 1:
                    dve.wait_ge(s["n_sq"], 1)
                    nc.vector.tensor_reduce(nrm[:, :], sqr[:, :].rearrange("p (h d) -> p h d", d=HD), AX.X, ALU.add).then_inc(s["n_ss"], 1)
                if b == 2:
                    dve.wait_ge(s["n_rs"], 1)
                    v = xc[:, 0:2 * SBW].rearrange("p (h d) -> p h d", d=HD)
                    link(nc.vector.tensor_tensor(v, v, nrm[:, :].unsqueeze(2).to_broadcast([NB, 2 * H, HD]), ALU.mult))
                    nc.vector.tensor_scalar(xc[:, 0:SBW], xc[:, 0:SBW], HD ** -0.5, None, ALU.mult).then_inc(s["qkv_ready"], 3)
            link(nc.vector.scalar_tensor_tensor(out=zd[:, :, :, :].rearrange("p g b h -> p (g b) h"),
                                                in0=zd[:, :, :, :].rearrange("p g b h -> p (g b) h"), scalar=HD ** -0.5,
                                                in1=g.sbb_bc[:, :].unsqueeze(1).to_broadcast([P, PG * NB, H]), op0=ALU.mult, op1=ALU.add))
            nc.vector.scalar_tensor_tensor(out=t1[:, :], in0=flat(zd[:, :, :, :]), scalar=-1.0, in1=flat(zd[:, :, :, :]),
                                           op0=ALU.mult, op1=ALU.min).then_inc(s["sb_w_in"], 1)
            dve.wait_ge(s["sb_lg"], 1)
            nc.vector.scalar_tensor_tensor(out=spd[:, :], in0=flat(zd[:, :, :, :]), scalar=0.0, in1=t1[:, :],
                                           op0=ALU.max, op1=ALU.add).then_inc(s["sb_sp"], 1)

            def delta(part):
                kb = lambda q: rows[:, 1, q].unsqueeze(2).to_broadcast([BH, HD // 2, HD])
                qb = lambda q: rows[:, 0, q].unsqueeze(2).to_broadcast([BH, HD // 2, HD])
                prv = pr.rearrange("p (d e) -> p d e", e=HD)
                halves = [slice(0, HD // 2), slice(HD // 2, HD)]
                if part == 0:
                    dve.wait_ge(s["state_loaded"], 16)
                    dve.wait_ge(s["sc_in"], 16 * 6)
                    for i, q in enumerate(halves):
                        link(nc.vector.tensor_tensor(prv, S0[:, q, :], kb(q), ALU.mult))
                        link(nc.vector.tensor_reduce(ks[:, :] if i == 0 else vn[:, :], prv.rearrange("p d e -> p e d"), AX.X, ALU.add))
                    link(nc.vector.tensor_tensor(ks[:, :], ks[:, :], vn[:, :], ALU.add))
                    link(nc.vector.tensor_scalar(ks[:, :], ks[:, :], gt[:, 1:2], None, ALU.mult))
                    link(nc.vector.tensor_tensor(ks[:, :], rows[:, 2, :], ks[:, :], ALU.subtract))
                    link(nc.vector.tensor_scalar(vn[:, :], ks[:, :], gt[:, 0:1], None, ALU.mult))
                    for i, q in enumerate(halves):
                        link(nc.vector.tensor_tensor(prv, vn[:, :].unsqueeze(1).to_broadcast([BH, HD // 2, HD]), kb(q), ALU.mult))
                        nc.vector.scalar_tensor_tensor(out=S0[:, q, :], in0=S0[:, q, :], scalar=gt[:, 1:2], in1=prv,
                                                       op0=ALU.mult, op1=ALU.add).then_inc(s["s_new"], 1)
                        dve.wait_ge(s["s_new"], i + 1)
                else:
                    for i, q in enumerate(halves):
                        link(nc.vector.tensor_tensor(prv, S0[:, q, :], qb(q), ALU.mult))
                        link(nc.vector.tensor_reduce(ks[:, :] if i == 0 else vn[:, :], prv.rearrange("p d e -> p e d"), AX.X, ALU.add))
                    nc.vector.tensor_tensor(o2[:, 0:HD], ks[:, :], vn[:, :], ALU.add).then_inc(s["o_ready"], 1)
                    dve.wait_ge(s["o_sq"], 1)
                    nc.vector.tensor_reduce(ors[:, :], osq[:, :], AX.X, ALU.add).then_inc(s["o_ss"], 1)
                    dve.wait_ge(s["o_rs"], 1)
                    dve.wait_ge(s["nw_loaded"], 16)
                    link(nc.vector.tensor_scalar(o2[:, 0:HD], o2[:, 0:HD], ors[:, 0:1], None, ALU.mult))
                    link(nc.vector.tensor_tensor(o2[:, 0:HD], o2[:, 0:HD], nw[:, :], ALU.mult))
                    nc.vector.tensor_tensor(o2[:, 0:HD], o2[:, 0:HD], rows[:, 3, :], ALU.mult).then_inc(s["on_ready"], 1)
                    dve.wait_ge(s["on_ready"], 1)
                    nc.vector.tensor_copy(o2[:, HD:2 * HD], o2[:, 0:HD]).then_inc(s["on_ready"], 1)

            dve.wait_ge(s["sb_cum"], 1)
            nc.vector.tensor_tensor(flat(ad[:, :, :, :]), g.PS[:, 5, 0:256], flat(zd[:, :, :, :]), ALU.add).then_inc(s["sb_w"], 1)
            delta(0)
            delta(1)
            dve.wait_ge(s["v_used"], NB)
            o = g.PS[:, 6, 0:64].rearrange("p (b c e) -> p c b e", b=NB, c=4)
            for half in range(2):
                q = slice(half * HD, (half + 1) * HD)
                nc.vector.tensor_copy(g.OT[q, 0:4, SEQ:T], o[q, :, :, half])
            for b in range(NB):
                n = 2 * NB + b
                dve.wait_ge(s_kv[n % 4], kv_total(n))
                dve.wait_ge(s["mqb_done"], b + 1)
                pv = prod[:, 0:2 * SBW].rearrange("p (g n) -> p g n", g=2)
                nc.vector.tensor_tensor(pv, KV[n % 4][:, 0:2, :], g.PS[:, b % 2, :].unsqueeze(1).to_broadcast([P, 2, SBW]), ALU.mult).then_inc(s["prod"], 1)
                dve.wait_ge(s["prod"], NB + b + 1)
                ins = nc.vector.tensor_reduce(sd[:, :, b, :], pv.rearrange("p g (h d) -> p g h d", d=P), AX.X, ALU.add)
                if b < NB - 1:
                    link(ins)
            ins.then_inc(s["mem_scores"], 1)
            dve.wait_ge(s["mem_t"], 1)
            link(nc.vector.tensor_reduce(st1[:, :], g.PS[0:32, 7, 0:NM], AX.X, ALU.max))
            nc.vector.tensor_scalar(st1[:, :], st1[:, :], -SC, None, ALU.mult).then_inc(s["mem_max"], 1)
            dve.wait_ge(s["mem_exp"], 1)
            link(nc.vector.reciprocal(st2[:, :], st2[:, :]))
            nc.vector.tensor_scalar(pm[:, :], pm[:, :], st2[:, 0:1], None, ALU.mult).then_inc(s["mem_p"], 1)
            dve.wait_ge(s["mem_pt"], 1)
            nc.vector.tensor_copy(pmt[:, :, :], g.PS[:, 5, 0:64].rearrange("p (m j) -> p m j", m=2)).then_inc(s["mem_ptc"], 1)
            dve.wait_ge(s["v_used"], 2 * NB)
            nc.vector.tensor_copy(g.OT[:, 8:12, SEQ:T], g.PS[:, 7, 256:288].rearrange("p (h b) -> p h b", h=MH))
            dve.wait_ge(s["o_t"], 1)
            ot = g.PS[:, 4, 0:BH].rearrange("p (b h) -> p h b", b=NB)
            for half in range(2):
                q = slice(half * HD, (half + 1) * HD)
                nc.vector.tensor_copy(g.OT[q, 4:8, SEQ:T], ot[q, half::2, :])

        @block.scalar
        def _(act):
            link = Link(act, s["alink"])
            exp_ln_table(nc)
            nc.scalar.activation(nrm[:, 0:H], g.A_bc[0:NB, :], ACT.Exp).then_inc(s["d_lg"], 1)
            act.wait_ge(s["d_in"], 1)
            link(nc.scalar.activation(dt[:, :], dt[:, :], ACT.Exp))
            nc.scalar.activation(dt[:, :], dt[:, :], ACT.Ln, bias=g.one_c[0:NB]).then_inc(s["d_lg"], 1)
            act.wait_ge(s["d_g"], 1)
            nc.scalar.activation(gates[:, 1, :], dt[:, :], ACT.Exp).then_inc(s["gates_ready"], 1)
            nc.scalar.activation(gates[:, 0, :], g.XS[:, BA0:BA0 + H], ACT.Sigmoid).then_inc(s["gates_ready"], 1)
            act.wait_ge(s["conv_r"], 1)
            link(nc.scalar.activation(xc[:, 0:3 * SBW], g.PS[0:NB, 2:5, :].rearrange("p b n -> p (b n)"), ACT.Silu))
            nc.scalar.activation(xc[:, 3 * SBW:4 * SBW], g.XS[:, 3072:3584], ACT.Silu).then_inc(s["z_silu"], 1)
            nc.scalar.activation(sqr[:, :], xc[:, 0:2 * SBW], ACT.Square).then_inc(s["n_sq"], 1)
            exp_ln_table(nc)
            act.wait_ge(s["n_ss"], 1)
            link(nc.scalar.activation(nrm[:, :], nrm[:, :], ACT.Ln, bias=g.eps_l2[0:NB]))
            nc.scalar.activation(nrm[:, :], nrm[:, :], ACT.Exp, scale=-0.5).then_inc(s["n_rs"], 1)
            act.wait_ge(s["qkv_ready"], 3)
            act.wait_ge(s["z_silu"], 1)
            act.dma_start(scr[:, :, :, :].rearrange("j b h e -> b j (h e)"), xc[:, :].rearrange("b (j n) -> b j n", j=4)).then_inc(s["sc_out"], 16)
            act.wait_ge(s["gates_ready"], 2)
            act.dma_start(scr2[:, :, :].rearrange("j b h -> b j h"), gates[:, :, :]).then_inc(s["sc_out"], 16)
            filler.copies(act, 1)
            act.wait_ge(s["sc_out"], 32)
            for j in range(4):
                act.dma_start(rows[:, j, :], scr[j].rearrange("b h e -> (b h) e")).then_inc(s["sc_in"], 16)
            with nc.allow_non_contiguous_dma(reason="64 gates"):
                for j in range(2):
                    act.dma_start(gt[:, j:j + 1], scr2[j].rearrange("b (h o) -> (b h) o", o=1)).then_inc(s["sc_in"], 16)

            filler.copies(act, 6)
            act.wait_ge(s["sb_w_in"], 1)
            link(nc.scalar.activation(t1[:, :], t1[:, :], ACT.Exp))
            nc.scalar.activation(t1[:, :], t1[:, :], ACT.Ln, bias=g.one_c).then_inc(s["sb_lg"], 1)
            filler.copies(act, 1)
            act.wait_ge(s["sb_w"], 1)
            nc.scalar.activation(flat(ad[:, :, :, :]), flat(ad[:, :, :, :]), ACT.Exp).then_inc(s["sb_a"], 1)
            filler.copies(act, 1)
            act.wait_ge(s["o_ready"], 1)
            nc.scalar.activation(osq[:, :], o2[:, 0:HD], ACT.Square).then_inc(s["o_sq"], 1)
            act.wait_ge(s["o_ss"], 1)
            link(nc.scalar.activation(ors[:, :], ors[:, :], ACT.Ln, bias=g.eps_l2[0:BH], scale=1.0 / HD))
            nc.scalar.activation(ors[:, :], ors[:, :], ACT.Exp, scale=-0.5).then_inc(s["o_rs"], 1)
            filler.copies(act, 5)
            act.wait_ge(s["mem_max"], 1)
            nc.scalar.activation(pm[:, :], g.PS[0:32, 7, 0:NM], ACT.Exp, bias=st1[:, 0:1], scale=SC, accum_out=st2[:, 0:1]).then_inc(s["mem_exp"], 1)
            filler.copies(act, 2)


def load_branch_weights(sp, g, x):
    for i, w in enumerate((x["w_br_sb"], x["w_br_gdn"], x["w_br_mem"])):
        sp.dma_start(g.BW[i][:, :, :], w.rearrange("(c p) n -> p c n", p=P)).then_inc(g.s_bw[i], 16)


def phase_merge(nc, g, x):
    W = g.BW
    s_mm, s_m, s_l = g.sem("branch_done"), g.sem("branch_gated"), g.sem("branch_link")
    with ExitStack() as ctx:
        tmp = ctx.enter_context(nc.sbuf_tensor("br_tmp", [P, 2, TH], F32))
        block = ctx.enter_context(nc.Block())

        @block.sync
        def _(sp):
            for i in range(2):
                sp.wait_ge(s_mm, KC * (i + 1))
                sp.dma_start(W[i][:, :, :], x["w_o"][i * 512:(i + 1) * 512, :].rearrange("(c p) n -> p c n", p=P)).then_inc(g.s_bw[i], 16)

        @block.tensor
        def _(pe):
            for n in range(24):
                br, j = n // KC, n % KC
                if j == 0:
                    pe.wait_ge(g.s_bw[br], 16)
                if n >= 3:
                    pe.wait_ge(s_m, n - 2)
                for h in range(2):
                    for c in range(4):
                        ins = nc.tensor.matmul(g.PS[:, 2 * (n % 3) + h, 0:TH], W[br][:, c, j * P:(j + 1) * P],
                                               g.OT[:, 4 * br + c, h * TH:(h + 1) * TH], start=c == 0, stop=c == 3)
                ins.then_inc(s_mm, 1)

        @block.vector
        def _(dve):
            link = Link(dve, s_l)
            for n in range(24):
                br, j = n // KC, n % KC
                half = lambda v: v.rearrange("p (h t) -> p h t", h=2)
                m = half(g.PT[:, MERGED[j], :])
                dve.wait_ge(s_mm, n + 1)
                if br:
                    dve.wait_ge(s_m, n)
                nc.vector.tensor_tensor(tmp[:, :, :] if br else m, g.PS[:, 2 * (n % 3):2 * (n % 3) + 2, 0:TH],
                                        half(g.PT[:, GATE[8 * br + j], :]), ALU.mult).then_inc(s_l if br else s_m, 1)
                if br:
                    link.n += 1
                    dve.wait_ge(s_l, link.n)
                    nc.vector.tensor_tensor(m, m, tmp[:, :, :], ALU.add).then_inc(s_m, 1)


def layer_norm_rows(nc, dve, link, src, dst, stats, agg, rstd, gain, shift, m, s_var, s_rstd, count):
    for h in range(2):
        ins = nc.vector.bn_stats(stats[0:m, h, :], src[:, h * 512:(h + 1) * 512])
    link(ins)
    nc.vector.bn_aggr(agg[0:m, :], stats[0:m, :, :]).then_inc(s_var, 1)
    dve.wait_ge(s_rstd, count)
    link(nc.vector.scalar_tensor_tensor(out=dst, in0=src, scalar=agg[0:m, 0:1], in1=gain[0:m, :], op0=ALU.subtract, op1=ALU.mult))
    return nc.vector.scalar_tensor_tensor(out=dst, in0=dst, scalar=rstd[0:m, 0:1], in1=shift[0:m, :], op0=ALU.mult, op1=ALU.add)


def phase_out(nc, g, x):
    s_mm, s_pre, s_var, s_rstd, s_h, s_tp, s_cp, s_st, s_l, s_al = (g.sem(n) for n in
        ("wo_done", "residual_ready", "ln1_var_ready", "ln1_rstd_ready", "h_ready", "h_transposed", "ht_copied",
         "h_stored", "out_link", "out_act_link"))
    s_in = [g.sem(f"out_in{i}_loaded") for i in range(4)]
    tiles = tok_tiles()
    with ExitStack() as ctx:
        sb = lambda n, sh: ctx.enter_context(nc.sbuf_tensor("out_" + n, sh, F32))
        W, xr = g.BW, sb("x", [P, 2, D])
        gain, shift, stats, agg, rstd = sb("gain", [P, D]), sb("shift", [P, D]), sb("stats", [P, 2, 6]), sb("agg", [P, 2]), sb("rstd", [P, 1])
        block = ctx.enter_context(nc.Block())

        @block.sync
        def _(sp):
            sp.dma_start(gain[:, :], x["ln1_g"].partition_broadcast(P)).then_inc(s_in[2], 16)
            sp.dma_start(shift[:, :], x["ln1_b"].partition_broadcast(P)).then_inc(s_in[3], 16)
            for t, (t0, m) in enumerate(tiles):
                if t >= 2:
                    sp.wait_ge(s_pre, t - 1)
                src = x["x_prompt"][0, t0:t0 + m, :] if t < NT else x["x_sample"].rearrange("b o d -> (b o) d")
                sp.dma_start(xr[0:m, t % 2, :], src).then_inc(s_in[t % 2], 16)
            for t, (t0, m) in enumerate(tiles):
                sp.wait_ge(s_h, t + 1)
                sp.dma_start(g.h_dram[t0:t0 + m, :], g.H[0:m, t, :]).then_inc(s_st, 16)
            sp.wait_ge(s_st, 16 * 5)

        @block.tensor
        def _(pe):
            for i in range(2):
                pe.wait_ge(g.s_bw[i], 32)

            def product(t):
                t0, m = tiles[t]
                if t >= 2:
                    pe.wait_ge(s_pre, t - 1)
                for h in range(2):
                    for k in range(KC):
                        ins = nc.tensor.matmul(g.PS[0:m, 2 * (t % 2) + h, :], g.PT[:, MERGED[k], t0:t0 + m], W[k // 4][:, k % 4, h * 512:(h + 1) * 512],
                                               start=k == 0, stop=k == KC - 1)
                ins.then_inc(s_mm, 1)

            def transposes(t):
                t0, m = tiles[t]
                pe.wait_ge(s_h, t + 1)
                if t >= 2:
                    pe.wait_ge(s_cp, t - 1)
                for k in range(KC):
                    ins = nc.tensor.transpose(g.PS[:, 4 + 2 * (t % 2) + k // 4, (k % 4) * P:(k % 4) * P + m], g.H[0:m, t, k::KC],
                                              g.ident[0:m, 0:m])
                ins.then_inc(s_tp, 1)

            for t in range(5):
                product(t)
                if t >= 2:
                    transposes(t - 2)
            transposes(3)
            transposes(4)

        @block.scalar
        def _(act):
            link = Link(act, s_al)

            def copy_ht(t):
                t0, m = tiles[t]
                act.wait_ge(s_tp, t + 1)
                src = g.PS[:, 4 + 2 * (t % 2):6 + 2 * (t % 2), :].rearrange("p b (k m) -> p (b k) m", m=P)[:, :, 0:m]
                nc.scalar.activation(g.XT[:, :, t0:t0 + m], src, ACT.Copy).then_inc(s_cp, 1)

            exp_ln_table(nc)
            for t, (t0, m) in enumerate(tiles):
                act.wait_ge(s_var, t + 1)
                link(nc.scalar.activation(rstd[0:m, :], agg[0:m, 1:2], ACT.Ln, bias=g.eps_ln[0:m]))
                nc.scalar.activation(rstd[0:m, :], rstd[0:m, :], ACT.Exp, scale=-0.5).then_inc(s_rstd, 1)
                if t >= 1:
                    copy_ht(t - 1)
            copy_ht(4)

        @block.vector
        def _(dve):
            link = Link(dve, s_l)
            dve.wait_ge(s_in[2], 16)
            dve.wait_ge(s_in[3], 16)
            for t, (t0, m) in enumerate(tiles):
                dve.wait_ge(s_mm, t + 1)
                dve.wait_ge(s_in[t % 2], 16 * (t // 2 + 1))
                h = g.H[0:m, t, :]
                nc.vector.scalar_tensor_tensor(out=h, in0=xr[0:m, t % 2, :], scalar=ALPHA,
                                               in1=g.PS[0:m, 2 * (t % 2):2 * (t % 2) + 2, :].rearrange("p b n -> p (b n)"),
                                               op0=ALU.mult, op1=ALU.add).then_inc(s_pre, 1)
                dve.wait_ge(s_pre, t + 1)
                layer_norm_rows(nc, dve, link, h, h, stats, agg, rstd, gain, shift, m, s_var, s_rstd, t + 1).then_inc(s_h, 1)


def expert_gate_up(sp, x, dst, e, sem):
    for j, w in enumerate((x["w_exp_gate"], x["w_exp_up"])):
        sp.dma_start(dst[:, j, :, :], w[e].rearrange("o (p k) f -> p (o k) f", k=KC)).then_inc(sem, 16)


def expert_down(sp, x, dst, e, sem):
    sp.dma_start(dst[:, :, :], x["w_exp_down"][e].rearrange("o (p j) n -> p (o j) n", j=2)).then_inc(sem, 16)


def phase_route(nc, g, x):
    names = ("w_loaded", "init", "tok0", "logits_done", "scores_ready", "chosen", "ranks_done", "dest_ready",
             "over_ready", "over_t", "table_cleared", "scattered", "table_in", "table_t", "slots_ready", "link",
             "gu_done", "sg_ready", "su_ready", "sh_ready", "ht_done", "ht_copied", "y_done", "y_copied",
             "sw_loaded")
    s = {n: g.sem("rt_" + n) for n in names}
    tiles = tok_tiles()
    with ExitStack() as ctx:
        sb = lambda n, sh, d=F32: ctx.enter_context(nc.sbuf_tensor("rt_" + n, sh, d))
        wr = sb("wr", [P, KC, NE])
        wgu, wd = sb("wgu", [P, 2, KC, DE]), sb("wd", [P, 2, D])
        SC, BI, M, DP, T1 = (sb(n, [P, 5, NE]) for n in ("SC", "BI", "M", "DP", "T1"))
        M8 = sb("M8", [P, 5, NG, 8])
        gs, cnt = sb("gs", [P, 5, NG]), sb("cnt", [P, 5, NG])
        A, B = sb("A", [P, 5, NG, NG]), sb("B", [P, 5, NG, NG])
        low, lowi = sb("low", [P, NG, NG]), sb("lowi", [P, NG, NG], I32)
        m8, den = sb("m8", [P, 5, 8]), sb("den", [P, 5])
        cn, ex, inc, ofs, ie, one64 = (sb(n, [P, NE]) for n in ("cn", "ex", "inc", "ofs", "ie", "one64"))
        oe, ip = sb("oe", [P, 2]), sb("ip", [P, 1])
        tok, dk = sb("tok", [P, 5, TOPK]), sb("dk", [P, 5, 8])
        toki = sb("toki", [P, 5, TOPK], I32)
        didx = sb("didx", [P, 5, TOPK], I32)
        free = sb("free", [NBLK, CAP])
        tabr = sb("tabr", [NBLK, CAP])
        sg, su, sht = sb("sg", [P, 5, DE]), sb("su", [P, 5, DE]), sb("sht", [P, 2, P])
        block = ctx.enter_context(nc.Block())

        @block.sync
        def _(sp):
            sp.dma_start(wr[:, :, :], x["w_router"].rearrange("(p k) n -> p k n", k=KC)).then_inc(s["w_loaded"], 16)
            for j, w in enumerate((x["w_sh_gate"], x["w_sh_up"])):
                sp.dma_start(wgu[:, j, :, :], w.rearrange("(p k) f -> p k f", k=KC)).then_inc(s["sw_loaded"], 16)
            sp.dma_start(wd[:, :, :], x["w_sh_down"].rearrange("(p j) n -> p j n", j=2)).then_inc(s["sw_loaded"], 16)
            sp.wait_ge(s["init"], 3)
            sp.dma_start(g.slot_dram.rearrange("(b p) o -> b (p o)", p=CAP), free[:, :]).then_inc(s["table_cleared"], 16)
            for b in range(NW):
                expert_gate_up(sp, x, g.WG[b], slice(b, b + 1), g.s_gu[b])
                expert_down(sp, x, g.WD[b], slice(b, b + 1), g.s_d[b])
            sp.wait_ge(s["scattered"], 16 * 40)
            sp.dma_start(tabr[:, :], g.slot_dram.rearrange("(b p) o -> b (p o)", p=CAP)).then_inc(s["table_in"], 16)

        @block.tensor
        def _(pe):
            pe.wait_ge(s["w_loaded"], 16)
            for t, (t0, m) in enumerate(tiles):
                for k in range(KC):
                    ins = nc.tensor.matmul(g.PS[0:m, 0, t * NE:(t + 1) * NE], g.XT[:, k, t0:t0 + m], wr[:, k, :],
                                           start=k == 0, stop=k == KC - 1)
            ins.then_inc(s["logits_done"], 1)

            def gate_up(t):
                t0, m = tiles[t]
                if t >= 2:
                    pe.wait_ge(s["su_ready"], t - 1)
                for k in range(KC):
                    ins = nc.tensor.matmul(g.PS[0:m, 3 + t % 2, :], g.XT[:, k, t0:t0 + m], wgu[:, :, k, :], start=k == 0, stop=k == KC - 1)
                ins.then_inc(s["gu_done"], 1)

            def down(t):
                t0, m = tiles[t]
                pe.wait_ge(s["sh_ready"], t + 1)
                for j in range(2):
                    ins = nc.tensor.transpose(g.PS[:, 5, j * P:j * P + m], sg[0:m, t, j::2], g.ident[0:m, 0:m])
                ins.then_inc(s["ht_done"], 1)
                pe.wait_ge(s["ht_copied"], t + 1)
                if t >= 1:
                    pe.wait_ge(s["y_copied"], t)
                for h in range(2):
                    for j in range(2):
                        ins = nc.tensor.matmul(g.PS[0:m, 6 + h, :], sht[:, j, 0:m], wd[:, j, h * 512:(h + 1) * 512], start=j == 0, stop=j == 1)
                ins.then_inc(s["y_done"], 1)

            pe.wait_ge(s["sw_loaded"], 48)
            for t in range(2):
                gate_up(t)
            pe.wait_ge(s["chosen"], 1)
            for t in range(5):
                kt = tiles[t][1]
                nc.tensor.matmul(g.PS[:, 1, t * NE:(t + 1) * NE], g.UTs[0:kt, :], M[0:kt, t, :], start=True, stop=t == 0)
                for j in range(t):
                    nc.tensor.matmul(g.PS[:, 1, t * NE:(t + 1) * NE], g.ones[:, :], M[:, j, :], start=False, stop=j == t - 1)
            for t in range(5):
                kt = tiles[t][1]
                ins = nc.tensor.matmul(g.PS[:, 2, 0:NE], g.ones[0:kt, :], M[0:kt, t, :], start=t == 0, stop=t == 4)
            ins.then_inc(s["ranks_done"], 1)
            for t in range(2, 5):
                gate_up(t)
            pe.wait_ge(s["over_ready"], 1)
            nc.tensor.transpose(g.PS[0:1, 2, 256:256 + 64], oe[0:64, 0:1], g.ident[0:64, 0:64]).then_inc(s["over_t"], 1)
            for t in range(5):
                down(t)
            pe.wait_ge(s["table_in"], 16)
            nc.tensor.transpose(g.PS[:, 0, 0:NBLK], tabr[:, :], g.ident[0:NBLK, 0:NBLK]).then_inc(s["table_t"], 1)

        @block.scalar
        def _(act):
            act.wait_ge(s["logits_done"], 1)
            act.wait_ge(s["init"], 1)
            nc.scalar.activation(SC[:, 0:4, :], g.PS[:, 0, 0:4 * NE].rearrange("p (t e) -> p t e", e=NE), ACT.Sigmoid).then_inc(s["scores_ready"], 1)
            nc.scalar.activation(SC[0:NB, 4, :], g.PS[0:NB, 0, 4 * NE:5 * NE], ACT.Sigmoid).then_inc(s["scores_ready"], 1)
            for t, (t0, m) in enumerate(tiles):
                act.wait_ge(s["gu_done"], t + 1)
                nc.scalar.activation(sg[0:m, t, :], g.PS[0:m, 3 + t % 2, 0:DE], ACT.Silu).then_inc(s["sg_ready"], 1)
                nc.scalar.activation(su[0:m, t, :], g.PS[0:m, 3 + t % 2, DE:2 * DE], ACT.Copy).then_inc(s["su_ready"], 1)
            for t, (t0, m) in enumerate(tiles):
                act.wait_ge(s["ht_done"], t + 1)
                nc.scalar.activation(sht[:, :, 0:m], g.PS[:, 5, 0:2 * P].rearrange("p (j m) -> p j m", j=2)[:, :, 0:m], ACT.Copy).then_inc(s["ht_copied"], 1)
                act.wait_ge(s["y_done"], t + 1)
                nc.scalar.activation(g.ACC[0:m, t, :], g.PS[0:m, 6:8, :].rearrange("p b n -> p (b n)"), ACT.Copy).then_inc(s["y_copied"], 1)

        @block.gpsimd
        def _(pool):
            pool.memset(SC[:, 4, :], 0.5).then_inc(s["init"], 1)
            pool.memset(one64[:, :], 1.0).then_inc(s["init"], 1)
            pool.memset(free[:, :], float(T * TOPK)).then_inc(s["init"], 1)
            pool.iota(lowi[:, :, :], pattern=[[1, NG], [-1, NG]], base=0, channel_multiplier=0).then_inc(s["tok0"], 1)
            pool.iota(toki[:, :, :], pattern=[[P * TOPK, 5], [1, TOPK]], base=0, channel_multiplier=TOPK).then_inc(s["tok0"], 1)
            pool.wait_ge(s["dest_ready"], 1)
            pool.wait_ge(s["table_cleared"], 16)
            for t, (t0, m) in enumerate(tiles):
                for k in range(8):
                    pool.indirect_dma_start(out=g.slot_dram, out_offset=bass.IndirectOffsetOnAxis(ap=didx[0:m, t, k:k + 1], axis=0),
                                            in_=tok[0:m, t, k:k + 1], in_offset=None).then_inc(s["scattered"], 16)

        @block.vector
        def _(dve):
            link = Link(dve, s["link"])
            V = nc.vector
            dve.wait_ge(s["tok0"], 2)
            V.tensor_copy(tok[:, :, :], toki[:, :, :])
            V.tensor_copy(ip[:, :], g.iota_p[:, :])
            V.tensor_copy(ie[:, :], g.iota_e[:, :])
            link(V.tensor_copy(low[:, :, :], lowi[:, :, :]))
            link(V.tensor_scalar(low[:, :, :], low[:, :, :], 0.0, None, ALU.is_gt))
            dve.wait_ge(s["scores_ready"], 2)
            link(V.tensor_tensor(BI[:, :, :], SC[:, :, :], g.rb_bc[:, :].unsqueeze(1).to_broadcast([P, 5, NE]), ALU.add))
            for t in range(5):
                for q in range(NG):
                    ins = V.max(M8[:, t, q, :], BI[:, t, q * 8:(q + 1) * 8])
            link(ins)
            link(V.tensor_tensor(gs[:, :, :], M8[:, :, :, 0], M8[:, :, :, 1], ALU.add))
            gi, gj = gs[:, :, :].unsqueeze(3).to_broadcast([P, 5, NG, NG]), gs[:, :, :].unsqueeze(2).to_broadcast([P, 5, NG, NG])
            V.tensor_tensor(A[:, :, :, :], gj, gi, ALU.is_gt)
            link(V.tensor_tensor(B[:, :, :, :], gj, gi, ALU.is_equal))
            link(V.tensor_tensor(B[:, :, :, :], B[:, :, :, :], low[:, :, :].unsqueeze(1).to_broadcast([P, 5, NG, NG]), ALU.mult))
            link(V.tensor_tensor(A[:, :, :, :], A[:, :, :, :], B[:, :, :, :], ALU.add))
            link(V.tensor_reduce(cnt[:, :, :], A[:, :, :, :], AX.X, ALU.add))
            link(V.tensor_scalar(cnt[:, :, :], cnt[:, :, :], 4.0, None, ALU.is_lt))
            e8 = lambda v: v.rearrange("p t (q e) -> p (t q) e", e=8)
            g8 = lambda v: v.rearrange("p t q -> p (t q)").unsqueeze(2).to_broadcast([P, 5 * NG, 8])
            link(V.tensor_tensor(e8(BI[:, :, :]), e8(BI[:, :, :]), g8(cnt[:, :, :]), ALU.mult))
            link(V.tensor_scalar(cnt[:, :, :], cnt[:, :, :], BIG, -BIG, ALU.mult, ALU.add))
            link(V.tensor_tensor(e8(BI[:, :, :]), e8(BI[:, :, :]), g8(cnt[:, :, :]), ALU.add))
            for t in range(5):
                ins = V.max(m8[:, t, :], BI[:, t, :])
            link(ins)
            for t in range(5):
                ins = V.match_replace(T1[:, t, :], m8[:, t, :], BI[:, t, :], -3.0 * BIG)
            link(ins)
            V.tensor_tensor(M[:, :, :], T1[:, :, :], BI[:, :, :], ALU.is_lt).then_inc(s["chosen"], 1)
            dve.wait_ge(s["chosen"], 1)
            link(V.tensor_tensor(SC[:, :, :], SC[:, :, :], M[:, :, :], ALU.mult))
            link(V.tensor_reduce(den[:, :], SC[:, :, :], AX.X, ALU.add))
            link(V.reciprocal(den[:, :], den[:, :]))
            link(V.tensor_scalar(den[:, :], den[:, :], ROUTE_SCALE, None, ALU.mult))
            link(V.tensor_tensor(SC[:, :, :], SC[:, :, :], den[:, :].unsqueeze(2).to_broadcast([P, 5, NE]), ALU.mult))
            dve.wait_ge(s["ranks_done"], 1)
            link(V.tensor_copy(cn[:, :], g.PS[:, 2, 0:NE]))
            link(V.tensor_scalar(ex[:, :], cn[:, :], float(CAP), None, ALU.is_gt))
            for q in range(2, (T - 1) // CAP + 1):
                link(V.scalar_tensor_tensor(out=ex[:, :], in0=cn[:, :], scalar=float(q * CAP), in1=ex[:, :], op0=ALU.is_gt, op1=ALU.add))
            dve.wait_ge(s["init"], 2)
            link(V.tensor_tensor_scan(inc[:, :], one64[:, :], ex[:, :], 0.0, ALU.mult, ALU.add))
            link(V.tensor_tensor(ofs[:, :], inc[:, :], ex[:, :], ALU.subtract))
            link(V.tensor_scalar(ofs[:, :], ofs[:, :], float(CAP), float(CAP * (NE - 1)), ALU.mult, ALU.add))
            link(V.tensor_tensor(ofs[:, :], ofs[:, :], ie[:, :], ALU.subtract))
            R = g.PS[:, 1, 0:5 * NE].rearrange("p (t e) -> p t e", e=NE)
            wide = lambda v: v.unsqueeze(1).to_broadcast([P, 5, NE])
            link(V.tensor_scalar(T1[:, :, :], R, float(CAP), None, ALU.is_ge))
            link(V.tensor_tensor(T1[:, :, :], T1[:, :, :], wide(ofs[:, :]), ALU.mult))
            link(V.tensor_tensor(T1[:, :, :], T1[:, :, :], R, ALU.add))
            link(V.tensor_tensor(T1[:, :, :], T1[:, :, :], wide(ie[:, :]), ALU.add))
            link(V.scalar_tensor_tensor(out=DP[:, :, :], in0=T1[:, :, :], scalar=1.0, in1=M[:, :, :], op0=ALU.add, op1=ALU.mult))
            for t in range(5):
                ins = V.max(dk[:, t, :], DP[:, t, :])
            link(ins)
            V.tensor_scalar(didx[:, :, :], dk[:, :, :], -1.0, None, ALU.add).then_inc(s["dest_ready"], 1)
            link(V.tensor_scalar(T1[:, 0, :], inc[:, :], ip[:, 0:1], 0.0, ALU.is_le, ALU.add, accum_out=oe[:, 0:1]))
            V.tensor_scalar(oe[:, 0:1], oe[:, 0:1], float(NE - 1), None, ALU.min).then_inc(s["over_ready"], 1)
            for t, (t0, m) in enumerate(tiles):
                dve.wait_ge(s["sg_ready"], t + 1)
                dve.wait_ge(s["su_ready"], t + 1)
                V.tensor_tensor(sg[0:m, t, :], sg[0:m, t, :], su[0:m, t, :], ALU.mult).then_inc(s["sh_ready"], 1)
            V.tensor_copy(g.over[0:1, 64:65], inc[0:1, NE - 1:NE])
            dve.wait_ge(s["over_t"], 1)
            V.tensor_copy(g.over[0:1, 0:64], g.PS[0:1, 2, 256:256 + 64])
            for t in range(5):
                for k in range(8):
                    ins = V.scalar_tensor_tensor(out=T1[:, t, :], in0=DP[:, t, :], scalar=dk[:, t, k:k + 1], in1=SC[:, t, :],
                                                 op0=ALU.is_equal, op1=ALU.mult, accum_out=g.wk[:, t, k:k + 1])
                    link(ins)
            dve.wait_ge(s["table_t"], 1)
            link(V.tensor_copy(g.slots[:, 1, :], g.PS[:, 0, 0:NBLK]))
            V.tensor_scalar(g.slots[:, 0, :], g.slots[:, 1, :], 3, None, ALU.logical_shift_right).then_inc(s["slots_ready"], 1)


def phase_moe(nc, g, x):
    names = ("xt_done", "xt_copied", "gu_done", "silu_ready", "h_ready", "ht_done", "ht_copied", "y_done",
             "y_copied", "o_gathered", "o_w", "o_xt", "o_xtc", "o_gu", "o_silu", "o_h", "o_ht", "o_htc", "o_y",
             "o_yc", "o_stored", "icol", "icol_seen", "o_free", "x_zeroed")
    s = {n: g.sem("moe_" + n) for n in names}
    s_x = [g.sem(f"moe_x{i}_gathered") for i in range(NW)]
    s_gu, s_d, WG, WD = g.s_gu, g.s_d, g.WG, g.WD
    s_y = [g.sem(f"moe_y{i}_stored") for i in range(2)]
    with ExitStack() as ctx:
        sb = lambda n, sh: ctx.enter_context(nc.sbuf_tensor("moe_" + n, sh, F32))
        xg, xt = [sb(f"x{i}", [P, D]) for i in range(NW)], [sb(f"xt{i}", [P, KC, P]) for i in range(2)]
        sg, hh, ht = [sb(f"sg{i}", [P, DE]) for i in range(2)], [sb(f"h{i}", [P, DE]) for i in range(2)], [sb(f"ht{i}", [P, 2, P]) for i in range(2)]
        yy = [sb(f"y{i}", [P, D]) for i in range(2)]
        gcol = [ctx.enter_context(nc.sbuf_tensor(f"moe_gcol{i}", [P, 1], I32)) for i in range(NW)]
        scol = [ctx.enter_context(nc.sbuf_tensor(f"moe_scol{i}", [P, 1], I32)) for i in range(2)]
        block = ctx.enter_context(nc.Block())
        pair = lambda b: g.PS[:, b:b + 2, :].rearrange("p b n -> p (b n)")
        BODY = NE // NW - 1

        @block.sync
        def _(sp):
            with sp.Fori(0, BODY) as i:
                for b in range(NW):
                    sp.wait_ge(s["gu_done"], i * NW + b + 1)
                    expert_gate_up(sp, x, WG[b], bass.ds(i * NW + NW + b, 1), s_gu[b])
                    sp.wait_ge(s["y_done"], i * NW + b + 1)
                    expert_down(sp, x, WD[b], bass.ds(i * NW + NW + b, 1), s_d[b])
            total = sp.value_load(g.over[0:1, NE:NE + 1], min_val=0, max_val=NOV)
            sp.wait_ge(s["y_done"], NE)
            sp.sem_inc(s["o_y"], 1)
            with sp.If(total > 0):
                with sp.Fori(0, NOV) as i:
                    with sp.If(total > i):
                        e = sp.value_load(g.over[0:1, bass.ds(i, 1)], min_val=0, max_val=NE - 1)
                        sp.wait_ge(s["o_y"], i + 1)
                        expert_gate_up(sp, x, WG[0], bass.ds(e, 1), s["o_w"])
                        expert_down(sp, x, WD[0], bass.ds(e, 1), s["o_w"])

        @block.gpsimd
        def _(pool):
            def indices(dst, which, col, count):
                pool.tensor_copy(dst[:, :], g.slots[:, which, col]).then_inc(s["icol"], 1)
                pool.wait_ge(s["icol"], count)
                pool.sem_inc(s["icol_seen"], 1)

            def gather(u, sem):
                pool.indirect_dma_start(out=xg[u][:, :], out_offset=None, in_=g.h_dram,
                                        in_offset=bass.IndirectOffsetOnAxis(ap=gcol[u][:, :], axis=0),
                                        bounds_check=T - 1, oob_is_err=False).then_inc(sem, 16)

            def scatter(b, sem):
                pool.indirect_dma_start(out=g.y_dram, out_offset=bass.IndirectOffsetOnAxis(ap=scol[b][:, :], axis=0),
                                        in_=yy[b][:, :], in_offset=None,
                                        bounds_check=T * TOPK - 1, oob_is_err=False).then_inc(sem, 16)

            col = lambda i, u: bass.ds(i * NW + u, 1) if not isinstance(i, int) else slice(i * NW + u, i * NW + u + 1)

            def step(i, u, last=False):
                if not last:
                    pool.wait_ge(s["xt_done"], i * NW + u + 2)
                    indices(gcol[(u + 1) % NW], 0, col(i, NW + u + 1), i * 2 * NW + NW + 2 * u + 2)
                    gather((u + 1) % NW, s_x[(u + 1) % NW])
                if not isinstance(i, int) or i * NW + u >= 2:
                    pool.wait_ge(s_y[u % 2], i * 16 * NW // 2 + 16 * (u // 2))
                indices(scol[u % 2], 1, col(i, u), i * 2 * NW + NW + 2 * u + 3 if not last else (i + 1) * NW + NE - NW + u + 1)
                pool.wait_ge(s["y_copied"], i * NW + u + 2)
                pool.sem_inc(s["icol_seen"], 1)
                scatter(u % 2, s_y[u % 2])

            for u in range(NW):
                pool.wait_ge(s["x_zeroed"], u + 1)
                indices(gcol[u], 0, slice(u, u + 1), u + 1)
                gather(u, s_x[u])
            pool.wait_ge(s["xt_done"], 1)
            indices(gcol[0], 0, slice(NW, NW + 1), NW + 1)
            gather(0, s_x[0])
            for u in range(NW):
                step(0, u)
            with pool.Fori(1, BODY - 1) as i:
                for u in range(NW):
                    step(i, u)
            for u in range(2 * NW):
                step(BODY - 1, u, last=u >= NW - 1)
            for b in range(2):
                pool.wait_ge(s_y[b], 16 * NE // 2)
            total = pool.value_load(g.over[0:1, NE:NE + 1], min_val=0, max_val=NOV)
            with pool.If(total > 0):
                with pool.Fori(0, NOV) as i:
                    with pool.If(total > i):
                        indices(gcol[0], 0, bass.ds(i + NE, 1), i * 2 + 2 * NE + 1)
                        gather(0, s["o_gathered"])
                        indices(scol[0], 1, bass.ds(i + NE, 1), i * 2 + 2 * NE + 2)
                        pool.wait_ge(s["o_yc"], i + 2)
                        pool.sem_inc(s["icol_seen"], 1)
                        scatter(0, s["o_stored"])
                        pool.wait_ge(s["o_stored"], i * 16 + 16)
                        pool.sem_inc(s["o_free"], 1)

        @block.tensor
        def _(pe):
            def rows_transpose(b):
                for k in range(KC):
                    ins = nc.tensor.transpose(g.PS[:, k // 4, (k % 4) * P:(k % 4 + 1) * P], xg[b][:, k::KC], g.ident[:, :])
                return ins

            def gate_up_products(b, w):
                for k in range(KC):
                    ins = nc.tensor.matmul(g.PS[:, 2 + b, :], xt[b][:, k, :], WG[w][:, :, k, :], start=k == 0, stop=k == KC - 1)
                return ins

            def h_transpose(b):
                for j in range(2):
                    ins = nc.tensor.transpose(g.PS[:, 4, j * P:(j + 1) * P], hh[b][:, j::2], g.ident[:, :])
                return ins

            def down_products(b, w):
                for h in range(2):
                    for j in range(2):
                        ins = nc.tensor.matmul(g.PS[:, 5 + h, :], ht[b][:, j, :], WD[w][:, j, h * 512:(h + 1) * 512], start=j == 0, stop=j == 1)
                return ins

            def rows_t(i, u):
                pe.wait_ge(s_x[u % NW], i * 16 + 16 * (u // NW + 1))
                pe.wait_ge(s["xt_copied"], i * NW + u + 1)
                rows_transpose(u % NW).then_inc(s["xt_done"], 1)

            def gate_up(i, u):
                pe.wait_ge(s_gu[u % NW], i * 32 + 32 * (u // NW + 1))
                pe.wait_ge(s["xt_copied"], i * NW + u + 2)
                pe.wait_ge(s["h_ready"], i * NW + u + 1)
                gate_up_products(u % 2, u % NW).then_inc(s["gu_done"], 1)

            def h_t(i, u):
                pe.wait_ge(s["h_ready"], i * NW + u + 3)
                h_transpose(u % 2).then_inc(s["ht_done"], 1)

            def down(i, u):
                pe.wait_ge(s_d[u % NW], i * 16 + 16 * (u // NW + 1))
                pe.wait_ge(s["ht_copied"], i * NW + u + 1)
                pe.wait_ge(s["y_copied"], i * NW + u + 1)
                down_products(u % 2, u % NW).then_inc(s["y_done"], 1)

            rows_t(0, 0)
            gate_up(0, 0)
            rows_t(0, 1)
            with pe.Fori(0, BODY) as i:
                for u in range(NW):
                    h_t(i, u)
                    gate_up(i, u + 1)
                    rows_t(i, u + 2)
                    down(i, u)
            for u in range(NW):
                h_t(BODY, u)
                if u + 1 < NW:
                    gate_up(BODY, u + 1)
                if u + 2 < NW:
                    rows_t(BODY, u + 2)
                down(BODY, u)
            total = pe.value_load(g.over[0:1, NE:NE + 1], min_val=0, max_val=NOV)
            pe.wait_ge(s["y_copied"], NE + 1)
            with pe.If(total > 0):
                with pe.Fori(0, NOV) as i:
                    with pe.If(total > i):
                        pe.wait_ge(s["o_gathered"], i * 16 + 16)
                        rows_transpose(0).then_inc(s["o_xt"], 1)
                        pe.wait_ge(s["o_xtc"], i + 1)
                        pe.wait_ge(s["o_w"], i * 48 + 48)
                        gate_up_products(0, 0).then_inc(s["o_gu"], 1)
                        pe.wait_ge(s["o_h"], i + 1)
                        h_transpose(0).then_inc(s["o_ht"], 1)
                        pe.wait_ge(s["o_htc"], i + 1)
                        pe.wait_ge(s["o_yc"], i + 1)
                        down_products(0, 0).then_inc(s["o_y"], 1)

        @block.scalar
        def _(act):
            def silu(i, u):
                act.wait_ge(s["gu_done"], i * NW + u + 1)
                act.wait_ge(s["h_ready"], i * NW + u + 1)
                nc.scalar.activation(sg[u % 2][:, :], g.PS[:, 2 + u % 2, 0:DE], ACT.Silu).then_inc(s["silu_ready"], 1)

            def rows_out(i, u):
                act.wait_ge(s["y_done"], i * NW + u + 1)
                if not isinstance(i, int) or i * NW + u >= 2:
                    act.wait_ge(s_y[u % 2], i * 16 * NW // 2 + 16 * (u // 2))
                nc.scalar.activation(yy[u % 2][:, :], pair(5), ACT.Copy).then_inc(s["y_copied"], 1)

            act.sem_inc(s["y_copied"], 1)
            act.sem_inc(s["o_yc"], 1)
            act.sem_inc(s["o_free"], 1)
            silu(0, 0)
            for u in range(NW):
                silu(0, u + 1)
                rows_out(0, u)
            with act.Fori(1, BODY) as i:
                for u in range(NW):
                    silu(i, u + 1)
                    rows_out(i, u)
            for u in range(NW):
                if u + 1 < NW:
                    silu(BODY, u + 1)
                rows_out(BODY, u)
            total = act.value_load(g.over[0:1, NE:NE + 1], min_val=0, max_val=NOV)
            for b in range(2):
                act.wait_ge(s_y[b], 16 * NE // 2)
            with act.If(total > 0):
                with act.Fori(0, NOV) as i:
                    with act.If(total > i):
                        act.wait_ge(s["o_gu"], i + 1)
                        nc.scalar.activation(sg[0][:, :], g.PS[:, 2, 0:DE], ACT.Silu).then_inc(s["o_silu"], 1)
                        act.wait_ge(s["o_y"], i + 2)
                        act.wait_ge(s["o_free"], i + 1)
                        nc.scalar.activation(yy[0][:, :], pair(5), ACT.Copy).then_inc(s["o_yc"], 1)

        @block.vector
        def _(dve):
            copy_rows = lambda b: nc.vector.tensor_copy(xt[b][:, :, :].rearrange("p k m -> p (k m)"), pair(0))
            copy_ht = lambda b: nc.vector.tensor_copy(ht[b][:, :, :].rearrange("p j m -> p (j m)"), g.PS[:, 4, 0:2 * P])
            gate = lambda b: nc.vector.tensor_tensor(hh[b][:, :], sg[b][:, :], g.PS[:, 2 + b, DE:2 * DE], ALU.mult)

            def rows_copy(i, u):
                dve.wait_ge(s["xt_done"], i * NW + u + 1)
                if not isinstance(i, int) or i * NW + u >= 2:
                    dve.wait_ge(s["gu_done"], i * NW + u - 1)
                copy_rows(u % 2).then_inc(s["xt_copied"], 1)

            def gated(i, u):
                dve.wait_ge(s["silu_ready"], i * NW + u + 1)
                if not isinstance(i, int) or i * NW + u >= 2:
                    dve.wait_ge(s["ht_done"], i * NW + u - 1)
                gate(u % 2).then_inc(s["h_ready"], 1)

            def ht_copy(i, u):
                dve.wait_ge(s["ht_done"], i * NW + u + 1)
                if not isinstance(i, int) or i * NW + u >= 2:
                    dve.wait_ge(s["y_done"], i * NW + u - 1)
                copy_ht(u % 2).then_inc(s["ht_copied"], 1)

            def step(i, u):
                ht_copy(i, u)
                gated(i, u + 1)
                rows_copy(i, u + 2)

            for u in range(NW):
                nc.vector.memset(xg[u][:, :], 0.0).then_inc(s["x_zeroed"], 1)
            dve.sem_inc(s["xt_copied"], 1)
            dve.sem_inc(s["h_ready"], 2)
            rows_copy(0, 0)
            rows_copy(0, 1)
            gated(0, 0)
            for u in range(NW):
                step(0, u)
            with dve.Fori(1, BODY) as i:
                for u in range(NW):
                    step(i, u)
            for u in range(NW):
                ht_copy(BODY, u)
                if u + 1 < NW:
                    gated(BODY, u + 1)
                if u + 2 < NW:
                    rows_copy(BODY, u + 2)
            total = dve.value_load(g.over[0:1, NE:NE + 1], min_val=0, max_val=NOV)
            with dve.If(total > 0):
                with dve.Fori(0, NOV) as i:
                    with dve.If(total > i):
                        dve.wait_ge(s["o_xt"], i + 1)
                        copy_rows(0).then_inc(s["o_xtc"], 1)
                        dve.wait_ge(s["o_silu"], i + 1)
                        gate(0).then_inc(s["o_h"], 1)
                        dve.wait_ge(s["o_ht"], i + 1)
                        copy_ht(0).then_inc(s["o_htc"], 1)


def phase_final(nc, g, x, y):
    NR, K = 4, TOPK // 2
    s_acc, s_var, s_rstd, s_y, s_st, s_l, s_al, s_used = (g.sem("fin_" + n) for n in
        ("acc_ready", "var_ready", "rstd_ready", "y_ready", "y_stored", "link", "act_link", "row_used"))
    s_dg, s_pe, s_ps = (g.sem("fin_" + n) for n in ("diagonals_ready", "products_done", "products_added"))
    s_sr, s_su = g.sem("fin_sample_rows_loaded"), g.sem("fin_sample_row_used")
    s_r = [g.sem(f"fin_row{i}_loaded") for i in range(NR)]
    s_h = [g.sem(f"fin_h{i}_loaded") for i in range(2)]
    s_in = g.sem("fin_norm_loaded")
    tiles = [(p, t, *tok_tiles()[t]) for p, t in enumerate((0, 1, 2, NT, 3))]
    with ExitStack() as ctx:
        sb = lambda n, sh: ctx.enter_context(nc.sbuf_tensor("fin_" + n, sh, F32))
        row, hb = [sb(f"row{i}", [P, K, D]) for i in range(NR)], [sb(f"h{i}", [P, D]) for i in range(2)]
        gain, shift, stats, agg, rstd = sb("gain", [P, D]), sb("shift", [P, D]), sb("stats", [P, 2, 6]), sb("agg", [P, 2]), sb("rstd", [P, 1])
        dg = sb("diagonals", [P, 2, K, P])
        srow = sb("sample_rows", [NB, TOPK, D])
        block = ctx.enter_context(nc.Block())

        @block.sync
        def _(sp):
            rows_of = lambda t0, m: g.y_dram[t0 * TOPK:(t0 + m) * TOPK, :].rearrange("(p k) d -> p k d", k=TOPK)
            sp.dma_start(srow[:, :, :], rows_of(SEQ, NB)).then_inc(s_sr, 16)
            for p, t, t0, m in tiles:
                rows = rows_of(t0, m)
                for j in (1, 0) if t < NT else ():
                    n = 2 * t + j
                    if t >= 2:
                        sp.wait_ge(s_pe, t - 1) if j else sp.wait_ge(s_used, K * (t - 1))
                    sp.dma_start(row[n % NR][0:m, :, :], rows[:, j * K:(j + 1) * K, :]).then_inc(s_r[n % NR], 16)
                if p >= 2:
                    sp.wait_ge(s_acc, p - 1)
                sp.dma_start(hb[p % 2][0:m, :], g.h_dram[t0:t0 + m, :]).then_inc(s_h[p % 2], 16)
                if p == 0:
                    sp.dma_start(gain[:, :], x["ln2_g"].partition_broadcast(P)).then_inc(s_in, 16)
                    sp.dma_start(shift[:, :], x["ln2_b"].partition_broadcast(P)).then_inc(s_in, 16)
            for p, t, t0, m in tiles:
                sp.wait_ge(s_y, p + 1)
                dst = y["y_prompt"][0, t0:t0 + m, :] if t < NT else y["y_sample"].rearrange("b o d -> (b o) d")
                sp.dma_start(dst, g.ACC[0:m, t, :]).then_inc(s_st, 16)
            sp.wait_ge(s_st, 16 * 5)

        @block.gpsimd
        def _(pool):
            pool.wait_ge(s_sr, 16)
            pool.tensor_tensor(srow[:, :, :], srow[:, :, :], g.wk[0:NB, NT, :].unsqueeze(2).to_broadcast([NB, TOPK, D]), ALU.mult).then_inc(s_su, 1)
            for n, half in enumerate((4, 2, 1)):
                pool.wait_ge(s_su, n + 1)
                pool.tensor_tensor(srow[:, 0:half, :], srow[:, 0:half, :], srow[:, half:2 * half, :], ALU.add).then_inc(s_su, 1)
            pool.wait_ge(s_su, 4)
            pool.tensor_tensor(g.ACC[0:NB, NT, :], g.ACC[0:NB, NT, :], srow[:, 0, :], ALU.add).then_inc(s_su, 1)

        @block.tensor
        def _(pe):
            for t in range(NT):
                n = 2 * t + 1
                pe.wait_ge(s_dg, K * (t + 1))
                pe.wait_ge(s_r[n % NR], 16 * (n // NR + 1))
                if t >= 2:
                    pe.wait_ge(s_ps, t - 1)
                for h in range(2):
                    for k in range(K):
                        ins = nc.tensor.matmul(g.PS[:, 2 * (t % 2) + h, :], dg[:, t % 2, k, :], row[n % NR][:, k, h * 512:(h + 1) * 512],
                                               start=k == 0, stop=k == K - 1)
                ins.then_inc(s_pe, 1)

        @block.scalar
        def _(act):
            link = Link(act, s_al)
            exp_ln_table(nc)

            def diagonals(t):
                if t >= 2:
                    act.wait_ge(s_pe, t - 1)
                for k in range(K):
                    nc.scalar.activation(dg[:, t % 2, k, :], g.ident[:, :], ACT.Copy, scale=g.wk[:, t, K + k:K + k + 1]).then_inc(s_dg, 1)

            diagonals(0)
            diagonals(1)
            for p, t, t0, m in tiles:
                if 2 <= t + 1 < NT:
                    diagonals(t + 1)
                act.wait_ge(s_var, p + 1)
                link(nc.scalar.activation(rstd[0:m, :], agg[0:m, 1:2], ACT.Ln, bias=g.eps_ln[0:m]))
                nc.scalar.activation(rstd[0:m, :], rstd[0:m, :], ACT.Exp, scale=-0.5).then_inc(s_rstd, 1)

        @block.vector
        def _(dve):
            link = Link(dve, s_l)
            for p, t, t0, m in tiles:
                acc = g.ACC[0:m, t, :]
                if t == NT:
                    dve.wait_ge(s_su, 5)
                for k in range(K if t < NT else 0):
                    if k == 0:
                        dve.wait_ge(s_r[2 * t % NR], 16 * (2 * t // NR + 1))
                    nc.vector.scalar_tensor_tensor(out=acc, in0=row[2 * t % NR][:, k, :], scalar=g.wk[:, t, k:k + 1], in1=acc,
                                                   op0=ALU.mult, op1=ALU.add).then_inc(s_used, 1)
                    dve.wait_ge(s_used, K * t + k + 1)
                if t < NT:
                    dve.wait_ge(s_pe, t + 1)
                    nc.vector.tensor_tensor(acc, acc, g.PS[:, 2 * (t % 2):2 * (t % 2) + 2, :].rearrange("p b n -> p (b n)"),
                                            ALU.add).then_inc(s_ps, 1)
                    dve.wait_ge(s_ps, t + 1)
                dve.wait_ge(s_h[p % 2], 16 * (p // 2 + 1))
                nc.vector.scalar_tensor_tensor(out=acc, in0=hb[p % 2][0:m, :], scalar=ALPHA, in1=acc,
                                               op0=ALU.mult, op1=ALU.add).then_inc(s_acc, 1)
                dve.wait_ge(s_acc, p + 1)
                if p == 0:
                    dve.wait_ge(s_in, 32)
                layer_norm_rows(nc, dve, link, acc, acc, stats, agg, rstd, gain, shift, m, s_var, s_rstd, p + 1).then_inc(s_y, 1)


def build(nc, x, y, stop=99):
    g = Shared()
    phase_sems = []

    def sem(name):
        phase_sems.append(nc.alloc_semaphore(name=name))
        return phase_sems[-1]

    def end_phase():
        nc.clear_and_free_semaphores(phase_sems)
        nc.all_engine_barrier(sem_only=True)
        phase_sems.clear()

    g.sem = sem
    g.h_dram = nc.dram_tensor("scratch_h", [T, D], F32, kind="Internal").ap()
    g.y_dram = nc.dram_tensor("scratch_expert_rows", [T * TOPK, D], F32, kind="Internal").ap()
    g.slot_dram = nc.dram_tensor("scratch_slot_tokens", [NBLK * CAP, 1], F32, kind="Internal").ap()
    with ExitStack() as ctx:
        alloc = lambda c: lambda n, s, d=F32: c.enter_context(nc.sbuf_tensor(n, s, d))
        sb = alloc(ctx)
        g.PS = ctx.enter_context(nc.psum_tensor("PS", [P, 8, 512], F32))
        g.ident, g.UT, g.UTs, g.TRI, g.ones, g.nones, g.bones = (
            sb(n, [P, P]) for n in ("ident", "UT", "UTs", "TRI", "ones", "nones", "bones"))
        g.LM = sb("LM", [P, 7, P])
        g.one_c, g.eps_l2, g.eps_ln = (sb(n, [P, 1])[:, :] for n in ("one_c", "eps_l2", "eps_ln"))
        g.iota_p, g.iota_e = sb("iota_p", [P, 1], I32), sb("iota_e", [P, NE], I32)
        g.A_bc, g.dt_bc, g.sbb_bc, g.rb_bc = (sb(n, [P, w]) for n, w in
                                              (("A_bc", H), ("dt_bc", H), ("sbb_bc", H), ("rb_bc", NE)))
        g.nw_col = sb("nw_col", [P, 1])
        g.S = sb("S", [P, 4, HD])
        g.wk = sb("wk", [P, 5, TOPK])
        g.slots, g.over = sb("slots", [P, 2, NBLK], I32), sb("over", [1, NE + 1], I32)
        g.XT = sb("XT", [P, KC, T])
        with ExitStack() as mix:
            ms = alloc(mix)
            g.OT, g.PT = ms("OT", [P, 12, T]), ms("PT", [P, NCH, T])
            with ExitStack() as att:
                ab = alloc(att)
                g.BA, g.XS, g.CW = ab("BA", [16, T]), ab("XS", [NB, GT0]), ab("CW", [P, 12, 4])
                g.MKV, g.VT = ab("MKV", [P, 2 * MH * NM]), ab("VT", [P, NT, SBW])
                g.GW = [v.rearrange("p (k n) -> p k n", k=KC) for v in (g.VT[:, :, :].rearrange("p t n -> p (t n)"), g.MKV[:, :])]
                g.MKT = g.MKV[:, 0:MH * NM].rearrange("p (h m) -> p h m", h=MH)
                g.MV = g.MKV[:, MH * NM:2 * MH * NM].rearrange("p (m n) -> p m n", m=2)
                with nc.sbuf_tensor("MT", [P, KC, NM], F32) as MT:
                    g.MT = MT
                    phase_load(nc, g, x)
                    end_phase()
                    if stop == 0: return
                    proj_cols(nc, g, x["w_in"], [(0, 0, 7), (MQ0, CM, 1)], "in")
                    end_phase()
                    if stop == 1: return
                    phase_small(nc, g, x, y)
                    end_phase()
                phase_rows(nc, g, x, y)
                end_phase()
                if stop == 2: return
                phase_sb(nc, g)
                end_phase()
                if stop == 3: return
                phase_mem(nc, g)
                end_phase()
                if stop == 4: return
                with ExitStack() as gd:
                    gb = alloc(gd)
                    g.KTM, g.VTM = g.PT[:, 0:NT, 0:SBW], g.PT[:, NT:2 * NT, 0:SBW]
                    g.GC, g.EGC, g.TAIL, g.BETA = (gb(n, [P, NT * H]) for n in ("GC", "EGC", "TAIL", "BETA"))
                    g.EGL, g.GCT = gb("EGL", [P, NT, 4]), gb("GCT", [NT * H, P])
                    phase_gdn_prep(nc, g, x)
                    end_phase()
                    phase_gdn(nc, g, y)
                    end_phase()
                if stop == 5: return
                phase_sample(nc, g, x, y)
                end_phase()
                if stop == 6: return
            g.BW = [ms(f"branch_w{i}", [P, 4, D]) for i in range(3)]
            g.s_bw = [nc.alloc_semaphore(name=f"branch_w{i}_loaded") for i in range(3)]
            late = G_PREP + G_SMP
            proj_cols(nc, g, x["w_in"], [(GT0 + late * P, GATE[late], (24 - late) // 4)], "in_g", sigmoid=True,
                      ahead=lambda sp: load_branch_weights(sp, g, x))
            end_phase()
            phase_merge(nc, g, x)
            end_phase()
            if stop == 7: return
            g.H = g.PT[:, 0:10, :].rearrange("p c t -> p (c t)")[:, 0:5 * D].rearrange("p (t d) -> p t d", d=D)
            phase_out(nc, g, x)
            end_phase()
            if stop == 8: return
        g.ACC = sb("ACC", [P, NT + 1, D])
        wts = ExitStack()
        ctx.enter_context(wts)
        wb = alloc(wts)
        g.WG, g.WD = [wb(f"w_gu{i}", [P, 2, KC, DE]) for i in range(NW)], [wb(f"w_d{i}", [P, 2, D]) for i in range(NW)]
        g.s_gu, g.s_d = ([nc.alloc_semaphore(name=f"expert_{n}{i}_loaded") for i in range(NW)] for n in ("gu", "d"))
        phase_route(nc, g, x)
        end_phase()
        if stop == 9: return
        phase_moe(nc, g, x)
        end_phase()
        if stop == 10: return
        wts.close()
        phase_final(nc, g, x, y)


INPUTS = ("x_prompt", "x_sample", "cache_sb_k", "cache_sb_v", "page_table", "state_gdn", "state_gdn_conv", "cache_mem_k",
          "cache_mem_v", "mem_prompt", "w_in", "sb_logit_bias", "conv_w", "gdn_A_log", "gdn_dt_bias", "gdn_norm_w",
          "w_mem_k", "w_mem_v", "w_br_sb", "w_br_gdn", "w_br_mem", "w_o", "ln1_g", "ln1_b", "w_router", "router_bias",
          "w_exp_gate", "w_exp_up", "w_exp_down", "w_sh_gate", "w_sh_up", "w_sh_down", "ln2_g", "ln2_b")
OUTPUTS = (("y_prompt", (1, SEQ, D)), ("y_sample", (NB, 1, D)),
           ("sb_k_prompt", (1, SEQ, H, HD)), ("sb_v_prompt", (1, SEQ, H, HD)),
           ("state_prompt", (1, H, HD, HD)), ("conv_prompt", (1, 3, 3 * SBW)),
           ("mem_k_prompt", (1, NM, MH, P)), ("mem_v_prompt", (1, NM, MH, P)),
           ("sb_k_sample", (NB, 1, H, HD)), ("sb_v_sample", (NB, 1, H, HD)),
           ("state_sample", (NB, H, HD, HD)), ("conv_sample", (NB, 3, 3 * SBW)))


def kernel(**inputs):
    import concourse.bacc as bacc
    from concourse.bass_utils import run_bass_kernel_spmd

    nc = bacc.Bacc("TRN2", target_bir_lowering=False, num_devices=1)
    arrays = {"in_" + n: np.ascontiguousarray(inputs[n]) for n in INPUTS}
    x = {n: nc.dram_tensor("in_" + n, arrays["in_" + n].shape, mybir.dt.from_np(arrays["in_" + n].dtype),
                                             kind="ExternalInput").ap() for n in INPUTS}
    y = {n: nc.dram_tensor("out_" + n, shape, F32, kind="ExternalOutput").ap() for n, shape in OUTPUTS}
    build(nc, x, y)
    r = run_bass_kernel_spmd(nc, [arrays], core_ids=[0])
    return tuple(r.results[0]["out_" + n] for n, _ in OUTPUTS)
```
